# Optimizing a Trainium2 kernel written in Bass

```python
import jax
import jax.numpy as jnp
from jax import lax
import numpy as np
import jax, jax.numpy as jnp

D_MODEL = 1024
BATCH = 1
SEQ = 512
DEPTH = 1

CHUNK = 64

D_MIX = D_MODEL
N_GROUPS = 4
GROUP_W = D_MIX // N_GROUPS
HEAD_DIM = 64

FOX_HEADS = GROUP_W // HEAD_DIM
FOX_DH = HEAD_DIM
Q_BLOCK = 128
FOX_BIAS_INIT = 2.0

GDN_HEADS = GROUP_W // HEAD_DIM
GDN_DK = HEAD_DIM
GDN_DV = HEAD_DIM
GDN_CONV = 4

HG_HEADS = GROUP_W // HEAD_DIM
HG_DK = HEAD_DIM
HG_DV = HEAD_DIM
HG_KW = HG_HEADS * HG_DK

GLA_HEADS = GROUP_W // HEAD_DIM
GLA_DV = HEAD_DIM
GLA_DK = HEAD_DIM // 2
GLA_KW = GLA_HEADS * GLA_DK
GLA_RANK = 16
GLA_NORM = 16.0

LA_BLOCK = 16

D_FF = ((8 * D_MODEL // 3 + 255) // 256) * 256
FFN_CONV = 3
EPS = 1e-6

IN_SIZES = (
    3 * GROUP_W, FOX_HEADS,
    3 * GROUP_W, GDN_HEADS, GDN_HEADS, GROUP_W,
    HG_KW, HG_KW, GROUP_W, GROUP_W,
    2 * GLA_KW, GROUP_W, GLA_RANK, GROUP_W,
)
IN_COLS = sum(IN_SIZES)


def _cut_points(sizes):
    cuts, acc = [], 0
    for s in sizes[:-1]:
        acc += s
        cuts.append(acc)
    return cuts

def rms_norm(x, g):
    xf = x.astype(jnp.float32)
    y = xf * lax.rsqrt(jnp.mean(xf * xf, axis=-1, keepdims=True) + EPS)
    return (y * g.astype(jnp.float32)).astype(x.dtype)

def l2norm(x):
    return x * lax.rsqrt(jnp.sum(x * x, axis=-1, keepdims=True) + EPS)

def split_heads(t, n):
    b, s, w = t.shape
    return t.reshape(b, s, n, w // n).transpose(0, 2, 1, 3)

def merge_heads(t):
    b, h, s, d = t.shape
    return t.transpose(0, 2, 1, 3).reshape(b, s, h * d)

def causal_dwconv(x, w):
    k_w = w.shape[0]
    s = x.shape[1]
    xp = jnp.pad(x, ((0, 0), (k_w - 1, 0), (0, 0)))
    y = xp[:, 0:s] * w[0]
    for j in range(1, k_w):
        y = y + xp[:, j:j + s] * w[j]
    return y

def fox_attention(q, k, v, log_f):
    b, h, s, d = q.shape
    c = jnp.cumsum(log_f, axis=-1)
    nb = s // Q_BLOCK
    qb = q.reshape(b, h, nb, Q_BLOCK, d).transpose(2, 0, 1, 3, 4)
    cb = c.reshape(b, h, nb, Q_BLOCK).transpose(2, 0, 1, 3)
    pos_k = jnp.arange(s)
    scale = d ** -0.5

    def one_block(args):
        qi, ci, bi = args
        pos_q = bi * Q_BLOCK + jnp.arange(Q_BLOCK)
        logits = jnp.einsum('bhqd,bhkd->bhqk', qi, k) * scale + ci[..., :, None] - c[:, :, None, :]
        logits = jnp.where(pos_k[None, :] <= pos_q[:, None], logits, -jnp.inf)
        probs = jax.nn.softmax(logits, axis=-1)
        return jnp.einsum('bhqk,bhkd->bhqd', probs, v)

    o = lax.map(one_block, (qb, cb, jnp.arange(nb)))
    return o.transpose(1, 2, 0, 3, 4).reshape(b, h, s, d)

def gated_delta_chunked(q, k, v, g, beta):
    b, h, s, dk = q.shape
    dv = v.shape[-1]
    c = CHUNK
    n = s // c
    q = (q * dk ** -0.5).reshape(b, h, n, c, dk)
    k = k.reshape(b, h, n, c, dk)
    v = v.reshape(b, h, n, c, dv)
    beta = beta.reshape(b, h, n, c)
    G = jnp.cumsum(g.reshape(b, h, n, c), axis=-1)
    causal = jnp.tril(jnp.ones((c, c), bool))
    strict = jnp.tril(jnp.ones((c, c), bool), -1)
    decay = jnp.exp(jnp.where(causal, G[..., :, None] - G[..., None, :], -jnp.inf))
    kb = k * beta[..., None]
    m = jnp.where(strict, jnp.einsum('bhnrd,bhnsd->bhnrs', kb, k) * decay, 0.0)
    t_mat = m + jnp.eye(c, dtype=m.dtype)
    w = lax.linalg.triangular_solve(t_mat, kb * jnp.exp(G)[..., None],
                                    left_side=True, lower=True, unit_diagonal=True)
    u = lax.linalg.triangular_solve(t_mat, v * beta[..., None],
                                    left_side=True, lower=True, unit_diagonal=True)
    a_qk = jnp.where(causal, jnp.einsum('bhnrd,bhnsd->bhnrs', q, k) * decay, 0.0)
    q_in = q * jnp.exp(G)[..., None]
    k_out = k * jnp.exp(G[..., -1:] - G)[..., None]
    a_chunk = jnp.exp(G[..., -1])

    def step(state, inp):
        qi, ki, wi, ui, ai_qk, ai = inp
        v_new = ui - jnp.einsum('bhcd,bhde->bhce', wi, state)
        o = jnp.einsum('bhcd,bhde->bhce', qi, state) + jnp.einsum('bhrs,bhse->bhre', ai_qk, v_new)
        state = state * ai[..., None, None] + jnp.einsum('bhcd,bhce->bhde', ki, v_new)
        return state, o

    xs = tuple(jnp.moveaxis(t, 2, 0) for t in (q_in, k_out, w, u, a_qk, a_chunk))
    _, o = lax.scan(step, jnp.zeros((b, h, dk, dv), q.dtype), xs)
    return jnp.moveaxis(o, 0, 2).reshape(b, h, s, dv)

def gla_chunked(q, k, v, log_a, scale):
    b, h, s, dk = q.shape
    dv = v.shape[-1]
    c = LA_BLOCK
    n = s // c
    q = (q * scale).reshape(b, h, n, c, dk)
    k = k.reshape(b, h, n, c, dk)
    v = v.reshape(b, h, n, c, dv)
    G = jnp.cumsum(log_a.reshape(b, h, n, c, dk), axis=3)
    causal = jnp.tril(jnp.ones((c, c), bool))
    rel = jnp.where(causal[:, :, None], G[:, :, :, :, None, :] - G[:, :, :, None, :, :], -jnp.inf)
    a_intra = jnp.einsum('bhnrd,bhnsd,bhnrsd->bhnrs', q, k, jnp.exp(rel))
    o_intra = jnp.einsum('bhnrs,bhnse->bhnre', a_intra, v)
    g_last = G[:, :, :, -1]
    q_in = q * jnp.exp(G)
    k_out = k * jnp.exp(g_last[:, :, :, None, :] - G)
    a_chunk = jnp.exp(g_last)

    def step(state, inp):
        qi, ki, vi, ai = inp
        o = jnp.einsum('bhcd,bhde->bhce', qi, state)
        state = state * ai[..., None] + jnp.einsum('bhcd,bhce->bhde', ki, vi)
        return state, o

    xs = tuple(jnp.moveaxis(t, 2, 0) for t in (q_in, k_out, v, a_chunk))
    _, o_inter = lax.scan(step, jnp.zeros((b, h, dk, dv), q.dtype), xs)
    return (o_intra + jnp.moveaxis(o_inter, 0, 2)).reshape(b, h, s, dv)

def hgrn_lower_bounds(lb_param):
    cs = jnp.cumsum(jax.nn.softmax(lb_param.astype(jnp.float32), axis=0), axis=0)
    return cs - cs[0:1]

def token_mix(h, w_in, fox_qn_g, fox_kn_g, fox_b_f, fox_on_g, gdn_conv_w, gdn_a_log,
              gdn_dt_bias, gdn_on_g, lb, hg_on_g, gla_w_gk, gla_b_gk, gla_on_g):
    p = (h @ w_in).astype(jnp.float32)
    (fox_qkv, fox_f, gdn_qkv, gdn_b, gdn_a, gdn_z, hg_q, hg_f, hg_i, hg_g,
     gla_qk, gla_v, gla_gk, gla_g) = jnp.split(p, _cut_points(IN_SIZES), axis=-1)

    q, k, v = jnp.split(fox_qkv, 3, axis=-1)
    q = rms_norm(split_heads(q, FOX_HEADS), fox_qn_g)
    k = rms_norm(split_heads(k, FOX_HEADS), fox_kn_g)
    log_f = jax.nn.log_sigmoid(fox_f + fox_b_f).transpose(0, 2, 1)
    o_a = rms_norm(fox_attention(q, k, split_heads(v, FOX_HEADS), log_f), fox_on_g)

    qkv = jax.nn.silu(causal_dwconv(gdn_qkv, gdn_conv_w))
    q, k, v = jnp.split(qkv, 3, axis=-1)
    beta = jax.nn.sigmoid(gdn_b).transpose(0, 2, 1)
    g = (-jnp.exp(gdn_a_log) * jax.nn.softplus(gdn_a + gdn_dt_bias)).transpose(0, 2, 1)
    o_b = gated_delta_chunked(l2norm(split_heads(q, GDN_HEADS)), l2norm(split_heads(k, GDN_HEADS)),
                              split_heads(v, GDN_HEADS), g, beta)
    o_b = rms_norm(o_b, gdn_on_g) * jax.nn.silu(split_heads(gdn_z, GDN_HEADS))

    lbh = lb.reshape(HG_HEADS, 1, HG_DK)
    f_logit = split_heads(hg_f, HG_HEADS)
    log_forget = jnp.logaddexp(jnp.log(lbh), jnp.log1p(-lbh) + jax.nn.log_sigmoid(f_logit))
    k_in = (1.0 - lbh) * jax.nn.sigmoid(-f_logit)
    o_c = gla_chunked(jax.nn.silu(split_heads(hg_q, HG_HEADS)), k_in, split_heads(hg_i, HG_HEADS),
                      log_forget, HG_DK ** -0.5)
    o_c = rms_norm(o_c, hg_on_g) * jax.nn.silu(split_heads(hg_g, HG_HEADS))

    q, k = jnp.split(gla_qk, 2, axis=-1)
    log_a = jax.nn.log_sigmoid(gla_gk @ gla_w_gk + gla_b_gk) / GLA_NORM
    o_d = gla_chunked(split_heads(q, GLA_HEADS), split_heads(k, GLA_HEADS), split_heads(gla_v, GLA_HEADS),
                      split_heads(log_a, GLA_HEADS), GLA_DK ** -0.5)
    o_d = rms_norm(o_d, gla_on_g) * jax.nn.silu(split_heads(gla_g, GLA_HEADS))

    return jnp.concatenate([merge_heads(o_a), merge_heads(o_b), merge_heads(o_c), merge_heads(o_d)], axis=-1)

def conv_glu_ffn(h, w_up, conv_w, conv_b, w_down):
    u = causal_dwconv(h @ w_up, conv_w) + conv_b
    gate, up = jnp.split(u, 2, axis=-1)
    return (jax.nn.silu(gate) * up) @ w_down

def first_inputs(seed: int = 0) -> dict:
    key = jax.random.key(seed)
    ks = jax.random.split(key, 24)
    f32 = jnp.float32

    def nrm(k, shape, scale):
        return scale * jax.random.normal(k, shape, f32)

    def gain(k, n):
        return 1.0 + 0.1 * jax.random.normal(k, (DEPTH, n), f32)

    dt = jnp.exp(jax.random.uniform(ks[8], (DEPTH, GDN_HEADS), f32, jnp.log(1e-3), jnp.log(1e-1)))
    return {
        'x': nrm(ks[0], (BATCH, SEQ, D_MODEL), 1.0),
        'norm1_g': gain(ks[1], D_MODEL),
        'w_in': nrm(ks[2], (DEPTH, D_MODEL, IN_COLS), D_MODEL ** -0.5),
        'fox_qn_g': gain(ks[3], FOX_DH),
        'fox_kn_g': gain(ks[4], FOX_DH),
        'fox_b_f': FOX_BIAS_INIT + nrm(ks[5], (DEPTH, FOX_HEADS), 0.1),
        'fox_on_g': gain(ks[6], FOX_DH),
        'gdn_conv_w': nrm(ks[7], (DEPTH, GDN_CONV, 3 * GROUP_W), GDN_CONV ** -0.5),
        'gdn_a_log': jnp.log(jax.random.uniform(ks[9], (DEPTH, GDN_HEADS), f32, 1.0, 16.0)),
        'gdn_dt_bias': dt + jnp.log(-jnp.expm1(-dt)),
        'gdn_on_g': gain(ks[10], GDN_DV),
        'hg_lb': nrm(ks[11], (DEPTH, HG_KW), 0.1),
        'hg_on_g': gain(ks[12], HG_DV),
        'gla_w_gk': nrm(ks[13], (DEPTH, GLA_RANK, GLA_KW), GLA_RANK ** -0.5),
        'gla_b_gk': nrm(ks[14], (DEPTH, GLA_KW), 0.1),
        'gla_on_g': gain(ks[15], GLA_DV),
        'w_out': nrm(ks[16], (DEPTH, D_MIX, D_MODEL), D_MIX ** -0.5),
        'norm2_g': gain(ks[17], D_MODEL),
        'w_up': nrm(ks[18], (DEPTH, D_MODEL, 2 * D_FF), D_MODEL ** -0.5),
        'ffn_conv_w': nrm(ks[19], (DEPTH, FFN_CONV, 2 * D_FF), FFN_CONV ** -0.5),
        'ffn_conv_b': nrm(ks[20], (DEPTH, 2 * D_FF), 0.02),
        'w_down': nrm(ks[21], (DEPTH, D_FF, D_MODEL), D_FF ** -0.5),
    }

def first_block(x, norm1_g, w_in, fox_qn_g, fox_kn_g, fox_b_f, fox_on_g, gdn_conv_w, gdn_a_log,
              gdn_dt_bias, gdn_on_g, hg_lb, hg_on_g, gla_w_gk, gla_b_gk, gla_on_g, w_out,
              norm2_g, w_up, ffn_conv_w, ffn_conv_b, w_down):
    lower_bounds = hgrn_lower_bounds(hg_lb)
    for l in range(DEPTH):
        mixed = token_mix(rms_norm(x, norm1_g[l]), w_in[l], fox_qn_g[l], fox_kn_g[l], fox_b_f[l],
                          fox_on_g[l], gdn_conv_w[l], gdn_a_log[l], gdn_dt_bias[l], gdn_on_g[l],
                          lower_bounds[l], hg_on_g[l], gla_w_gk[l], gla_b_gk[l], gla_on_g[l])
        x = x + mixed.astype(x.dtype) @ w_out[l]
        x = x + conv_glu_ffn(rms_norm(x, norm2_g[l]), w_up[l], ffn_conv_w[l], ffn_conv_b[l], w_down[l])
    return x


DEPTH_2 = 2

N_CONV_LAYERS = DEPTH_2 // 2
N_MLA_LAYERS = DEPTH_2 - N_CONV_LAYERS
CONV_WIDTH = 3
V_HEAD_DIM = 128
N_HEADS = D_MODEL // V_HEAD_DIM
QK_NOPE_DIM = 128
QK_ROPE_DIM = 64
KV_LORA_RANK = D_MODEL // 4
Q_LORA_RANK = 3 * D_MODEL // 8
D_FF_2 = -(-8 * D_MODEL // (3 * 256)) * 256
ROPE_THETA = 10000.0
RMS_EPS = 1e-6


def rms_norm_2(x, g):
    xf = x.astype(jnp.float32)
    y = xf * lax.rsqrt(jnp.mean(xf * xf, axis=-1, keepdims=True) + RMS_EPS)
    return (y * g.astype(jnp.float32)).astype(x.dtype)

def rope_tables(positions):
    inv_freq = ROPE_THETA ** (-jnp.arange(0, QK_ROPE_DIM, 2, dtype=jnp.float32) / QK_ROPE_DIM)
    ang = positions.astype(jnp.float32)[..., None] * inv_freq
    return jnp.cos(ang), jnp.sin(ang)

def apply_rope(x, cos, sin):
    cos = cos.astype(x.dtype)
    sin = sin.astype(x.dtype)
    x1, x2 = jnp.split(x, 2, axis=-1)
    return jnp.concatenate([x1 * cos - x2 * sin, x1 * sin + x2 * cos], axis=-1)

def short_conv_mixer(h, w_in, conv_w, w_out):
    s = h.shape[1]
    u = h @ w_in
    gate_b, gate_c, val = jnp.split(u, 3, axis=-1)
    z = gate_c * val
    zp = jnp.pad(z, ((0, 0), (CONV_WIDTH - 1, 0), (0, 0)))
    conv = sum(conv_w[k] * zp[:, k:k + s] for k in range(CONV_WIDTH))
    return (gate_b * conv) @ w_out

def swiglu_ffn(h, w13, w2):
    g, u = jnp.split(h @ w13, 2, axis=-1)
    return (jax.nn.silu(g) * u) @ w2

def shared_mla_kv(h, kv_norm_g, w_dkv, kv_latent_norm_g, w_ukv, cos, sin):
    b, s, _ = h.shape
    hn = rms_norm_2(h, kv_norm_g)
    ckv = hn @ w_dkv
    c_lat = rms_norm_2(ckv[..., :KV_LORA_RANK], kv_latent_norm_g)
    k_pe = apply_rope(ckv[..., KV_LORA_RANK:], cos, sin)
    kv = (c_lat @ w_ukv).reshape(b, s, N_HEADS, QK_NOPE_DIM + V_HEAD_DIM)
    k_nope, v = kv[..., :QK_NOPE_DIM], kv[..., QK_NOPE_DIM:]
    return k_nope, k_pe, v

def causal_block_attention(q_nope, q_pe, k_nope, k_pe, v):
    b, s = q_nope.shape[:2]
    nb = s // Q_BLOCK
    qn = q_nope.reshape(b, nb, Q_BLOCK, N_HEADS, QK_NOPE_DIM).transpose(1, 0, 2, 3, 4)
    qr = q_pe.reshape(b, nb, Q_BLOCK, N_HEADS, QK_ROPE_DIM).transpose(1, 0, 2, 3, 4)
    starts = jnp.arange(nb, dtype=jnp.int32) * Q_BLOCK
    k_idx = jnp.arange(s, dtype=jnp.int32)
    scale = (QK_NOPE_DIM + QK_ROPE_DIM) ** -0.5
    neg = jnp.finfo(jnp.float32).min

    def one_block(args):
        qn_b, qr_b, start = args
        sc = (jnp.einsum('bqhd,bkhd->bhqk', qn_b, k_nope)
              + jnp.einsum('bqhr,bkr->bhqk', qr_b, k_pe))
        sc = sc.astype(jnp.float32) * scale
        q_idx = start + jnp.arange(Q_BLOCK, dtype=jnp.int32)
        mask = k_idx[None, :] <= q_idx[:, None]
        p = jax.nn.softmax(jnp.where(mask, sc, neg), axis=-1).astype(v.dtype)
        return jnp.einsum('bhqk,bkhd->bqhd', p, v)

    out = lax.map(one_block, (qn, qr, starts))
    return out.transpose(1, 0, 2, 3, 4).reshape(b, s, N_HEADS, V_HEAD_DIM)

def mla_mixer(h, w_dq, q_norm_g, w_uq, w_o, k_nope, k_pe, v, cos_h, sin_h):
    b, s, _ = h.shape
    cq = rms_norm_2(h @ w_dq, q_norm_g)
    q = (cq @ w_uq).reshape(b, s, N_HEADS, QK_NOPE_DIM + QK_ROPE_DIM)
    q_nope = q[..., :QK_NOPE_DIM]
    q_pe = apply_rope(q[..., QK_NOPE_DIM:], cos_h, sin_h)
    attn = causal_block_attention(q_nope, q_pe, k_nope, k_pe, v)
    return attn.reshape(b, s, N_HEADS * V_HEAD_DIM) @ w_o

def second_inputs(seed: int = 0) -> dict:
    key = jax.random.key(seed)
    ks = iter(jax.random.split(key, 32))
    f32 = jnp.float32
    res_scale = (2 * DEPTH_2) ** -0.5

    def w(shape, fan_in, extra=1.0):
        return jax.random.normal(next(ks), shape, f32) * (fan_in ** -0.5) * extra

    def gain(shape):
        return 1.0 + 0.02 * jax.random.normal(next(ks), shape, f32)

    na, nm = N_CONV_LAYERS, N_MLA_LAYERS
    x = jax.random.normal(next(ks), (BATCH, SEQ, D_MODEL), f32)
    positions = jnp.broadcast_to(jnp.arange(SEQ, dtype=jnp.int32), (BATCH, SEQ))
    return {
        "x": x,
        "positions": positions,
        "conv_norm_g": gain((na, D_MODEL)),
        "conv_w_in": w((na, D_MODEL, 3 * D_MODEL), D_MODEL),
        "conv_w": w((na, CONV_WIDTH, D_MODEL), CONV_WIDTH),
        "conv_w_out": w((na, D_MODEL, D_MODEL), D_MODEL, res_scale),
        "conv_ffn_norm_g": gain((na, D_MODEL)),
        "conv_ffn_w13": w((na, D_MODEL, 2 * D_FF_2), D_MODEL),
        "conv_ffn_w2": w((na, D_FF_2, D_MODEL), D_FF_2, res_scale),
        "kv_norm_g": gain((D_MODEL,)),
        "w_dkv": w((D_MODEL, KV_LORA_RANK + QK_ROPE_DIM), D_MODEL),
        "kv_latent_norm_g": gain((KV_LORA_RANK,)),
        "w_ukv": w((KV_LORA_RANK, N_HEADS * (QK_NOPE_DIM + V_HEAD_DIM)), KV_LORA_RANK),
        "mla_norm_g": gain((nm, D_MODEL)),
        "mla_w_dq": w((nm, D_MODEL, Q_LORA_RANK), D_MODEL),
        "mla_q_norm_g": gain((nm, Q_LORA_RANK)),
        "mla_w_uq": w((nm, Q_LORA_RANK, N_HEADS * (QK_NOPE_DIM + QK_ROPE_DIM)), Q_LORA_RANK),
        "mla_w_o": w((nm, N_HEADS * V_HEAD_DIM, D_MODEL), N_HEADS * V_HEAD_DIM, res_scale),
        "mla_ffn_norm_g": gain((nm, D_MODEL)),
        "mla_ffn_w13": w((nm, D_MODEL, 2 * D_FF_2), D_MODEL),
        "mla_ffn_w2": w((nm, D_FF_2, D_MODEL), D_FF_2, res_scale),
        "final_norm_g": gain((D_MODEL,)),
    }

def second_block(x, positions,
              conv_norm_g, conv_w_in, conv_w, conv_w_out,
              conv_ffn_norm_g, conv_ffn_w13, conv_ffn_w2,
              kv_norm_g, w_dkv, kv_latent_norm_g, w_ukv,
              mla_norm_g, mla_w_dq, mla_q_norm_g, mla_w_uq, mla_w_o,
              mla_ffn_norm_g, mla_ffn_w13, mla_ffn_w2,
              final_norm_g):
    cos, sin = rope_tables(positions)
    cos_h, sin_h = cos[:, :, None, :], sin[:, :, None, :]
    h = x
    k_nope = k_pe = v = None
    for i in range(DEPTH_2):
        if i < N_CONV_LAYERS:
            h = h + short_conv_mixer(rms_norm_2(h, conv_norm_g[i]), conv_w_in[i], conv_w[i], conv_w_out[i])
            h = h + swiglu_ffn(rms_norm_2(h, conv_ffn_norm_g[i]), conv_ffn_w13[i], conv_ffn_w2[i])
        else:
            if i == N_CONV_LAYERS:
                k_nope, k_pe, v = shared_mla_kv(h, kv_norm_g, w_dkv, kv_latent_norm_g, w_ukv, cos, sin)
            j = i - N_CONV_LAYERS
            h = h + mla_mixer(rms_norm_2(h, mla_norm_g[j]), mla_w_dq[j], mla_q_norm_g[j], mla_w_uq[j],
                              mla_w_o[j], k_nope, k_pe, v, cos_h, sin_h)
            h = h + swiglu_ffn(rms_norm_2(h, mla_ffn_norm_g[j]), mla_ffn_w13[j], mla_ffn_w2[j])
    return rms_norm_2(h, final_norm_g)


def setup_inputs(seed=0):
    out = dict(first_inputs(seed))
    for name, value in second_inputs(seed + 1).items():
        if name != "x":
            out[name + "_2"] = value
    return out


def reference(
    x, norm1_g, w_in, fox_qn_g, fox_kn_g, fox_b_f, fox_on_g, gdn_conv_w, gdn_a_log, gdn_dt_bias,
    gdn_on_g, hg_lb, hg_on_g, gla_w_gk, gla_b_gk, gla_on_g, w_out, norm2_g, w_up, ffn_conv_w,
    ffn_conv_b, w_down, positions_2, conv_norm_g_2, conv_w_in_2, conv_w_2, conv_w_out_2,
    conv_ffn_norm_g_2, conv_ffn_w13_2, conv_ffn_w2_2, kv_norm_g_2, w_dkv_2, kv_latent_norm_g_2,
    w_ukv_2, mla_norm_g_2, mla_w_dq_2, mla_q_norm_g_2, mla_w_uq_2, mla_w_o_2, mla_ffn_norm_g_2,
    mla_ffn_w13_2, mla_ffn_w2_2, final_norm_g_2,
):
    x = first_block(
        x, norm1_g, w_in, fox_qn_g, fox_kn_g, fox_b_f, fox_on_g, gdn_conv_w, gdn_a_log,
        gdn_dt_bias, gdn_on_g, hg_lb, hg_on_g, gla_w_gk, gla_b_gk, gla_on_g, w_out, norm2_g,
        w_up, ffn_conv_w, ffn_conv_b, w_down,
    )
    return second_block(
        x, positions_2, conv_norm_g_2, conv_w_in_2, conv_w_2, conv_w_out_2, conv_ffn_norm_g_2,
        conv_ffn_w13_2, conv_ffn_w2_2, kv_norm_g_2, w_dkv_2, kv_latent_norm_g_2, w_ukv_2,
        mla_norm_g_2, mla_w_dq_2, mla_q_norm_g_2, mla_w_uq_2, mla_w_o_2, mla_ffn_norm_g_2,
        mla_ffn_w13_2, mla_ffn_w2_2, final_norm_g_2,
    )


_drawn_inputs = setup_inputs


def setup_inputs(seed=0):
    import zlib

    import numpy as np

    out = dict(_drawn_inputs(seed))
    spreads = {}
    factors = {'fox_b_f': 17.342,
     'gla_b_gk': 4.251,
     'ffn_conv_b': 3.886,
     'conv_norm_g_2': 4.487,
     'conv_ffn_norm_g_2': 27.13,
     'kv_norm_g_2': 40.593,
     'kv_latent_norm_g_2': 47.072,
     'mla_norm_g_2': 41.852,
     'mla_q_norm_g_2': 41.572,
     'mla_ffn_norm_g_2': 39.276,
     'final_norm_g_2': 7.994}
    for name, (base, spread) in spreads.items():
        noise = np.random.default_rng([zlib.crc32(name.encode()), seed]).standard_normal(out[name].shape)
        drawn = base * np.exp(spread * noise) if base else spread * noise
        out[name] = jnp.asarray(drawn.astype(out[name].dtype))
    for name, factor in factors.items():
        out[name] = (out[name] * factor).astype(out[name].dtype)
    return out
```

```python
import numpy as np
import concourse.bass as bass
from concourse import mybir
from contextlib import ExitStack

F32 = mybir.dt.float32
F32R = mybir.dt.float32r
I32 = mybir.dt.int32
ALU = mybir.AluOpType
ACT = mybir.ActivationFunctionType
AX = mybir.AxisListType

P = 128
T = 512
D = 1024
KT = D // P
TT = T // P
DH = 64
FF = 2816
FT = FF // P
THIRDS = ((0, 8), (8, 7), (15, 7))
GC = 64
LC = 16
NL = T // LC
NH2 = 8
EPS = 1e-6
UNIT = KT * P
RAW = 4
PARTS = 2

_LEVELS = [1, 2, 4, 8, 16, 32]
_COLS = {}


def _lay():
    at = 0
    sizes = [("ident", P), ("hsum", P), ("ones", P), ("neg", P), ("incl", P)]
    sizes += [(f"lev{b}", P) for b in _LEVELS]
    sizes += [("gla0", P), ("gla1", P), ("perm", P)]
    sizes += [(f"foxrow{h}", P) for h in range(4)] + [(f"gdnrow{h}", P) for h in range(4)]
    sizes += [(f"beta{p}", P) for p in range(2)] + [(f"gpair{p}", P) for p in range(2)]
    sizes += [("cmask", 8), ("hmask", 2), ("qmask", 4), ("freq", 1), ("sign", 1), ("eps", 1)]
    for name, n in sizes:
        _COLS[name] = (at, n)
        at += n
    return at


NCONST = _lay()


def constants():
    c = np.zeros((P, NCONST), np.float32)

    def put(name, a):
        at, n = _COLS[name]
        c[:, at:at + n] = a

    i = np.arange(P)
    s, r = i[:, None], i[None, :]
    put("ident", s == r)
    put("hsum", s // DH == r // DH)
    put("ones", 1.0)
    put("neg", np.where(r > s, -1e30, 0.0))
    put("incl", (s // GC == r // GC) & (s <= r))
    for b in _LEVELS:
        put(f"lev{b}", (s // (2 * b) == r // (2 * b)) & (s % (2 * b) < b) & (r % (2 * b) >= b))
    for w in range(2):
        put(f"gla{w}", s // 32 == 2 * w + r // DH)
    put("perm", (s // 64 == r // 64) & (s % 64 == (r + 32) % 64))
    for h in range(4):
        put(f"foxrow{h}", (s == h) & (r >= 0))
        put(f"gdnrow{h}", (s == 64 + h) & (r >= 0))
    for p in range(2):
        put(f"beta{p}", s == 32 + 2 * p + r // DH)
        put(f"gpair{p}", s == 64 + 2 * p + r // DH)
    put("cmask", i[:, None] // LC == np.arange(8)[None, :])
    put("hmask", i[:, None] // 64 == np.arange(2)[None, :])
    put("qmask", i[:, None] // 32 == np.arange(4)[None, :])
    inv = np.float32(10000.0) ** (-np.arange(0, 64, 2, dtype=np.float32) / np.float32(64))
    put("freq", inv[i % 32][:, None])
    put("sign", np.where(i % 64 < 32, -1.0, 1.0)[:, None])
    put("eps", EPS)
    return c


_ROWS = {}
_row_at = 0
for _name, _n in [("norm1_g", 8), ("norm2_g", 8), ("conv_norm_g_2", 8), ("conv_ffn_norm_g_2", 8), ("kv_norm_g_2", 8),
                  ("mla_norm_g_2", 8), ("mla_ffn_norm_g_2", 8), ("final_norm_g_2", 8), ("kv_latent_norm_g_2", 2),
                  ("mla_q_norm_g_2", 3), ("conv_w_2", 24), ("gdn_conv_w", 24), ("gla_b_gk", 1), ("fox_qn_g", 1),
                  ("fox_kn_g", 1), ("fox_on_g", 1), ("gdn_on_g", 1), ("hg_on_g", 1), ("gla_on_g", 1)]:
    _ROWS[_name] = (_row_at, _n)
    _row_at += _n
NROW0 = _row_at
NCONVW = 3 * 2 * FT
NROW1 = P
NROW2 = NCONVW - P + 2 * FT
NPCOL = NROW0 + NROW1 + NROW2

UNITS = []
FIRST = {}


def _units():
    def add(stage, name, kt, pieces):
        FIRST.setdefault(stage, len(UNITS))
        UNITS.append((name, kt, sum(n for _, _, n in pieces), pieces))

    gdn, z, hg, gla, gk, gg = 772, 1548, 1804, 2828, 3340, 3356
    add("w_in", "w_in", KT, [(0, 768, 32), (0, 1540, 32), (0, 1544, 32), (0, gk, 32)])
    for c in [gdn + P * i for i in range(6)] + [z, z + P]:
        add("w_in", "w_in", KT, [(0, c, P)])
    for c in [gla, gla + P, gla + 2 * P, gla + 3 * P, gg, gg + P]:
        add("w_in", "w_in", KT, [(0, c, P)])
    for i in range(8):
        add("w_in", "w_in", KT, [(0, hg + P * i, P)])
    for i in range(6):
        add("w_in", "w_in", KT, [(0, P * i, P)])
    for i in range(KT):
        add("w_out", "w_out", KT, [(0, P * i, P)])

    def ffn(stage, up, down):
        for i in range(FT):
            add(stage + "_up", up, KT, [(0, P * i, P)])
            add(stage + "_up", up, KT, [(0, FF + P * i, P)])
        for i in range(KT):
            for k0, k in THIRDS:
                add(stage + "_down", down, k, [(k0 * P, P * i, P)])

    ffn("ffn1", "w_up", "w_down")
    for i in range(KT):
        for part in range(3):
            add("conv_in", "conv_w_in_2", KT, [(0, part * D + P * i, P)])
    for i in range(KT):
        add("conv_out", "conv_w_out_2", KT, [(0, P * i, P)])
    ffn("ffn2", "conv_ffn_w13_2", "conv_ffn_w2_2")
    for c in [0, P, P + 64]:
        add("dkv", "w_dkv_2", KT, [(0, c, P)])
    for i in range(3):
        add("dq", "mla_w_dq_2", KT, [(0, P * i, P)])
    for part in range(2):
        for g in range(2):
            add("ukv", "w_ukv_2", 2, [(0, (4 * g + h) * 256 + part * P, P) for h in range(4)])
    for g in range(2):
        for p in range(2):
            add("uq", "mla_w_uq_2", 3, [(0, 192 * (4 * g + 2 * p + h), P) for h in range(2)])
        add("uq", "mla_w_uq_2", 3, [(0, 192 * (4 * g + h) + P, 64) for h in range(4)])
    for i in range(KT):
        add("w_o", "mla_w_o_2", KT, [(0, P * i, P)])
    ffn("ffn3", "mla_ffn_w13_2", "mla_ffn_w2_2")


_units()
LOADED = []
_sum = [0] * RAW
for _u, (_n, _k, _c, _pieces) in enumerate(UNITS):
    _sum[_u % RAW] += 16 * len(_pieces)
    LOADED.append(_sum[_u % RAW])


class Steps:

    def __init__(self, sems, known):
        self.sems, self.known = sems, known
        self.count = dict.fromkeys(sems, 0)
        self.at, self.banks, self.ring, self.last = {}, {}, 0, {}

    def step(self, engine, name):
        assert name not in self.at, name
        self.count[engine] += 1
        self.at[name] = (engine, self.count[engine])
        return self.sems[engine], 1

    def after(self, name):
        if self.known is None:
            return self.sems["dve"], 1
        engine, value = self.known.at[name]
        return self.sems[engine], value

    def take_bank(self, key, n):
        b = self.ring % n
        self.ring += 1
        self.banks[key] = b
        before = self.last.get(b)
        self.last[b] = key
        return b, before

    def bank(self, key):
        return self.known.banks[key] if self.known else 0



TILE0, NORM0, PAIR0 = {}, {}, {}
_t = _p = 0
for _s in ["w_out", "ffn1_up", "ffn1_down", "conv_in", "conv_out", "ffn2_up", "ffn2_down", "w_o", "ffn3_up", "ffn3_down"]:
    if _s == "conv_in" or _s.endswith("_up"):
        _n = KT if _s == "conv_in" else FT
        TILE0[_s], PAIR0[_s] = _t, _p
        _t += (3 if _s == "conv_in" else 2) * _n
        _p += _n
    else:
        NORM0[_s] = KT * (1 + len(NORM0))


def build(nc, A, cst_d, out_d, known):
    ctx = ExitStack()
    with ctx:
        def sb(name, shape, dt=F32, c=ctx):
            return c.enter_context(nc.sbuf_tensor(name, shape, dt))

        def sem(name):
            return ctx.enter_context(nc.semaphore(name))

        xT = sb("xT", [P, KT, T])
        xhi = sb("xhi", [P, KT, T], F32R)
        xlo = sb("xlo", [P, KT, T], F32R)
        raw = sb("raw", [P, RAW, UNIT])
        whi = sb("whi", [P, PARTS, UNIT], F32R)
        wlo = sb("wlo", [P, PARTS, UNIT], F32R)
        cst = sb("cst", [P, NCONST])
        pcol = sb("pcol", [P, NPCOL])
        gbias = sb("gbias", [P, 4])
        sq = sb("sq", [P, 2, T])
        ssq = sb("ssq", [P, T])
        rs = sb("rs", [P, T])
        xg = sb("xg", [P, 2, T])
        stat = sb("stat", [P, 4, 4])
        ps = ctx.enter_context(nc.psum_tensor("ps", [P, 8, T], F32))
        NRING = 6

        def acc(tile):
            return ps[:, tile % 2, :]

        def ring(b):
            return ps[:, 2 + b, :]

        def C(name):
            at, n = _COLS[name]
            return cst[:, at:at + n]

        def par(name, k=0):
            return pcol[:, _ROWS[name][0] + k:_ROWS[name][0] + k + 1]

        def tile_of(buf, m):
            return buf[:, bass.ds(m, 1), :].rearrange("p o t -> p (o t)")

        S = Steps({e: sem(f"{e}_steps") for e in ("pe", "act", "dve", "pool")}, known)
        step, after = S.step, S.after
        unit_loaded = [sem(f"unit_loaded{i}") for i in range(RAW)]
        hi_split, lo_split, unit_used = sem("hi_split"), sem("lo_split"), sem("unit_used")
        tile_free = [sem(f"tile_free{i}") for i in range(2)]
        residual, squared, summed = sem("residual"), sem("squared"), sem("summed")
        tap_done, tap2_done, gated = sem("tap_done"), sem("tap2_done"), sem("gated")
        prod_done, prod_hi, prod_lo = sem("prod_done"), sem("prod_hi"), sem("prod_lo")
        cst_loaded, x_loaded, rows_loaded, small_loaded = (sem(n) for n in
                                                           ("cst_loaded", "x_loaded", "rows_loaded", "small_loaded"))
        pos_loaded, stored = sem("pos_loaded"), sem("stored")
        v, a, g, t_ = nc.vector, nc.scalar, nc.gpsimd, nc.tensor

        def f32(ap):
            return ap.bitcast(F32)

        def pe_ring(pe, key):
            b, before = S.take_bank(key, NRING)
            if before is not None:
                pe.wait_ge(*after(f"{before} taken"))
            return ring(b)

        def full(eng, key):
            eng.wait_ge(*after(f"{key} full"))
            return ring(S.bank(key))

        def unit_view(buf, u):
            _, kt, n, _ = UNITS[u]
            return buf[:, u % (RAW if buf is raw else PARTS), 0:kt * n].rearrange("p (k c) -> p k c", c=n)

        def is_past(u, i, per):
            return u + (per * i if isinstance(i, int) else 0) >= len(UNITS)

        def in_loop(value, i, per):
            return value if i is None else value + per * i

        def load_unit(sp, u):
            name, kt, n, pieces = UNITS[u]
            if u >= RAW:
                sp.wait_ge(lo_split, u - RAW + 1)
            at = 0
            for r0, c0, m in pieces:
                dst = unit_view(raw, u)[:, :, at:at + m]
                src = A[name][r0:r0 + kt * P, c0:c0 + m].rearrange("(k p) c -> p k c", p=P)
                sp.dma_start(dst, src).then_inc(unit_loaded[u % RAW], 16)
                at += m

        def load_loop(sp, stage, n_units, per, col):
            with sp.Fori(0, n_units // per) as i:
                for j in range(per):
                    u = FIRST[stage] + j
                    name, kt, n, pieces = UNITS[u]
                    r0 = pieces[0][0]
                    sp.wait_ge(lo_split, u - RAW + 1 + per * i)
                    src = A[name][r0:r0 + kt * P, bass.ds(col(i, j), n)].rearrange("(k p) c -> p k c", p=P)
                    sp.dma_start(unit_view(raw, u), src).then_inc(unit_loaded[u % RAW], 16)

        def split_hi(act, u, i=None, per=0):
            if is_past(u, i, per):
                return
            n = UNITS[u][1] * UNITS[u][2]
            act.wait_ge(unit_loaded[u % RAW], in_loop(LOADED[u], i, 16 * per // RAW))
            if u >= PARTS:
                act.wait_ge(unit_used, in_loop(u - PARTS + 1, i, per))
            a.activation(whi[:, u % PARTS, 0:n], raw[:, u % RAW, 0:n], ACT.Copy).then_inc(hi_split, 1)

        def split_lo(dve, u, i=None, per=0):
            if is_past(u, i, per):
                return
            n = UNITS[u][1] * UNITS[u][2]
            dve.wait_ge(hi_split, in_loop(u + 1, i, per))
            v.tensor_tensor(wlo[:, u % PARTS, 0:n], raw[:, u % RAW, 0:n], f32(whi[:, u % PARTS, 0:n]),
                            ALU.subtract).then_inc(lo_split, 1)

        def passes(out, wh, wl, xh, xl, first, last):
            t_.matmul(out, wh, xh, start=first, stop=False)
            t_.matmul(out, wh, xl, start=False, stop=False)
            return t_.matmul(out, wl, xh, start=False, stop=last)

        def product(pe, u, tile, i=None, per=0, x=(xhi, xlo), k0=0, start=True, stop=True, ready=None, cols=0,
                    full=None):
            kt = UNITS[u][1]
            pe.wait_ge(lo_split, in_loop(u + 1, i, per))
            for k in range(kt):
                if ready is not None:
                    pe.wait_ge(*after(f"{ready} lo{k}"))
                wh, wl = (unit_view(b, u)[:, k, cols:cols + P] for b in (whi, wlo))
                last = passes(acc(tile), wh, wl, x[0][:, k0 + k, :], x[1][:, k0 + k, :],
                              start and k == 0, stop and k == kt - 1)
            last.then_inc(*(step("pe", full) if full else (unit_used, 1)))

        def pe_sum(pe, name, n0):
            out = pe_ring(pe, f"{name} sum")
            pe.wait_ge(summed, n0 + KT + 2)
            t_.matmul(out, C("ones"), ssq[:, :], start=True, stop=True).then_inc(*step("pe", f"{name} sum full"))

        def act_rstd(act, name, width, out):
            key = f"{name} sum"
            a.preload_act_table_set("natural_log_exp_and_others")
            bank = full(act, key)
            a.activation(out, bank, ACT.Ln, scale=1.0 / width, bias=C("eps")).then_inc(*step("act", f"{key} taken"))
            act.wait_ge(*after(f"{key} taken"))
            a.activation(out, out, ACT.Exp, scale=-0.5).then_inc(*step("act", f"{name} rstd"))

        def dve_scale(dve, name, tiles, src, gain, hi, lo, rstd, r, before=None):
            def low(k):
                dve.wait_ge(*after(f"{name} hi{k}"))
                v.tensor_tensor(lo[:, k, :], xg[:, k % 2, :], f32(hi[:, k, :]),
                                ALU.subtract).then_inc(*step("dve", f"{name} lo{k}"))
            dve.wait_ge(*after(rstd))
            if before:
                dve.wait_ge(*after(before))
            for k in range(tiles):
                if k >= 2:
                    dve.wait_ge(*after(f"{name} lo{k - 2}"))
                v.scalar_tensor_tensor(xg[:, k % 2, :], src[:, k, :], par(gain, k), r, ALU.mult,
                                       ALU.mult).then_inc(*step("dve", f"{name} scaled{k}"))
                if k:
                    low(k - 1)
            low(tiles - 1)

        def act_hi(act, name, tiles, hi, used=0):
            if used:
                act.wait_ge(unit_used, used)
            for k in range(tiles):
                act.wait_ge(*after(f"{name} scaled{k}"))
                a.activation(hi[:, k, :], xg[:, k % 2, :], ACT.Copy).then_inc(*step("act", f"{name} hi{k}"))

        def pe_residual(pe, stage, thirds, x, ready):
            per, parts = (12, THIRDS) if thirds else (4, ((0, KT),))
            tiles, r0 = per // len(parts), NORM0[stage] - KT
            ready(pe)
            with pe.Fori(0, KT // tiles) as i:
                for j in range(per):
                    m, part = divmod(j, len(parts))
                    if part == 0:
                        pe.wait_ge(residual, r0 + m + 1 + tiles * i)
                    product(pe, FIRST[stage] + j, m, i, per, x, parts[part][0], part == 0, part == len(parts) - 1)

        def rounds(engine, stage, n, body):
            last = FIRST[stage] + n * 12 == len(UNITS)
            with engine.Fori(0, n - last) as i:
                body(i)
            if last:
                body(n - 1)

        def act_residual(act, stage, thirds):
            per, np_ = (12, 3) if thirds else (4, 1)
            tiles, n0 = per // np_, NORM0[stage]

            def body(i):
                for j in range(per):
                    split_hi(act, FIRST[stage] + j + 1, i, per)
                    if j % np_ == np_ - 1:
                        m = j // np_
                        act.wait_ge(residual, n0 - KT + m + 3 + tiles * i)
                        act.wait_ge(summed, n0 + m + 1 + tiles * i)
                        a.activation(sq[:, m % 2, :], tile_of(xT, m + tiles * i), ACT.Square).then_inc(squared, 1)
            rounds(act, stage, KT // tiles, body)

        def dve_residual(dve, stage, thirds):
            per, np_ = (12, 3) if thirds else (4, 1)
            tiles, n0 = per // np_, NORM0[stage]
            dve.wait_ge(*after(f"{stage} sum cleared"))

            def body(i):
                for j in range(per):
                    split_lo(dve, FIRST[stage] + j + 1, i, per)
                    if j % np_ == np_ - 1:
                        m = j // np_
                        dve.wait_ge(unit_used, FIRST[stage] + j + 1 + per * i)
                        x = tile_of(xT, m + tiles * i)
                        v.tensor_tensor(x, acc(m), x, ALU.add).then_inc(residual, 1)
                        dve.wait_ge(squared, n0 + m + 1 + tiles * i)
                        dve.wait_ge(summed, n0 + m + 2 + tiles * i)
                        v.tensor_tensor(ssq[:, :], ssq[:, :], sq[:, m % 2, :], ALU.add).then_inc(summed, 1)
            rounds(dve, stage, KT // tiles, body)

        def pool_clear(pool, stage, reader):
            pool.wait_ge(*after(reader))
            g.memset(ssq[:, :], 0.0).then_inc(*step("pool", f"{stage} sum cleared"))

        def ffn_w(k, m):
            return pcol[:, bass.ds(NROW0 + k * 2 * FT + m, 1)]

        def ffn_b(m):
            return pcol[:, bass.ds(NROW0 + NCONVW + m, 1)]

        def pe_up(pe, stage, conv, name):
            n0, p0 = TILE0[stage], PAIR0[stage]
            for k in range(KT):
                pe.wait_ge(*after(f"{name} lo{k}"))
            with pe.Fori(0, FT // 2) as i:
                for j in range(4):
                    if conv or j % 2 == 0:
                        pe.wait_ge(tile_free[j % 2], n0 // 2 + j // 2 + 1 + 2 * i)
                    else:
                        pe.wait_ge(prod_done, p0 + j // 2 + 2 + 2 * i)
                    product(pe, FIRST[stage] + j, j, i, 4)

        def act_up(act, stage, conv, h_hi, yg, yu):
            u0, p0, n0 = FIRST[stage], PAIR0[stage], TILE0[stage]
            a.preload_act_table_set("silu_and_others")
            with act.Fori(0, FT // 2) as i:
                for j in range(4):
                    pair, is_up = j // 2, j % 2
                    m = pair + 2 * i
                    split_hi(act, u0 + j + 1, i, 4)
                    act.wait_ge(prod_done, p0 + pair + 1 + 2 * i)
                    if conv and is_up:
                        act.wait_ge(tile_free[0], n0 // 2 + pair + 2 + 2 * i)
                        a.activation(yg[:, pair, :], yg[:, pair, :], ACT.Silu).then_inc(gated, 1)
                    if conv or not is_up:
                        act.wait_ge(unit_used, u0 + j + 1 + 4 * i)
                    if conv:
                        mt = m + FT * is_up
                        a.activation((yu if is_up else yg)[:, pair, :], acc(j), ACT.Identity, scale=ffn_w(2, mt),
                                     bias=ffn_b(mt)).then_inc(tap_done, 1)
                    elif not is_up:
                        a.activation(yg[:, pair, :], acc(j), ACT.Silu).then_inc(tile_free[0], 1)
                    if is_up:
                        act.wait_ge(prod_done, p0 + pair + 3 + 2 * i)
                        a.activation(tile_of(h_hi, m), xg[:, pair, :], ACT.Copy).then_inc(prod_hi, 1)

        def dve_up(dve, stage, conv, h_hi, h_lo, yg, yu):
            u0, p0, n0 = FIRST[stage], PAIR0[stage], TILE0[stage]
            with dve.Fori(0, FT // 2) as i:
                for j in range(4):
                    pair, is_up = j // 2, j % 2
                    m = pair + 2 * i
                    split_lo(dve, u0 + j + 1, i, 4)
                    if conv:
                        y, mt = (yu if is_up else yg)[:, pair, :], m + FT * is_up
                        dve.wait_ge(tap_done, j + 1 + 4 * i)
                        v.scalar_tensor_tensor(y[:, 1:T], acc(j)[:, 0:T - 1], ffn_w(1, mt), y[:, 1:T], ALU.mult,
                                               ALU.add).then_inc(tap2_done, 1)
                        dve.wait_ge(tap2_done, j + 1 + 4 * i)
                        v.scalar_tensor_tensor(y[:, 2:T], acc(j)[:, 0:T - 2], ffn_w(0, mt), y[:, 2:T], ALU.mult,
                                               ALU.add).then_inc(tile_free[j % 2], 1)
                    if is_up:
                        if conv:
                            dve.wait_ge(tile_free[1], n0 // 2 + pair + 2 + 2 * i)
                            dve.wait_ge(gated, pair + 1 + 2 * i)
                            v.tensor_tensor(xg[:, pair, :], yg[:, pair, :], yu[:, pair, :],
                                            ALU.mult).then_inc(prod_done, 1)
                        else:
                            dve.wait_ge(tile_free[0], n0 // 2 + pair + 2 + 2 * i)
                            dve.wait_ge(unit_used, u0 + j + 1 + 4 * i)
                            v.tensor_tensor(xg[:, pair, :], yg[:, pair, :], acc(j), ALU.mult).then_inc(prod_done, 1)
                        dve.wait_ge(prod_hi, p0 + pair + 1 + 2 * i)
                        v.tensor_tensor(tile_of(h_lo, m), xg[:, pair, :], f32(tile_of(h_hi, m)),
                                        ALU.subtract).then_inc(prod_lo, 1)

        def pe_conv_in(pe):
            n0 = TILE0["conv_in"]
            for k in range(KT):
                pe.wait_ge(*after(f"conv norm lo{k}"))
            with pe.Fori(0, KT // 4) as i:
                for j in range(12):
                    pe.wait_ge(tile_free[j % 2], n0 // 2 + j // 2 + 1 + 6 * i)
                    product(pe, FIRST["conv_in"] + j, j, i, 12)

        def act_conv_in(act, h_hi, bS, cS):
            u0, p0 = FIRST["conv_in"], PAIR0["conv_in"]
            with act.Fori(0, KT // 4) as i:
                for j in range(12):
                    m, part = divmod(j, 3)
                    split_hi(act, u0 + j + 1, i, 12)
                    if part < 2:
                        act.wait_ge(unit_used, u0 + j + 1 + 12 * i)
                        act.wait_ge(prod_done, p0 + m + 1 + 4 * i)
                        a.activation((bS, cS)[part][:, m % 2, :], acc(j), ACT.Copy).then_inc(tile_free[j % 2], 1)
                    else:
                        act.wait_ge(prod_done, p0 + m + 3 + 4 * i)
                        a.activation(tile_of(h_hi, m + 4 * i), xg[:, m % 2, :], ACT.Copy).then_inc(prod_hi, 1)

        def dve_conv_in(dve, h_hi, h_lo, bS, cS, zS, yS):
            u0, p0, n0 = FIRST["conv_in"], PAIR0["conv_in"], TILE0["conv_in"]
            with dve.Fori(0, KT // 4) as i:
                for j in range(12):
                    m, part = divmod(j, 3)
                    split_lo(dve, u0 + j + 1, i, 12)
                    if part < 2:
                        continue
                    z, y, mi = zS[:, m % 2, :], yS[:, m % 2, :], m + 4 * i
                    w = [pcol[:, bass.ds(_ROWS["conv_w_2"][0] + KT * k + m + 4 * i, 1)] for k in range(3)]
                    c0 = 2 * FT + 3 * m + 12 * i
                    dve.wait_ge(unit_used, u0 + j + 1 + 12 * i)
                    dve.wait_ge(tile_free[(j - 1) % 2], n0 // 2 + (j - 1) // 2 + 2 + 6 * i)
                    v.tensor_tensor(z, cS[:, m % 2, :], acc(j), ALU.mult).then_inc(tile_free[j % 2], 1)
                    dve.wait_ge(tile_free[j % 2], n0 // 2 + j // 2 + 2 + 6 * i)
                    v.tensor_scalar(y, z, w[2], None, ALU.mult).then_inc(tap2_done, 1)
                    dve.wait_ge(tap2_done, c0 + 1)
                    v.scalar_tensor_tensor(y[:, 1:T], z[:, 0:T - 1], w[1], y[:, 1:T], ALU.mult,
                                           ALU.add).then_inc(tap2_done, 1)
                    dve.wait_ge(tap2_done, c0 + 2)
                    v.scalar_tensor_tensor(y[:, 2:T], z[:, 0:T - 2], w[0], y[:, 2:T], ALU.mult,
                                           ALU.add).then_inc(tap2_done, 1)
                    dve.wait_ge(tap2_done, c0 + 3)
                    v.tensor_tensor(xg[:, m % 2, :], y, bS[:, m % 2, :], ALU.mult).then_inc(prod_done, 1)
                    dve.wait_ge(prod_hi, p0 + m + 1 + 4 * i)
                    v.tensor_tensor(tile_of(h_lo, mi), xg[:, m % 2, :], f32(tile_of(h_hi, mi)),
                                    ALU.subtract).then_inc(prod_lo, 1)

        mixers = ctx.enter_context(ExitStack())
        mx = sb("mx", [P, 36, T], c=mixers)
        mixT = sb("mixT", [P, KT, T], c=mixers)
        graw = sb("graw", [P, T], c=mixers)
        grow = sb("grow", [P, T], c=mixers)
        gcol = sb("gcol", [P, TT, P], c=mixers)
        ecol = sb("ecol", [P, TT, 36], c=mixers)
        lastone = sb("lastone", [P, T], c=mixers)
        vnew = sb("vnew", [P, 2, 4 * DH], c=mixers)
        state = sb("state", [P, 2, P], c=mixers)
        wgk = sb("wgk", [P, P], c=mixers)
        hr = (rs[:, :], ssq[:, :])
        wide = mx[:, :, :].rearrange("p a t -> p (a t)")

        def wtile(k, n):
            return wide[:, k * T:(k + n) * T]

        xtok = wtile(0, 8).rearrange("p (t d) -> p t d", d=D)
        prow = wtile(8, 1).rearrange("p (n c) -> p n c", c=P)
        scanmask = mx[:, 35, :]
        Q, K, V = 0, 2, 4
        KZ, KB, MTt, X_, XT_, AT, Y = 10, 14, 16, 20, 24, 28, 32
        kbg, vb, kout, wT = wtile(10, 2), wtile(12, 2), wtile(4, 2), wtile(14, 2)
        kbg, vb, kout = (b.rearrange("p (t c) -> p t c", t=TT) for b in (kbg, vb, kout))
        wT = wT.rearrange("p (h t) -> p h t", h=2)
        uu, oo = (wtile(k, 2).rearrange("p (t c) -> p t c", t=TT) for k in (32, 34))

        def sp_load_inputs(sp):
            for t in range(TT):
                sp.dma_start(xtok[:, t, :], A["x"][0, t * P:(t + 1) * P, :]).then_inc(x_loaded, 16)

        N_SMALL = 4

        def act_load_inputs(act):
            act.dma_start(cst[:, :], cst_d).then_inc(cst_loaded, 16)
            n = 0
            act.wait_ge(*after("rows cleared"))
            for name, (r0, rows) in _ROWS.items():
                src = A[name]
                if src.shape[-1] == DH:
                    row = src if len(src.shape) == 2 else src.rearrange("(o n) -> o n", o=1)
                    for half in range(2):
                        act.dma_start(prow[r0:r0 + 1, 0, half * DH:(half + 1) * DH], row).then_inc(rows_loaded, 16)
                        n += 1
                    continue
                if len(src.shape) == 1:
                    src = src.rearrange("(m c) -> m c", c=P)
                elif len(src.shape) == 2:
                    src = src.rearrange("o (m c) -> (o m) c", c=P)
                else:
                    src = src.rearrange("o k (m c) -> (o k m) c", c=P)
                act.dma_start(prow[r0:r0 + rows, 0, :], src).then_inc(rows_loaded, 16)
                n += 1
            w = A["ffn_conv_w"].rearrange("o k (m c) -> (o k m) c", c=P)
            bias = A["ffn_conv_b"].rearrange("o (m c) -> (o m) c", c=P)
            act.dma_start(prow[:, 1, :], w[0:P, :]).then_inc(rows_loaded, 16)
            act.dma_start(prow[0:NCONVW - P, 2, :], w[P:NCONVW, :]).then_inc(rows_loaded, 16)
            act.dma_start(prow[NCONVW - P:NROW2, 2, :], bias).then_inc(rows_loaded, 16)
            act.wait_ge(*after("small cleared"))
            act.dma_start(gbias[0:4, 0:1], A["fox_b_f"].rearrange("o h -> h o")).then_inc(small_loaded, 16)
            act.dma_start(gbias[64:68, 0:1], A["gdn_dt_bias"].rearrange("o h -> h o")).then_inc(small_loaded, 16)
            act.dma_start(gbias[64:68, 1:2], A["gdn_a_log"].rearrange("o h -> h o")).then_inc(small_loaded, 16)
            act.dma_start(wgk[96:112, :], A["gla_w_gk"][0]).then_inc(small_loaded, 16)
            return n + 3

        N_ROWS = sum(2 if A[n].shape[-1] == DH else 1 for n in _ROWS) + 3

        def pool_init(pool):
            g.memset(prow[:, :, :], 0.0).then_inc(*step("pool", "rows cleared"))
            g.memset(gbias[:, :], 0.0)
            g.memset(wgk[:, :], 0.0).then_inc(*step("pool", "small cleared"))
            g.memset(ssq[:, :], 0.0).then_inc(*step("pool", "norm1 sum cleared"))
            for n, s in enumerate((tile_free[0], tile_free[1], residual, summed, prod_done)):
                g.memset(stat[:, n % 4, n // 4:n // 4 + 1], 0.0).then_inc(s, 1 if n < 2 else 2)
            g.memset(scanmask, 1.0).then_inc(*step("pool", "scanmask ones"))
            pool.wait_ge(*after("scanmask ones"))
            g.memset(scanmask[64:68].rearrange("p (n c) -> p n c", c=GC)[:, :, 0:1], 0.0).then_inc(
                *step("pool", "scanmask"))
            pool.wait_ge(*after("scanmask"))
            g.memset(lastone[:, :], 0.0).then_inc(*step("pool", "lastone zeros"))
            pool.wait_ge(*after("lastone zeros"))
            g.memset(lastone[:, :].rearrange("p (n c) -> p n c", c=LC)[:, :, LC - 1:LC], 1.0)
            g.memset(mx[:, 33, :], 0.0)
            g.memset(vnew[:, :, :], 0.0)
            g.memset(state[:, :, :], 0.0).then_inc(*step("pool", "mixers cleared"))

        def pe_load(pe):
            pe.wait_ge(cst_loaded, 16)
            pe.wait_ge(x_loaded, 16 * TT)
            for k in range(KT):
                out = pe_ring(pe, f"x{k}")
                for t in range(TT):
                    last = t_.transpose(out[:, t * P:(t + 1) * P], xtok[:, t, k * P:(k + 1) * P], C("ident"))
                last.then_inc(*step("pe", f"x{k} full"))
            pe.wait_ge(rows_loaded, 16 * N_ROWS)
            out = pe_ring(pe, "params")
            at = 0
            for n, rows in enumerate((NROW0, NROW1, NROW2)):
                last = t_.transpose(out[:, at:at + rows], prow[0:rows, n, :], C("ident")[0:rows, 0:rows])
                at += rows
            last.then_inc(*step("pe", "params full"))
            pe_sum(pe, "norm1", 0)

        def act_load(act):
            for k in range(KT):
                act.wait_ge(*after(f"x{k} taken"))
                act.wait_ge(summed, k + 1)
                a.activation(sq[:, k % 2, :], xT[:, k, :], ACT.Square).then_inc(squared, 1)
            split_hi(act, 0)
            act_rstd(act, "norm1", D, rs[:, :])
            act_hi(act, "norm1", KT, xhi)

        def dve_load(dve):
            dve.wait_ge(*after("norm1 sum cleared"))
            def add(k):
                dve.wait_ge(squared, k + 1)
                dve.wait_ge(summed, k + 2)
                v.tensor_tensor(ssq[:, :], ssq[:, :], sq[:, k % 2, :], ALU.add).then_inc(summed, 1)
            for k in range(KT):
                v.tensor_copy(xT[:, k, :], full(dve, f"x{k}")).then_inc(*step("dve", f"x{k} taken"))
                if k:
                    add(k - 1)
            add(KT - 1)
            v.tensor_copy(pcol[:, :], full(dve, "params")[:, 0:NPCOL]).then_inc(*step("dve", "params taken"))
            split_lo(dve, 0)
            dve.wait_ge(*after("params taken"))
            dve_scale(dve, "norm1", KT, xT, "norm1_g", xhi, xlo, "norm1 rstd", rs[:, :])

        def pe_in(pe, u):
            if u >= 2:
                pe.wait_ge(*after(f"in{u - 2} taken"))
            product(pe, u, u, ready="norm1" if u == 0 else None)

        def act_copy_in(act, u, dst, scale=1.0):
            act.wait_ge(unit_used, u + 1)
            a.activation(dst, acc(u), ACT.Copy, scale=scale).then_inc(*step("act", f"in{u} taken"))

        silu_n = {"act": 0, "dve": 0}

        def act_silu(act, name, x, ready):
            n = silu_n["act"]
            silu_n["act"] += 1
            act.wait_ge(*after(ready))
            if n >= 2:
                act.wait_ge(*after(f"silu{n - 2} used"))
            a.activation(xg[:, n % 2, :], x, ACT.Exp, scale=-1.0).then_inc(*step("act", f"{name} exp"))

        def dve_silu(dve, name, x, scale=1.0):
            n = silu_n["dve"]
            silu_n["dve"] += 1
            e = xg[:, n % 2, :]
            dve.wait_ge(*after(f"{name} exp"))
            v.tensor_scalar(e, e, 1.0, None, ALU.add).then_inc(*step("dve", f"{name} exp+1"))
            dve.wait_ge(*after(f"{name} exp+1"))
            v.reciprocal(e, e).then_inc(*step("dve", f"{name} sigmoid"))
            dve.wait_ge(*after(f"{name} sigmoid"))
            v.scalar_tensor_tensor(x, x, scale, e, ALU.mult, ALU.mult).then_inc(*step("dve", f"silu{n} used"))

        def act_head_norm(act, name, src, ready, scale, n=0):
            for i, x in enumerate(src):
                act.wait_ge(*after(ready[i]))
                if i >= 2:
                    act.wait_ge(*after(f"{name} sum{i - 2} full"))
                a.activation(sq[:, i % 2, :], x, ACT.Square).then_inc(*step("act", f"{name} square{i}"))
                if i:
                    act_head_rs(act, name, i - 1, scale)
            act_head_rs(act, name, len(src) - 1, scale)

        def act_head_rs(act, name, i, scale):
            key = f"{name} sum{i}"
            if i >= 2:
                act.wait_ge(*after(f"{name} {i - 2}"))
            r = hr[i % 2]
            a.activation(r, full(act, key), ACT.Ln, scale=scale, bias=C("eps")).then_inc(*step("act", f"{key} taken"))
            act.wait_ge(*after(f"{key} taken"))
            a.activation(r, r, ACT.Exp, scale=-0.5).then_inc(*step("act", f"{name} rs{i}"))

        def pe_head_norm(pe, name, n):
            for i in range(n):
                out = pe_ring(pe, f"{name} sum{i}")
                pe.wait_ge(*after(f"{name} square{i}"))
                t_.matmul(out, C("hsum"), sq[:, i % 2, :], start=True, stop=True).then_inc(
                    *step("pe", f"{name} sum{i} full"))

        def dve_head_norm(dve, name, src, gain):
            for i, x in enumerate(src):
                dve.wait_ge(*after(f"{name} rs{i}"))
                v.scalar_tensor_tensor(x, x, gain[i], hr[i % 2], ALU.mult,
                                       ALU.mult).then_inc(*step("dve", f"{name} {i}"))

        def pe_transpose(pe, key, x, ready):
            out = pe_ring(pe, key)
            if ready:
                pe.wait_ge(*after(ready))
            for t in range(TT):
                last = t_.transpose(out[:, t * P:(t + 1) * P], x[:, t * P:(t + 1) * P], C("ident"))
            last.then_inc(*step("pe", f"{key} full"))

        LS, LG = mx[:, 32, :], mx[:, 34, :]
        D1 = mx[:, 33, :]

        def dve_gate_in(dve):
            dve.wait_ge(small_loaded, 16 * N_SMALL)
            dve.wait_ge(unit_used, 1)
            v.tensor_scalar(graw[:, :], acc(0), gbias[:, 0:1], None, ALU.add).then_inc(*step("dve", "in0 taken"))

        def act_gates(act):
            act.wait_ge(*after("in0 taken"))
            a.activation(gbias[64:68, 2:3], gbias[64:68, 1:2], ACT.Exp).then_inc(*step("act", "exp a_log"))
            a.activation(LG, graw[:, :], ACT.Abs).then_inc(*step("act", "gate abs"))
            act.wait_ge(*after("gate abs"))
            a.activation(LG, LG, ACT.Exp, scale=-1.0).then_inc(*step("act", "gate exp"))
            act.wait_ge(*after("gate exp"))
            a.activation(LG, LG, ACT.Ln, bias=1.0).then_inc(*step("act", "gate ln"))
            act.wait_ge(*after("gate scan"))
            a.activation(grow[32:36, :], LS[32:36, :], ACT.Exp).then_inc(*step("act", "beta"))

        def dve_gates(dve):
            dve.wait_ge(*after("gate ln"))
            dve.wait_ge(*after("mixers cleared"))
            v.scalar_tensor_tensor(LS, graw[:, :], 0.0, LG, ALU.min, ALU.subtract).then_inc(*step("dve", "log sigmoid"))
            dve.wait_ge(*after("log sigmoid"))
            v.tensor_scalar(D1[0:4], LS[0:4], -1.0, None, ALU.mult)
            v.tensor_tensor(D1[64:68], LS[64:68], graw[64:68, :], ALU.subtract).then_inc(*step("dve", "-softplus"))
            dve.wait_ge(*after("-softplus"))
            v.tensor_scalar(D1[64:68], D1[64:68], gbias[64:68, 2:3], None, ALU.mult).then_inc(*step("dve", "decay"))
            dve.wait_ge(*after("decay"))
            v.tensor_tensor_scan(grow[:, :], scanmask, D1, 0.0, ALU.mult, ALU.add).then_inc(*step("dve", "gate scan"))
            dve.wait_ge(*after("gate scan"))
            G3 = grow[64:68, :].rearrange("p (n c) -> p n c", c=GC)
            v.tensor_tensor(grow[96:100, :].rearrange("p (n c) -> p n c", c=GC),
                            G3[:, :, GC - 1:GC].to_broadcast([4, T // GC, GC]), G3,
                            ALU.subtract).then_inc(*step("dve", "to chunk end"))

        def pe_gates(pe):
            pe.wait_ge(*after("beta"))
            pe_transpose(pe, "gcol", grow[:, :], "to chunk end")

        def dve_gcol(dve):
            v.tensor_copy(gcol[:, :, :].rearrange("p t c -> p (t c)"),
                          full(dve, "gcol")).then_inc(*step("dve", "gcol taken"))

        def act_ecol(act):
            act.wait_ge(*after("gcol taken"))
            a.activation(ecol[:, :, :], gcol[:, :, 64:100], ACT.Exp).then_inc(*step("act", "ecol"))

        def act_gdn_tap(act, i):
            act.wait_ge(unit_used, i + 2)
            if i == 0:
                act.wait_ge(*after("x7 taken"))
                act.wait_ge(*after("params taken"))
            a.activation(mx[:, i, :], acc(i + 1), ACT.Identity,
                         scale=par("gdn_conv_w", 18 + i)).then_inc(*step("act", f"gdn tap{i}"))

        def dve_gdn_conv(dve, i):
            y = mx[:, i, :]
            dve.wait_ge(*after(f"gdn tap{i}"))
            for back in (1, 2, 3):
                name = f"in{i + 1} taken" if back == 3 else f"gdn tap{i} {back}"
                v.scalar_tensor_tensor(y[:, back:T], acc(i + 1)[:, 0:T - back], par("gdn_conv_w", 6 * (3 - back) + i),
                                       y[:, back:T], ALU.mult, ALU.add).then_inc(*step("dve", name))
                if back < 3:
                    dve.wait_ge(*after(name))

        GDN_QK = [mx[:, i, :] for i in range(4)]

        def pe_gdn_setup(pe):
            pe_head_norm(pe, "gdn qk", 4)
            for p in range(2):
                out = pe_ring(pe, f"beta{p}")
                t_.matmul(out, C(f"beta{p}"), grow[:, :], start=True, stop=True).then_inc(
                    *step("pe", f"beta{p} full"))
            for h in range(4):
                out = pe_ring(pe, f"gdn G{h}")
                t_.matmul(out, C(f"gdnrow{h}"), grow[:, :], start=True, stop=True).then_inc(
                    *step("pe", f"gdn G{h} full"))

        def pool_gdn(pool):
            for h in range(4):
                pool.wait_ge(*after(f"gdn qk {2 + h // 2}"))
                g.tensor_scalar(mx[:, KZ + h, :], mx[:, K + h // 2, :], C("hmask")[:, h % 2:h % 2 + 1], None,
                                ALU.mult).then_inc(*step("pool", f"gdn kz{h}"))

        def act_gdn_setup(act):
            act_head_norm(act, "gdn qk", GDN_QK, [f"silu{i} used" for i in range(4)], 1.0)
            for h in range(4):
                act.wait_ge(*after(f"gdn G{h} taken"))
                a.activation(mx[:, Y + h, :], mx[:, Y + h, :], ACT.Exp).then_inc(*step("act", f"gdn decay{h}"))

        def dve_gdn_setup(dve):
            gains = [0.125, 0.125, 1.0, 1.0]
            dve_head_norm(dve, "gdn qk", GDN_QK, gains)
            for p in range(2):
                dve.wait_ge(*after(f"gdn qk {2 + p}"))
                v.tensor_tensor(mx[:, KB + p, :], mx[:, K + p, :], full(dve, f"beta{p}"),
                                ALU.mult).then_inc(*step("dve", f"beta{p} taken"))
            for h in range(4):
                bank = full(dve, f"gdn G{h}")
                if h == 0:
                    dve.wait_ge(*after("gcol taken"))
                    dve.wait_ge(*after("beta"))
                for t in range(TT):
                    blk = slice(t * P, (t + 1) * P)
                    last = t == TT - 1
                    v.tensor_scalar(mx[:, Y + h, blk], bank[:, blk], gcol[:, t, 64 + h:65 + h], 0.0, ALU.subtract,
                                    ALU.min).then_inc(*step("dve", f"gdn G{h} taken" if last else f"gdn exponent{h} {t}"))
            for h in range(4):
                e = mx[:, Y + h, :].rearrange("p (t r) -> p t r", r=P)
                dve.wait_ge(*after(f"gdn decay{h}"))
                v.tensor_tensor(e, e, C("incl").unsqueeze(1).to_broadcast([P, TT, P]),
                                ALU.mult).then_inc(*step("dve", f"gdn masked{h}"))

        def blocks(tile):
            return mx[:, tile, :].rearrange("p (t r) -> p t r", r=P)

        def pe_block_products(pe, key, lhs, rhs):
            out = pe_ring(pe, key)
            for t in range(TT):
                blk = slice(t * P, (t + 1) * P)
                last = t_.matmul(out[:, blk], lhs[:, blk], rhs[:, blk], start=True, stop=True)
            last.then_inc(*step("pe", f"{key} full"))

        def pe_gdn_triangles(pe):
            for h in range(4):
                pe.wait_ge(*after(f"gdn kz{h}"))
                pe.wait_ge(*after(f"beta{h // 2} taken"))
                pe_block_products(pe, f"gdn M{h}", mx[:, KZ + h, :], mx[:, KB + h // 2, :])
                pe_block_products(pe, f"gdn A{h}", mx[:, KZ + h, :], mx[:, Q + h // 2, :])

        def dve_gdn_triangles(dve):
            for h in range(4):
                dve.wait_ge(*after(f"gdn masked{h}"))
                v.tensor_tensor(mx[:, MTt + h, :], full(dve, f"gdn M{h}"), mx[:, Y + h, :],
                                ALU.mult).then_inc(*step("dve", f"gdn M{h} taken"))
                v.tensor_tensor(mx[:, AT + h, :], full(dve, f"gdn A{h}"), mx[:, Y + h, :],
                                ALU.mult).then_inc(*step("dve", f"gdn A{h} taken"))

        def bmask(b):
            return C(f"lev{b}").unsqueeze(1).to_broadcast([P, TT, P])

        def pool_gdn_level(pool, b, h):
            if b == 2:
                pool.wait_ge(*after(f"gdn A{h} taken"))
            else:
                pool.wait_ge(*after(f"gdn Y{b // 2} {h} full"))
            g.tensor_tensor(blocks(Y + h), blocks(MTt + h), bmask(b), ALU.mult).then_inc(
                *step("pool", f"gdn O{b} {h}"))

        def dve_gdn_first(dve, h):
            dve.wait_ge(*after(f"gdn M{h} taken"))
            v.tensor_tensor(blocks(XT_ + h), blocks(MTt + h), bmask(1), ALU.mult).then_inc(*step("dve", f"gdn O1 {h}"))
            dve.wait_ge(*after(f"gdn O1 {h}"))
            v.tensor_tensor(blocks(XT_ + h), C("ident").unsqueeze(1).to_broadcast([P, TT, P]), blocks(XT_ + h),
                            ALU.subtract).then_inc(*step("dve", f"gdn XT1 {h}"))

        def pe_gdn_inverse(pe):
            for h in range(4):
                pe_transpose(pe, f"gdn X1 {h}", mx[:, XT_ + h, :], f"gdn XT1 {h}")
            for b in _LEVELS[1:]:
                for h in range(4):
                    pe.wait_ge(*after(f"gdn O{b} {h}"))
                    pe.wait_ge(*after(f"gdn X1 {h} taken" if b == 2 else f"gdn XOX{b // 2} {h} taken"))
                    pe_block_products(pe, f"gdn Y{b} {h}", mx[:, Y + h, :], mx[:, X_ + h, :])
                for h in range(4):
                    pe.wait_ge(*after(f"gdn Y{b} {h} taken"))
                    if b > 2:
                        pe.wait_ge(*after(f"gdn XOXT{b // 2} {h} taken"))
                    if b < 32:
                        pe_block_products(pe, f"gdn XOX{b} {h}", mx[:, XT_ + h, :], mx[:, OX + h, :])
                    pe_block_products(pe, f"gdn XOXT{b} {h}", mx[:, OX + h, :], mx[:, XT_ + h, :])

        OX = KZ

        def act_gdn_inverse(act):
            for h in range(4):
                a.activation(mx[:, X_ + h, :], full(act, f"gdn X1 {h}"), ACT.Copy).then_inc(
                    *step("act", f"gdn X1 {h} taken"))
            for b in _LEVELS[1:]:
                for h in range(4):
                    if b == 2:
                        act.wait_ge(*after(f"gdn A{h} full"))
                    else:
                        act.wait_ge(*after(f"gdn XOXT{b // 2} {h} full"))
                    a.activation(mx[:, OX + h, :], full(act, f"gdn Y{b} {h}"), ACT.Copy).then_inc(
                        *step("act", f"gdn Y{b} {h} taken"))

        def dve_gdn_inverse(dve):
            for b in _LEVELS[1:]:
                for h in range(4):
                    dve.wait_ge(*after(f"gdn XOXT{b} {h} full"))
                    if b < 32:
                        v.tensor_tensor(mx[:, X_ + h, :], mx[:, X_ + h, :], full(dve, f"gdn XOX{b} {h}"),
                                        ALU.subtract).then_inc(*step("dve", f"gdn XOX{b} {h} taken"))
                    v.tensor_tensor(mx[:, XT_ + h, :], mx[:, XT_ + h, :], full(dve, f"gdn XOXT{b} {h}"),
                                    ALU.subtract).then_inc(*step("dve", f"gdn XOXT{b} {h} taken"))

        def pe_gdn_operands(pe):
            for p in range(2):
                pe_transpose(pe, f"gdn kT{p}", mx[:, K + p, :], f"gdn qk {2 + p}")
            for p in range(2):
                pe_transpose(pe, f"gdn vT{p}", mx[:, V + p, :], f"silu{4 + p} used")
            for p in range(2):
                out = pe_ring(pe, f"gdn Gp{p}")
                t_.matmul(out, C(f"gpair{p}"), grow[:, :], start=True, stop=True).then_inc(
                    *step("pe", f"gdn Gp{p} full"))
            for h in range(4):
                out = pe_ring(pe, f"gdn w{h}")
                pe.wait_ge(*after(f"gdn kbg {h}"))
                pe.wait_ge(*after(f"gdn XOXT32 {h} taken"))
                for t in range(TT):
                    last = t_.matmul(out[:, t * P:(t + 1) * P], kbg[:, t, P * (h // 2):P * (h // 2) + P],
                                     blocks(XT_ + h)[:, t, :], start=True, stop=True)
                last.then_inc(*step("pe", f"gdn w{h} full"))
            for i in range(2):
                out = pe_ring(pe, f"gdn u{i}")
                pe.wait_ge(*after("gdn vT1 taken"))
                for t in (2 * i, 2 * i + 1):
                    for h in range(4):
                        at = (t % 2) * 4 * DH + h * DH
                        last = t_.matmul(out[:, at:at + DH], blocks(XT_ + h)[:, t, :], vb[:, t, h * DH:(h + 1) * DH],
                                         start=True, stop=True)
                last.then_inc(*step("pe", f"gdn u{i} full"))

        def head_cols(buf, p):
            return buf[:, :, P * p:P * (p + 1)].rearrange("p t (h c) -> p t h c", h=2)

        def dve_gdn_operands(dve):
            dve.wait_ge(*after("ecol"))
            dve.wait_ge(*after("gdn XOXT32 3 full"))
            for p in range(2):
                bank = full(dve, f"gdn kT{p}").rearrange("p (t h c) -> p t h c", t=TT, h=2)
                for hh in range(2):
                    h = 2 * p + hh
                    dst = kbg[:, :, h * DH:(h + 1) * DH]
                    v.tensor_tensor(dst, bank[:, :, hh, :], gcol[:, :, 32 + h:33 + h].to_broadcast([P, TT, DH]),
                                    ALU.mult).then_inc(*step("dve", f"gdn kb {h}"))
                    dve.wait_ge(*after(f"gdn kb {h}"))
                    v.tensor_tensor(dst, dst, ecol[:, :, h:h + 1].to_broadcast([P, TT, DH]),
                                    ALU.mult).then_inc(*step("dve", f"gdn kbg {h}"))
            for p in range(2):
                bank = full(dve, f"gdn vT{p}").rearrange("p (t h c) -> p t h c", t=TT, h=2)
                for hh in range(2):
                    h = 2 * p + hh
                    v.tensor_tensor(vb[:, :, h * DH:(h + 1) * DH], bank[:, :, hh, :],
                                    gcol[:, :, 32 + h:33 + h].to_broadcast([P, TT, DH]),
                                    ALU.mult).then_inc(*step("dve", f"gdn vT{p} taken" if hh else f"gdn vb {h}"))
            for p in range(2):
                bank = full(dve, f"gdn kT{p}").rearrange("p (t h c) -> p t h c", t=TT, h=2)
                if p == 0:
                    dve.wait_ge(*after("gdn vT1 full"))
                for hh in range(2):
                    h = 2 * p + hh
                    v.tensor_tensor(kout[:, :, h * DH:(h + 1) * DH], bank[:, :, hh, :],
                                    ecol[:, :, 32 + h:33 + h].to_broadcast([P, TT, DH]),
                                    ALU.mult).then_inc(*step("dve", f"gdn kT{p} taken" if hh else f"gdn ko {h}"))
            for p in range(2):
                dve.wait_ge(*after(f"gdn Gp{p} taken"))
                v.tensor_tensor(mx[:, Q + p, :], mx[:, Q + p, :], mx[:, 8 + p, :],
                                ALU.mult).then_inc(*step("dve", f"gdn q_in{p}"))
            for i in range(2):
                v.tensor_copy(uu[:, 2 * i:2 * i + 2, :].rearrange("p t c -> p (t c)"),
                              full(dve, f"gdn u{i}")).then_inc(*step("dve", f"gdn u{i} taken"))

        def act_gdn_operands(act):
            for p in range(2):
                a.activation(mx[:, 8 + p, :], full(act, f"gdn Gp{p}"), ACT.Exp).then_inc(
                    *step("act", f"gdn Gp{p} taken"))
            for h in range(4):
                rows = slice(64 * (h % 2), 64 * (h % 2) + 64)
                a.activation(wT[rows, h // 2, :], full(act, f"gdn w{h}")[rows, :], ACT.Copy).then_inc(
                    *step("act", f"gdn w{h} taken"))

        def pe_gdn_chunks(pe):
            for c in range(T // GC):
                t, par_ = c // 2, c % 2
                blk = slice(t * P, (t + 1) * P)
                out = pe_ring(pe, f"gdn wS{c}")
                if c == 0:
                    pe.wait_ge(*after("gdn w3 taken"))
                    pe.wait_ge(*after("mixers cleared"))
                    pe.wait_ge(*after("gdn q_in1"))
                else:
                    pe.wait_ge(*after(f"gdn kv{c - 1} taken"))
                for p in range(2):
                    last = t_.matmul(out[:, P * p:P * (p + 1)], wT[:, p, blk], state[:, p, :], start=True, stop=True)
                last.then_inc(*step("pe", f"gdn wS{c} full"))
                outo = pe_ring(pe, f"gdn o{c}")
                outk = pe_ring(pe, f"gdn kv{c}")
                pe.wait_ge(*after(f"gdn wS{c} taken"))
                for p in range(2):
                    last = t_.matmul(outk[:, P * p:P * (p + 1)], kout[:, t, P * p:P * (p + 1)],
                                     vnew[:, par_, P * p:P * (p + 1)], start=True, stop=True)
                last.then_inc(*step("pe", f"gdn kv{c} full"))
                for p in range(2):
                    for hh in range(2):
                        h = 2 * p + hh
                        cols = slice(h * DH, (h + 1) * DH)
                        t_.matmul(outo[:, cols], mx[:, Q + p, blk], state[:, p, hh * DH:(hh + 1) * DH], start=True,
                                  stop=False)
                        last = t_.matmul(outo[:, cols], blocks(AT + h)[:, t, :], vnew[:, par_, cols], start=False,
                                         stop=True)
                last.then_inc(*step("pe", f"gdn o{c} full"))

        def dve_gdn_chunks(dve):
            for c in range(T // GC):
                t, rows = c // 2, slice(64 * (c % 2), 64 * (c % 2) + 64)
                bank = full(dve, f"gdn wS{c}")
                if c == 0:
                    dve.wait_ge(*after("gdn u1 taken"))
                if c >= 2:
                    dve.wait_ge(*after(f"gdn o{c - 2} full"))
                v.tensor_tensor(vnew[rows, c % 2, :], uu[rows, t, :], bank[rows, 0:4 * DH],
                                ALU.subtract).then_inc(*step("dve", f"gdn wS{c} taken"))
                bank = full(dve, f"gdn kv{c}")
                dve.wait_ge(*after(f"gdn o{c} full"))
                for h in range(4):
                    p, r = h // 2, slice(64 * (h % 2), 64 * (h % 2) + 64)
                    end = GC * c + GC - 1
                    st = state[r, p, r]
                    v.scalar_tensor_tensor(st, st, mx[r, 8 + p, end:end + 1], bank[r, P * p + r.start:P * p + r.stop],
                                           ALU.mult, ALU.add).then_inc(
                                               *step("dve", f"gdn kv{c} taken" if h == 3 else f"gdn state{c} {h}"))

        def act_gdn_chunks(act):
            for c in range(T // GC):
                t, rows = c // 2, slice(64 * (c % 2), 64 * (c % 2) + 64)
                a.activation(oo[rows, t, :], full(act, f"gdn o{c}")[rows, 0:4 * DH], ACT.Copy).then_inc(
                    *step("act", f"gdn o{c} taken"))

        GDN_O = [mx[:, K + p, :] for p in range(2)]

        def pe_gdn_out(pe):
            for p in range(2):
                out = pe_ring(pe, f"gdn oT{p}")
                pe.wait_ge(*after("gdn o7 taken"))
                for t in range(TT):
                    last = t_.transpose(out[:, t * P:(t + 1) * P], oo[:, t, P * p:P * (p + 1)], C("ident"))
                last.then_inc(*step("pe", f"gdn oT{p} full"))
            pe_head_norm(pe, "gdn out", 2)

        def act_gdn_out(act):
            for p in range(2):
                a.activation(GDN_O[p], full(act, f"gdn oT{p}"), ACT.Copy).then_inc(*step("act", f"gdn oT{p} taken"))
            act_head_norm(act, "gdn out", GDN_O, [f"gdn oT{p} taken" for p in range(2)], 1.0 / DH)

        def dve_gdn_out(dve):
            dve_head_norm(dve, "gdn out", GDN_O, [par("gdn_on_g")] * 2)
            for p in range(2):
                dve.wait_ge(*after(f"gdn out {p}"))
                v.tensor_tensor(mixT[:, 2 + p, :], mixT[:, 2 + p, :], GDN_O[p], ALU.mult).then_inc(
                    *step("dve", f"mix{2 + p}"))

        A0, PP, SF, AM, KO, KOT, VT, VX, KV, AX_, ST, O_, QI = 0, 1, 2, 3, 14, 15, 16, 18, 20, 24, 28, 32, 34
        TJ, PROD, TMP, QZ = (5, 35), (8, 9), (20, 21), 10

        def chunks(x):
            return x.rearrange("p (n c) -> p n c", c=LC)

        LA = {"gla": dict(q=mx[:, 6, :], k=mx[:, 7, :], a=mx[:, A0, :], v=[mixT[:, 0, :], mixT[:, 1, :]],
                          o=[mx[:, O_, :], mx[:, O_ + 1, :]], red=["gla0", "gla1"], dk=32, mask="qmask")}
        for p in range(2):
            LA[f"hg{p}"] = dict(q=mx[:, 6 + p, :], k=mx[:, 12 + p, :], a=mixT[:, p, :], v=[mx[:, (0, 17)[p], :]],
                                o=[mx[:, O_ + p, :]], red=["hsum"], dk=64, mask="hmask")
        am = wtile(AM, 2)
        KVw, AXw, STw = (wtile(k, 4) for k in (KV, AX_, ST))
        for L in LA.values():
            L["heads"] = [(L["dk"] * h, h // 2, 64 * (h % 2)) for h in range(P // L["dk"])]

        def pool_la(pool, nm, ready):
            L = LA[nm]
            ax = chunks(L["a"])
            for r in ready:
                pool.wait_ge(*after(r))
            g.tensor_copy(am[:, 0:T], L["a"]).then_inc(*step("pool", f"{nm} am copy"))
            g.memset(mx[:, VX, :], 0.0).then_inc(*step("pool", f"{nm} d1 zeros"))
            g.memset(AXw.rearrange("p (d c) -> p d c", c=NL)[:, :, 0:1], 0.0).then_inc(*step("pool", f"{nm} ax zeros"))
            pool.wait_ge(*after(f"{nm} am copy"))
            g.memset(chunks(am[:, 0:T])[:, :, 0:1], 0.0)
            g.memset(am[:, T:T + 1], 0.0)
            pool.wait_ge(*after(f"{nm} d1 zeros"))
            g.tensor_copy(chunks(mx[:, VX, :])[:, :, 0:1], ax[:, :, 0:1]).then_inc(*step("pool", f"{nm} scan inputs"))
            for h in range(len(L["heads"])):
                pool.wait_ge(*after(f"{nm} q_in"))
                g.tensor_scalar(mx[:, QZ + h, :], mx[:, QI, :], C(L["mask"])[:, h:h + 1], None,
                                ALU.mult).then_inc(*step("pool", f"{nm} qz{h}"))
            n = 0
            cm = C("cmask").unsqueeze(2).to_broadcast([P, 8, DH])
            for h, (_, vi, r0) in enumerate(L["heads"]):
                for t in range(TT):
                    pool.wait_ge(*after(f"{nm} v{vi} taken"))
                    if n >= 2:
                        pool.wait_ge(*after(f"{nm} kv{n - 2} full"))
                    src = mx[:, VT + vi, t * P + r0:t * P + r0 + DH].unsqueeze(1).to_broadcast([P, 8, DH])
                    if n == 0:
                        pool.wait_ge(*after(f"{nm} suffix"))
                    g.tensor_tensor(mx[:, VX + n % 2, :].rearrange("p (c d) -> p c d", d=DH), src, cm,
                                    ALU.mult).then_inc(*step("pool", f"{nm} spread{n}"))
                    n += 1
            m = 0
            for j in range(1, LC):
                def t_next(j):
                    prev = chunks(L["q"] if j == 1 else mx[:, TJ[(j - 1) % 2], :])
                    if j >= 3:
                        pool.wait_ge(*after(f"{nm} prod{j - 2}"))
                    if j >= 2:
                        pool.wait_ge(*after(f"{nm} t{j - 1}"))
                    g.tensor_tensor(chunks(mx[:, TJ[j % 2], :])[:, :, j:LC], prev[:, :, j:LC], ax[:, :, 1:LC + 1 - j],
                                    ALU.mult).then_inc(*step("pool", f"{nm} t{j}"))
                if j == 1:
                    t_next(1)
                if j + 1 < LC:
                    t_next(j + 1)
                for vi in range(len(L["v"])):
                    n = LC - j
                    pool.wait_ge(*after(f"{nm} intra{j} {vi} taken"))
                    if j >= 2:
                        pool.wait_ge(*after(f"{nm} o{j - 1} {vi}"))
                    o3 = chunks(L["o"][vi])[:, :, j:LC]
                    g.tensor_tensor(o3, o3, mx[:, TMP[m % 2], 0:NL * n].rearrange("p (n c) -> p n c", c=n),
                                    ALU.add).then_inc(*step("pool", f"{nm} o{j} {vi}"))
                    m += 1

        def act_la(act, nm):
            L = LA[nm]
            act.wait_ge(*after(f"{nm} prefix"))
            act.wait_ge(*after(f"{nm} ax zeros"))
            A3 = AXw.rearrange("p (d c) -> p d c", c=NL)
            a.activation(A3[:, :, 1:NL], chunks(mx[:, PP, :])[:, 1:NL, LC - 1].unsqueeze(1).to_broadcast([P, DH, NL - 1]),
                         ACT.Copy).then_inc(*step("act", f"{nm} chunk decays"))
            for vi in range(len(L["v"])):
                a.activation(mx[:, VT + vi, :], full(act, f"{nm} v{vi}"), ACT.Copy).then_inc(
                    *step("act", f"{nm} v{vi} taken"))
            a.activation(mx[:, KOT, :], full(act, f"{nm} ko"), ACT.Copy).then_inc(*step("act", f"{nm} ko taken"))
            n = 0
            for h, (row, vi, r0) in enumerate(L["heads"]):
                rows = slice(row, row + L["dk"])
                dst = KVw.rearrange("p (d c) -> p c d", c=NL)
                for t in range(TT):
                    bank = full(act, f"{nm} kv{n}").rearrange("p (c d) -> p c d", d=DH)
                    a.activation(dst[rows, 8 * t:8 * t + 8, :], bank[rows, :, :], ACT.Copy).then_inc(
                        *step("act", f"{nm} kv{n} taken"))
                    n += 1

        def pe_la(pe, nm, vready):
            L = LA[nm]
            for vi, x in enumerate(L["v"]):
                pe_transpose(pe, f"{nm} v{vi}", x, vready[vi])
            pe_transpose(pe, f"{nm} ko", mx[:, KO, :], f"{nm} k_out")
            n = 0
            for h in range(len(L["heads"])):
                for t in range(TT):
                    out = pe_ring(pe, f"{nm} kv{n}")
                    pe.wait_ge(*after(f"{nm} spread{n}"))
                    pe.wait_ge(*after(f"{nm} ko taken"))
                    t_.matmul(out, mx[:, KOT, t * P:(t + 1) * P], mx[:, VX + n % 2, :], start=True,
                              stop=True).then_inc(*step("pe", f"{nm} kv{n} full"))
                    n += 1
            for j in range(LC):
                pe.wait_ge(*after(f"{nm} prod{j}"))
                n = NL * (LC - j)
                for vi, red in enumerate(L["red"]):
                    out = pe_ring(pe, f"{nm} intra{j} {vi}")
                    t_.matmul(out[:, 0:n], C(red), mx[:, PROD[j % 2], 0:n], start=True,
                              stop=True).then_inc(*step("pe", f"{nm} intra{j} {vi} full"))
            S3 = STw.rearrange("p (d c) -> p d c", c=NL)
            outs = [pe_ring(pe, f"{nm} inter{vi}") for vi in range(len(L["v"]))]
            pe.wait_ge(*after(f"{nm} states"))
            for h, (_, vi, r0) in enumerate(L["heads"]):
                pe.wait_ge(*after(f"{nm} qz{h}"))
                for c in range(1, NL):
                    cols = slice(LC * c, LC * c + LC)
                    last = t_.matmul(outs[vi][r0:r0 + DH, cols], S3[:, :, c - 1], mx[:, QZ + h, cols], start=True, stop=True)
                if h % 2:
                    last.then_inc(*step("pe", f"{nm} inter{vi} full"))

        def dve_la(dve, nm):
            L = LA[nm]
            n_heads = len(L["heads"])
            dve.wait_ge(*after(f"{nm} scan inputs"))
            v.tensor_tensor_scan(mx[:, PP, :], am[:, 0:T], mx[:, VX, :], 0.0, ALU.mult,
                                 ALU.add).then_inc(*step("dve", f"{nm} prefix"))
            v.tensor_tensor_scan(mx[:, SF, ::-1], am[:, 1:T + 1][:, ::-1], lastone[:, ::-1], 0.0, ALU.mult,
                                 ALU.add).then_inc(*step("dve", f"{nm} suffix"))
            dve.wait_ge(*after(f"{nm} prefix"))
            v.tensor_tensor(mx[:, QI, :], L["q"], mx[:, PP, :], ALU.mult).then_inc(*step("dve", f"{nm} q_in"))
            dve.wait_ge(*after(f"{nm} suffix"))
            v.tensor_tensor(mx[:, KO, :], L["k"], mx[:, SF, :], ALU.mult).then_inc(*step("dve", f"{nm} k_out"))
            dve.wait_ge(*after(f"{nm} chunk decays"))
            dve.wait_ge(*after(f"{nm} kv{4 * n_heads - 1} taken"))
            v.tensor_tensor_scan(STw, AXw, KVw, 0.0, ALU.mult, ALU.add).then_inc(*step("dve", f"{nm} states"))
            dve.wait_ge(*after(f"{nm} states"))
            m = 0
            for j in range(LC + 1):
                if j < LC:
                    n = LC - j
                    if j:
                        dve.wait_ge(*after(f"{nm} t{j}"))
                    if j >= 2:
                        dve.wait_ge(*after(f"{nm} intra{j - 2} {len(L['v']) - 1} full"))
                    tj = chunks(L["q"] if j == 0 else mx[:, TJ[j % 2], :])
                    v.tensor_tensor(mx[:, PROD[j % 2], 0:NL * n].rearrange("p (n c) -> p n c", c=n), tj[:, :, j:LC],
                                    chunks(L["k"])[:, :, 0:n], ALU.mult).then_inc(*step("dve", f"{nm} prod{j}"))
                if j:
                    jj, n = j - 1, LC - j + 1
                    for vi in range(len(L["v"])):
                        bank = full(dve, f"{nm} intra{jj} {vi}")[:, 0:NL * n].rearrange("p (n c) -> p n c", c=n)
                        if jj == 0:
                            dst = chunks(L["o"][vi])
                        else:
                            if m >= 2:
                                jb, vb_ = divmod(m - 2, len(L["v"]))
                                dve.wait_ge(*after(f"{nm} o{jb + 1} {vb_}"))
                            dst = mx[:, TMP[m % 2], 0:NL * n].rearrange("p (n c) -> p n c", c=n)
                            m += 1
                        v.tensor_tensor(dst, bank, chunks(L["v"][vi])[:, :, 0:n],
                                        ALU.mult).then_inc(*step("dve", f"{nm} intra{jj} {vi} taken"))
            for vi in range(len(L["v"])):
                dve.wait_ge(*after(f"{nm} o{LC - 1} {vi}"))
                o = L["o"][vi]
                v.tensor_tensor(o[:, LC:T], o[:, LC:T], full(dve, f"{nm} inter{vi}")[:, LC:T],
                                ALU.add).then_inc(*step("dve", f"{nm} inter{vi} taken"))

        def act_la_out(act, nm, outs):
            act_head_norm(act, f"{nm} out", [o for o, _, _ in outs], [r for _, r, _ in outs], 1.0 / DH)

        def dve_la_out(dve, nm, gain, outs):
            dve_head_norm(dve, f"{nm} out", [o for o, _, _ in outs], [par(gain)] * len(outs))
            for i, (o, _, m) in enumerate(outs):
                dve.wait_ge(*after(f"{nm} out {i}"))
                v.tensor_tensor(mixT[:, m, :], mixT[:, m, :], o, ALU.mult).then_inc(*step("dve", f"mix{m}"))

        GLA_OUT = [(mx[:, O_ + i, :], f"gla inter{i} taken", 6 + i) for i in range(2)]
        HG_OUT = [(mx[:, O_ + i, :], f"hg{i} inter0 taken", 4 + i) for i in range(2)]

        def pe_gla_gate(pe):
            out = pe_ring(pe, "gla gate")
            pe.wait_ge(small_loaded, 16 * N_SMALL)
            pe.wait_ge(*after("in0 taken"))
            t_.matmul(out, wgk[:, :], graw[:, :], start=True, stop=True).then_inc(*step("pe", "gla gate full"))

        def act_gla_gate(act):
            z, e = mx[:, 1, :], mx[:, 2, :]
            act.wait_ge(*after("gdn o7 full"))
            a.activation(z, full(act, "gla gate"), ACT.Identity, bias=par("gla_b_gk")).then_inc(
                *step("act", "gla gate taken"))
            act.wait_ge(*after("gla gate taken"))
            act.wait_ge(*after("mix3"))
            a.activation(e, z, ACT.Abs).then_inc(*step("act", "gla abs"))
            act.wait_ge(*after("gla abs"))
            a.activation(e, e, ACT.Exp, scale=-1.0).then_inc(*step("act", "gla exp"))
            act.wait_ge(*after("gla exp"))
            a.activation(e, e, ACT.Ln, bias=1.0).then_inc(*step("act", "gla ln"))
            act.wait_ge(*after("gla log sigmoid"))
            a.activation(mx[:, A0, :], z, ACT.Exp, scale=1.0 / 16).then_inc(*step("act", "gla decay"))

        def dve_gla_gate(dve):
            dve.wait_ge(*after("gla ln"))
            v.scalar_tensor_tensor(mx[:, 1, :], mx[:, 1, :], 0.0, mx[:, 2, :], ALU.min,
                                   ALU.subtract).then_inc(*step("dve", "gla log sigmoid"))

        def act_hg_gate(act, p):
            act.wait_ge(unit_used, 18 + p)
            a.activation(mixT[:, p, :], acc(17 + p), ACT.Exp, scale=-1.0).then_inc(*step("act", f"hg exp(-f) {p}"))
            a.activation(mx[:, 12 + p, :], acc(17 + p), ACT.Exp).then_inc(*step("act", f"in{17 + p} taken"))

        def dve_hg_gate(dve, p):
            dve.wait_ge(*after(f"in{17 + p} taken"))
            for x, n in ((mixT[:, p, :], "a"), (mx[:, 12 + p, :], "k")):
                v.tensor_scalar(x, x, 1.0, None, ALU.add).then_inc(*step("dve", f"hg {n}{p} +1"))
                dve.wait_ge(*after(f"hg {n}{p} +1"))
                v.reciprocal(x, x).then_inc(*step("dve", f"hg {n}{p}"))

        PB = {}

        def attn_pe(pe, tag, heads, logits, values, PT, ready):
            n_all = heads * TT
            for n in range(n_all + 1):
                if n < n_all:
                    h, i = divmod(n, TT)
                    out = pe_ring(pe, f"{tag} L{n}")
                    if i == 0:
                        ready(pe, h)
                    logits(out[:, 0:P * (i + 1)], h, i).then_inc(*step("pe", f"{tag} L{n} full"))
                if n:
                    h, i = divmod(n - 1, TT)
                    out = pe_ring(pe, f"{tag} T{n - 1}")
                    pe.wait_ge(*after(f"{tag} P{n - 1}"))
                    for k in range(i + 1):
                        last = t_.transpose(out[:, k * P:(k + 1) * P], PB[tag][:, (n - 1) % 2, k * P:(k + 1) * P],
                                            C("ident"))
                    last.then_inc(*step("pe", f"{tag} T{n - 1} full"))
                    if i == TT - 1:
                        out = pe_ring(pe, f"{tag} O{h}")
                        pe.wait_ge(*after(f"{tag} T{n - 1} taken"))
                        for k in range(TT):
                            last = t_.matmul(out[:, k * P:T], values(k, h), PT[:, h % 2, k, k * P:T], start=k == 0,
                                             stop=k == TT - 1)
                        last.then_inc(*step("pe", f"{tag} O{h} full"))

        def attn_act(act, tag, heads, PT, each=None):
            n_all = heads * TT
            for n in range(n_all + 1):
                if n < n_all:
                    i = n % TT
                    W = P * (i + 1)
                    act.wait_ge(*after(f"{tag} max{n}"))
                    if n >= 2:
                        act.wait_ge(*after(f"{tag} T{n - 2} full"))
                    a.activation(PB[tag][:, n % 2, 0:W], full(act, f"{tag} L{n}")[:, 0:W], ACT.Exp,
                                 bias=stat[:, n % 4, 0:1],
                                 accum_out=stat[:, n % 4, 1:2]).then_inc(*step("act", f"{tag} L{n} taken"))
                if n:
                    h, i = divmod(n - 1, TT)
                    W = P * (i + 1)
                    bank = full(act, f"{tag} T{n - 1}")
                    if h >= 2 and i == 0:
                        act.wait_ge(*after(f"{tag} O{h - 2} full"))
                    a.activation(PT[:, h % 2, 0:i + 1, i * P:(i + 1) * P],
                                 bank[:, 0:W].rearrange("p (k q) -> p k q", q=P),
                                 ACT.Copy).then_inc(*step("act", f"{tag} T{n - 1} taken"))
                    if each and i == 0 and h:
                        each(h - 1)
            if each:
                each(heads - 1)

        def attn_dve(dve, tag, heads, each):
            n_all = heads * TT
            for n in range(n_all + 1):
                if n < n_all:
                    i = n % TT
                    bank = full(dve, f"{tag} L{n}")
                    diag = bank[:, i * P:(i + 1) * P]
                    v.tensor_tensor(diag, diag, C("neg"), ALU.add).then_inc(*step("dve", f"{tag} masked{n}"))
                    dve.wait_ge(*after(f"{tag} masked{n}"))
                    v.tensor_reduce(stat[:, n % 4, 0:1], bank[:, 0:P * (i + 1)], AX.X, ALU.max,
                                    negate=True).then_inc(*step("dve", f"{tag} max{n}"))
                if n:
                    m = n - 1
                    W = P * (m % TT + 1)
                    dve.wait_ge(*after(f"{tag} L{m} taken"))
                    v.reciprocal(stat[:, m % 4, 2:3], stat[:, m % 4, 1:2]).then_inc(*step("dve", f"{tag} 1/sum{m}"))
                    dve.wait_ge(*after(f"{tag} 1/sum{m}"))
                    pm = PB[tag][:, m % 2, 0:W]
                    v.tensor_scalar(pm, pm, stat[:, m % 4, 2:3], None, ALU.mult).then_inc(*step("dve", f"{tag} P{m}"))
                    if m % TT == 0 and m:
                        each(m // TT - 1)
            each(heads - 1)

        FQ, FK, FV, FZ, FVT, FO = 0, 2, 4, 6, 10, 22
        PB["fox"] = mx[:, 12:14, :]
        fox_PT = wtile(14, 8).rearrange("p (b k t) -> p b k t", b=2, t=T)
        FOX_QK = [mx[:, i, :] for i in range(4)]
        FOX_O = [mx[:, FO + p, :] for p in range(2)]

        def pe_fox(pe):
            pe_head_norm(pe, "fox qk", 4)
            for p in range(2):
                pe_transpose(pe, f"fox v{p}", mx[:, FV + p, :], f"in{27 + p} taken")

            def ready(pe, h):
                pe.wait_ge(*after(f"fox kz{h}"))
                pe.wait_ge(*after(f"fox v{h // 2} taken"))

            def logits(out, h, i):
                W = P * (i + 1)
                t_.matmul(out, mx[:, FQ + h // 2, i * P:(i + 1) * P], mx[:, FZ + h, 0:W], start=True, stop=False)
                return t_.matmul(out, C(f"foxrow{h}"), grow[:, 0:W], start=False, stop=True)

            attn_pe(pe, "fox", 4, logits, lambda k, h: mx[:, FVT + h // 2, k * P:(k + 1) * P], fox_PT, ready)
            pe_head_norm(pe, "fox out", 2)

        def act_fox(act):
            act_head_norm(act, "fox qk", FOX_QK, [f"in{23 + i} taken" for i in range(4)], 1.0 / DH)
            for p in range(2):
                a.activation(mx[:, FVT + p, :], full(act, f"fox v{p}"), ACT.Copy).then_inc(
                    *step("act", f"fox v{p} taken"))
            attn_act(act, "fox", 4, fox_PT)
            act_head_norm(act, "fox out", FOX_O, ["fox O1 taken", "fox O3 taken"], 1.0 / DH)

        def dve_fox(dve):
            v.tensor_scalar(gbias[:, 3:4], par("fox_qn_g"), 0.125, None, ALU.mult).then_inc(*step("dve", "fox q gain"))
            dve.wait_ge(*after("fox q gain"))
            dve_head_norm(dve, "fox qk", FOX_QK, [gbias[:, 3:4]] * 2 + [par("fox_kn_g")] * 2)

            def out(h):
                rows = slice(64 * (h % 2), 64 * (h % 2) + 64)
                v.tensor_copy(FOX_O[h // 2][rows, :], full(dve, f"fox O{h}")[rows, :]).then_inc(
                    *step("dve", f"fox O{h} taken"))
            attn_dve(dve, "fox", 4, out)
            for i in range(2):
                dve.wait_ge(*after(f"fox out rs{i}"))
                v.scalar_tensor_tensor(mixT[:, i, :], FOX_O[i], par("fox_on_g"), hr[i], ALU.mult,
                                       ALU.mult).then_inc(*step("dve", f"mix{i}"))

        def pool_fox(pool):
            for h in range(4):
                pool.wait_ge(*after(f"fox qk {2 + h // 2}"))
                g.tensor_scalar(mx[:, FZ + h, :], mx[:, FK + h // 2, :], C("hmask")[:, h % 2:h % 2 + 1], None,
                                ALU.mult).then_inc(*step("pool", f"fox kz{h}"))

        MIX_ORDER = (2, 3, 6, 7, 4, 5, 0, 1)

        def act_mix(act):
            act.wait_ge(unit_used, FIRST["w_out"])
            for m in MIX_ORDER:
                act.wait_ge(*after(f"mix{m}"))
                a.activation(xhi[:, m, :], mixT[:, m, :], ACT.Copy).then_inc(*step("act", f"mix hi{m}"))

        def dve_mix(dve):
            for m in MIX_ORDER:
                dve.wait_ge(*after(f"mix hi{m}"))
                v.tensor_tensor(xlo[:, m, :], mixT[:, m, :], f32(xhi[:, m, :]),
                                ALU.subtract).then_inc(*step("dve", f"mix lo{m}"))

        mixers.close()
        ffn = ctx.enter_context(ExitStack())
        h_hi = sb("h_hi", [P, FT, T], F32R, ffn)
        h_lo = sb("h_lo", [P, FT, T], F32R, ffn)
        yg, yu = (sb(n, [P, 2, T], F32, ffn) for n in ("yg", "yu"))
        ffn.close()
        conv = ctx.enter_context(ExitStack())
        c_hi = sb("c_hi", [P, KT, T], F32R, conv)
        c_lo = sb("c_lo", [P, KT, T], F32R, conv)
        bS, cS, zS, yS = (sb(n, [P, 2, T], F32, conv) for n in ("bS", "cS", "zS", "yS"))
        conv.close()
        mla = ctx.enter_context(ExitStack())
        kn = sb("kn", [P, NH2, T], c=mla)
        qn = sb("qn", [P, NH2, T], c=mla)
        qp = sb("qp", [P, NH2 // 2, T], c=mla)
        kpz = sb("kpz", [P, 2, T], c=mla)
        vtok = sb("vtok", [P, TT, D], c=mla)
        rot = sb("rot", [P, 2, T], c=mla)
        latent = ctx.enter_context(ExitStack())
        lhi, llo = (sb(n, [P, 2, T], F32R, latent) for n in ("lhi", "llo"))
        chi, clo = (sb(n, [P, 3, T], F32R, latent) for n in ("chi", "clo"))
        lat = sb("lat", [P, 3, T], c=latent)
        kraw = sb("kraw", [P, T], c=latent)
        rl = sb("rl", [P, T], c=latent)
        ang = sb("ang", [P, 2, T], c=latent)
        turns = sb("turns", [P, T], I32, latent)
        latent.close()
        attn = ctx.enter_context(ExitStack())
        PB["mla"] = sb("mla_P", [P, 2, T], c=attn)
        mla_PT = sb("mla_PT", [P, 2, TT, T], c=attn)
        attn.close()
        mla.close()
        ffn3 = ctx.enter_context(ExitStack())
        h3_hi = sb("h3_hi", [P, FT, T], F32R, ffn3)
        h3_lo = sb("h3_lo", [P, FT, T], F32R, ffn3)
        yg3 = sb("yg3", [P, 2, T], F32, ffn3)
        ffn3.close()
        fin = sb("fin", [P, KT, T])

        MLA_TILES = [f"dkv{i}" for i in range(3)] + [f"dq{i}" for i in range(3)] + [f"kn{h}" for h in range(NH2)]
        MLA_TILES += [f"v{g}{t}" for g in range(2) for t in range(TT)]
        for _g in range(2):
            MLA_TILES += [f"qn{4 * _g + h}" for h in range(4)] + [f"qp{2 * _g + p}" for p in range(2)]
        tile_no = {n: i for i, n in enumerate(MLA_TILES)}

        def mla_acc(name):
            return acc(tile_no[name])

        def pe_mla_wait(pe, name):
            if tile_no[name] >= 2:
                pe.wait_ge(*after(f"{MLA_TILES[tile_no[name] - 2]} taken"))

        def pe_latent_sum(pe, name, n):
            out = pe_ring(pe, f"{name} sum")
            for k in range(n):
                pe.wait_ge(*after(f"{name} square{k}"))
                t_.matmul(out, C("ones"), sq[:, k % 2, :], start=k == 0, stop=k == n - 1).then_inc(
                    *step("pe", f"{name} sum full" if k == n - 1 else f"{name} add{k}"))

        def act_latent(act, name, n, hi):
            for k in range(n):
                if k >= 2:
                    act.wait_ge(*after(f"{name} add{k - 2}"))
                act.wait_ge(*after(f"{('dkv', 'dq')[name == 'cq']}{k} taken"))
                a.activation(sq[:, k % 2, :], lat[:, k, :], ACT.Square).then_inc(*step("act", f"{name} square{k}"))
            act_rstd(act, name, n * P, rl[:, :])
            act_hi(act, name, n, hi)

        def pe_mla(pe):
            u = FIRST["dkv"]
            for i in range(3):
                pe_mla_wait(pe, f"dkv{i}")
                product(pe, u + i, tile_no[f"dkv{i}"], ready="kv norm" if i == 0 else None)
            pe_latent_sum(pe, "lat", 2)
            u = FIRST["dq"]
            for i in range(3):
                pe_mla_wait(pe, f"dq{i}")
                product(pe, u + i, tile_no[f"dq{i}"], ready="q norm" if i == 0 else None)
            out = pe_ring(pe, "k swapped")
            pe.wait_ge(*after("dkv2 taken"))
            t_.matmul(out, C("perm"), kraw[:, :], start=True, stop=True).then_inc(*step("pe", "k swapped full"))
            u = FIRST["ukv"]
            for h in range(NH2):
                pe_mla_wait(pe, f"kn{h}")
                product(pe, u + h // 4, tile_no[f"kn{h}"], x=(lhi, llo), ready="lat" if h == 0 else None,
                        cols=P * (h % 4), full=f"kn{h} full" if h % 4 < 3 else None)
            for gr in range(2):
                pe.wait_ge(lo_split, u + 2 + gr + 1)
                wh, wl = (unit_view(b, u + 2 + gr) for b in (whi, wlo))
                for t in range(TT):
                    pe_mla_wait(pe, f"v{gr}{t}")
                    blk = slice(t * P, (t + 1) * P)
                    for k in range(2):
                        last = passes(mla_acc(f"v{gr}{t}"), lhi[:, k, blk], llo[:, k, blk], wh[:, k, :], wl[:, k, :],
                                      k == 0, k == 1)
                    last.then_inc(*(step("pe", f"v{gr}{t} full") if t < TT - 1 else (unit_used, 1)))
            pe_latent_sum(pe, "cq", 3)
            u = FIRST["uq"]
            for gr in range(2):
                for p in range(2):
                    for hh in range(2):
                        name = f"qn{4 * gr + 2 * p + hh}"
                        pe_mla_wait(pe, name)
                        product(pe, u + 3 * gr + p, tile_no[name], x=(chi, clo), ready="cq" if name == "qn0" else None,
                                cols=P * hh, full=f"{name} full" if hh == 0 else None)
                for p in range(2):
                    name = f"qp{2 * gr + p}"
                    pe_mla_wait(pe, name)
                    product(pe, u + 3 * gr + 2, tile_no[name], x=(chi, clo), cols=P * p, full=f"{name} full" if p == 0 else None)
                for p in range(2):
                    i = 2 * gr + p
                    out = pe_ring(pe, f"q swapped{i}")
                    pe.wait_ge(*after(f"qp{i} taken"))
                    t_.matmul(out, C("perm"), qp[:, i, :], start=True, stop=True).then_inc(
                        *step("pe", f"q swapped{i} full"))

            def ready(pe, h):
                if h == 0:
                    pe.wait_ge(*after("kpz1"))
                    pe.wait_ge(*after("kpz0"))
                    pe.wait_ge(*after(f"kn{NH2 - 1} taken"))
                    pe.wait_ge(*after("v13 taken"))
                pe.wait_ge(*after(f"qn{h} taken"))
                pe.wait_ge(*after(f"rotated{h // 2}"))

            def logits(out, h, i):
                blk = slice(i * P, (i + 1) * P)
                W = P * (i + 1)
                t_.matmul(out, qn[:, h, blk], kn[:, h, 0:W], start=True, stop=False)
                return t_.matmul(out, qp[:, h // 2, blk], kpz[:, h % 2, 0:W], start=False, stop=True)

            attn_pe(pe, "mla", NH2, logits, lambda k, h: vtok[:, k, h * P:(h + 1) * P], mla_PT, ready)

        QSCALE = float((128 + 64) ** -0.5)

        def act_mla(act):
            act_rstd(act, "mla norm", D, rs[:, :])
            act_hi(act, "kv norm", KT, xhi)
            act_positions(act)
            u = FIRST["dkv"]
            for i in range(3):
                split_hi(act, u + i + 1)
                act.wait_ge(unit_used, u + i + 1)
                a.activation(lat[:, i, :] if i < 2 else kraw[:, :], mla_acc(f"dkv{i}"), ACT.Copy).then_inc(
                    *step("act", f"dkv{i} taken"))
            act_hi(act, "q norm", KT, xhi, used=FIRST["dq"])
            act_latent(act, "lat", 2, lhi)
            u = FIRST["dq"]
            for i in range(3):
                split_hi(act, u + i + 1)
                act.wait_ge(unit_used, u + i + 1)
                if i == 0:
                    act.wait_ge(*after("lat lo1"))
                a.activation(lat[:, i, :], mla_acc(f"dq{i}"), ACT.Copy).then_inc(*step("act", f"dq{i} taken"))
            u = FIRST["ukv"]
            for h in range(NH2):
                if h % 4 == 0:
                    split_hi(act, u + h // 4 + 1)
                act.wait_ge(*after(f"kn{h} full") if h % 4 < 3 else (unit_used, u + h // 4 + 1))
                a.activation(kn[:, h, :], mla_acc(f"kn{h}"), ACT.Copy).then_inc(*step("act", f"kn{h} taken"))
            for n in ("sin", "cos"):
                act.wait_ge(*after(f"{n} reduced"))
                a.activation(rot[:, n == "sin", :], ang[:, n == "cos", :], ACT.Sin).then_inc(*step("act", n))
            for gr in range(2):
                split_hi(act, u + 2 + gr + 1)
            act_latent(act, "cq", 3, chi)
            u = FIRST["uq"]
            for gr in range(2):
                for p in range(2):
                    split_hi(act, u + 3 * gr + p + 1)
                    for hh in range(2):
                        h = 4 * gr + 2 * p + hh
                        act.wait_ge(*after(f"qn{h} full") if hh == 0 else (unit_used, u + 3 * gr + p + 1))
                        a.activation(qn[:, h, :], mla_acc(f"qn{h}"), ACT.Copy, scale=QSCALE).then_inc(
                            *step("act", f"qn{h} taken"))
                split_hi(act, u + 3 * gr + 3)
                for p in range(2):
                    i = 2 * gr + p
                    act.wait_ge(*after(f"qp{i} full") if p == 0 else (unit_used, u + 3 * gr + 3))
                    a.activation(qp[:, i, :], mla_acc(f"qp{i}"), ACT.Copy, scale=QSCALE).then_inc(
                        *step("act", f"qp{i} taken"))

            def each(h):
                a.activation(xhi[:, h, :], full(act, f"mla O{h}"), ACT.Copy).then_inc(*step("act", f"mla hi{h}"))
            attn_act(act, "mla", NH2, mla_PT, each)

        def pool_mla(pool):
            pool.wait_ge(*after("kv norm scaled0"))
            g.memset(kpz[:, :, :], 0.0).then_inc(*step("pool", "kpz zeros"))

        def act_positions(act):
            act.wait_ge(*after("kv norm scaled0"))
            act.dma_start(turns[:, :], A["positions_2"][0].partition_broadcast(P)).then_inc(pos_loaded, 16)

        TWO_PI = 2 * np.pi
        TURN = [6.28125, 0.0019350051879882812, float(TWO_PI - 6.28125 - 0.0019350051879882812)]

        def dve_angles(dve):
            n = [0]

            def did(ins, name=None):
                n[0] += 1
                name = name or f"angle{n[0]}"
                ins.then_inc(*step("dve", name))
                dve.wait_ge(*after(name))

            s, c, w = ang[:, 0, :], ang[:, 1, :], rl[:, :]
            dve.wait_ge(pos_loaded, 16)
            dve.wait_ge(*after("lat lo1"))
            did(v.tensor_copy(s, turns[:, :]))
            did(v.tensor_scalar(s, s, C("freq"), None, ALU.mult))
            did(v.tensor_scalar(turns[:, :], s, float(1 / TWO_PI), None, ALU.mult))
            did(v.tensor_copy(w, turns[:, :]))
            for part in TURN:
                did(v.scalar_tensor_tensor(s, w, -part, s, ALU.mult, ALU.add))

            def wrap(x):
                for side, op in ((1.0, ALU.is_gt), (-1.0, ALU.is_lt)):
                    did(v.tensor_scalar(w, x, side * float(np.pi), -side * float(TWO_PI), op, ALU.mult))
                    did(v.tensor_tensor(x, x, w, ALU.add))

            wrap(s)
            did(v.tensor_scalar(c, s, float(np.pi / 2), None, ALU.add))
            wrap(c)
            for x, name in ((s, "sin"), (c, "cos")):
                did(v.tensor_scalar(x, x, 3.1415925, -3.1415925, ALU.min, ALU.max), f"{name} reduced")

        def dve_rotate(dve, key, x, name, before):
            w = xg[:, 0, :]
            dve.wait_ge(*after(before))
            v.tensor_tensor(w, full(dve, key), rot[:, 1, :], ALU.mult).then_inc(*step("dve", f"{key} taken"))
            v.tensor_tensor(x, x, rot[:, 0, :], ALU.mult).then_inc(*step("dve", f"{name} cos"))
            dve.wait_ge(*after(f"{name} cos"))
            v.tensor_tensor(x, x, w, ALU.add).then_inc(*step("dve", name))

        def dve_mla(dve):
            dve_scale(dve, "kv norm", KT, xT, "kv_norm_g_2", xhi, xlo, "mla norm rstd", rs[:, :])
            u = FIRST["dkv"]
            for i in range(3):
                split_lo(dve, u + i + 1)
            dve_scale(dve, "q norm", KT, xT, "mla_norm_g_2", xhi, xlo, "mla norm rstd", rs[:, :],
                      "kv norm lo7")
            dve_scale(dve, "lat", 2, lat, "kv_latent_norm_g_2", lhi, llo, "lat rstd", rl[:, :],
                      "q norm lo7")
            u = FIRST["dq"]
            for i in range(3):
                split_lo(dve, u + i + 1)
            dve_angles(dve)
            u = FIRST["ukv"]
            for i in range(2):
                split_lo(dve, u + i + 1)
            dve.wait_ge(*after("cos"))
            s = rot[:, 1, :]
            v.tensor_scalar(s, s, C("sign"), None, ALU.mult).then_inc(*step("dve", "signed sin"))
            dve.wait_ge(*after("signed sin"))
            dve_rotate(dve, "k swapped", kraw[:, :], "k rotated", "lat lo1")
            dve.wait_ge(*after("k rotated"))
            dve.wait_ge(*after("kpz zeros"))
            for half in range(2):
                v.tensor_copy(kpz[64 * half:64 * half + 64, half, :], kraw[64:P, :]).then_inc(
                    *step("dve", f"kpz{half}"))
            for gr in range(2):
                split_lo(dve, u + 2 + gr + 1)
                for t in range(TT):
                    dve.wait_ge(*after(f"v{gr}{t} full") if t < TT - 1 else (unit_used, u + 2 + gr + 1))
                    v.tensor_copy(vtok[:, t, 4 * P * gr:4 * P * (gr + 1)], mla_acc(f"v{gr}{t}")).then_inc(
                        *step("dve", f"v{gr}{t} taken"))
            dve_scale(dve, "cq", 3, lat, "mla_q_norm_g_2", chi, clo, "cq rstd", rl[:, :], "k rotated")
            u = FIRST["uq"]
            for gr in range(2):
                for p in range(3):
                    split_lo(dve, u + 3 * gr + p + 1)
                for p in range(2):
                    i = 2 * gr + p
                    dve_rotate(dve, f"q swapped{i}", qp[:, i, :], f"rotated{i}", f"rotated{i - 1}" if i else "cq lo2")

            def each(h):
                dve.wait_ge(*after(f"mla hi{h}"))
                v.tensor_tensor(xlo[:, h, :], full(dve, f"mla O{h}"), f32(xhi[:, h, :]),
                                ALU.subtract).then_inc(*step("dve", f"mla O{h} taken"))
            attn_dve(dve, "mla", NH2, each)

        def pe_final(pe):
            pe_sum(pe, "final norm", NORM0["ffn3_down"])
            for k in range(KT):
                pe.wait_ge(*after(f"final{k}"))
                out = pe_ring(pe, f"final{k}")
                for t in range(TT):
                    last = t_.transpose(out[:, t * P:(t + 1) * P], xg[:, k % 2, t * P:(t + 1) * P], C("ident"))
                last.then_inc(*step("pe", f"final{k} full"))

        def act_final(act):
            act_rstd(act, "final norm", D, rs[:, :])
            for k in range(KT):
                a.activation(fin[:, k, :], full(act, f"final{k}"), ACT.Copy).then_inc(*step("act", f"final{k} taken"))

        def dve_final(dve):
            dve.wait_ge(*after("final norm rstd"))
            for k in range(KT):
                if k >= 2:
                    dve.wait_ge(*after(f"final{k - 2} full"))
                v.scalar_tensor_tensor(xg[:, k % 2, :], xT[:, k, :], par("final_norm_g_2", k), rs[:, :], ALU.mult,
                                       ALU.mult).then_inc(*step("dve", f"final{k}"))

        def sp_final(sp):
            for k in range(KT):
                sp.wait_ge(*after(f"final{k} taken"))
                dst = out_d[0, :, k * P:(k + 1) * P].rearrange("(t p) c -> p t c", p=P)
                sp.dma_start(dst, fin[:, k, :].rearrange("p (t c) -> p t c", c=P)).then_inc(stored, 16)
            sp.wait_ge(stored, 16 * KT)

        GLA_READY = ["gla decay", "mix3"]

        def hg_ready(p):
            return [f"silu{10 + p} used", f"hg a{p}", f"hg k{p}", f"in{19 + p} taken"]

        block = ctx.enter_context(nc.Block())

        @block.sync
        def _(sp):
            sp_load_inputs(sp)
            for u in range(FIRST["w_out"]):
                load_unit(sp, u)
            def up(i, j):
                return (j % 2) * FF + (j // 2) * P + 2 * P * i
            def one(i, j):
                return j * P + 4 * P * i
            def thirds(i, j):
                return (j // 3) * P + 4 * P * i
            load_loop(sp, "w_out", KT, 4, one)
            load_loop(sp, "ffn1_up", 2 * FT, 4, up)
            load_loop(sp, "ffn1_down", 3 * KT, 12, thirds)
            load_loop(sp, "conv_in", 3 * KT, 12, lambda i, j: (j % 3) * D + (j // 3) * P + 4 * P * i)
            load_loop(sp, "conv_out", KT, 4, one)
            load_loop(sp, "ffn2_up", 2 * FT, 4, up)
            load_loop(sp, "ffn2_down", 3 * KT, 12, thirds)
            for u in range(FIRST["dkv"], FIRST["w_o"]):
                load_unit(sp, u)
            load_loop(sp, "w_o", KT, 4, one)
            load_loop(sp, "ffn3_up", 2 * FT, 4, up)
            load_loop(sp, "ffn3_down", 3 * KT, 12, thirds)
            sp_final(sp)

        @block.gpsimd
        def _(pool):
            pool_init(pool)
            pool_gdn(pool)
            for b in _LEVELS[1:]:
                for h in range(4):
                    pool_gdn_level(pool, b, h)
            pool_la(pool, "gla", GLA_READY)
            for p in range(2):
                pool_la(pool, f"hg{p}", hg_ready(p))
            pool_fox(pool)
            pool_clear(pool, "w_out", "mix1")
            pool_clear(pool, "ffn1_down", "norm2 sum full")
            pool_clear(pool, "conv_out", "conv norm sum full")
            pool_clear(pool, "ffn2_down", "ffn2 norm sum full")
            pool_clear(pool, "w_o", "mla norm sum full")
            pool_mla(pool)
            pool_clear(pool, "ffn3_down", "ffn3 norm sum full")

        @block.tensor
        def _(pe):
            pe_load(pe)
            for u in range(9):
                pe_in(pe, u)
            pe_gates(pe)
            for u in range(9, 15):
                pe_in(pe, u)
            pe_gdn_setup(pe)
            pe_gdn_triangles(pe)
            pe_gdn_inverse(pe)
            pe_gdn_operands(pe)
            pe_gdn_chunks(pe)
            pe_gdn_out(pe)
            pe_gla_gate(pe)
            pe_la(pe, "gla", ["in11 taken", "in12 taken"])
            pe_head_norm(pe, "gla out", 2)
            for u in range(15, 23):
                pe_in(pe, u)
            for p in range(2):
                pe_la(pe, f"hg{p}", [f"in{19 + p} taken"])
            pe_head_norm(pe, "hg out", 2)
            for u in range(23, 29):
                pe_in(pe, u)
            pe_fox(pe)

            def mixed(pe):
                for m in MIX_ORDER:
                    pe.wait_ge(*after(f"mix lo{m}"))
            pe_residual(pe, "w_out", False, (xhi, xlo), mixed)
            pe_sum(pe, "norm2", NORM0["w_out"])
            pe_up(pe, "ffn1_up", True, "norm2")
            def products(stage, n):
                return lambda pe: pe.wait_ge(prod_lo, PAIR0[stage] + n)
            pe_residual(pe, "ffn1_down", True, (h_hi, h_lo), products("ffn1_up", FT))
            pe_sum(pe, "conv norm", NORM0["ffn1_down"])
            pe_conv_in(pe)
            pe_residual(pe, "conv_out", False, (c_hi, c_lo), products("conv_in", KT))
            pe_sum(pe, "ffn2 norm", NORM0["conv_out"])
            pe_up(pe, "ffn2_up", False, "ffn2 norm")
            pe_residual(pe, "ffn2_down", True, (h_hi, h_lo), products("ffn2_up", FT))
            pe_sum(pe, "mla norm", NORM0["ffn2_down"])
            pe_mla(pe)
            pe_residual(pe, "w_o", False, (xhi, xlo), lambda pe: pe.wait_ge(*after(f"mla O{NH2 - 1} taken")))
            pe_sum(pe, "ffn3 norm", NORM0["w_o"])
            pe_up(pe, "ffn3_up", False, "ffn3 norm")
            pe_residual(pe, "ffn3_down", True, (h3_hi, h3_lo), products("ffn3_up", FT))
            pe_final(pe)

        @block.scalar
        def _(act):
            act_load_inputs(act)
            act_load(act)
            for u in range(9):
                split_hi(act, u + 1)
                if 1 <= u <= 6:
                    act_gdn_tap(act, u - 1)
                    if u >= 2:
                        act_silu(act, f"conv{u - 2}", mx[:, u - 2, :], f"in{u - 1} taken")
                elif u >= 7:
                    act_copy_in(act, u, mixT[:, u - 5, :])
                    if u == 7:
                        act_silu(act, "conv5", mx[:, 5, :], "in6 taken")
                    act_silu(act, f"z{u - 7}", mixT[:, u - 5, :], f"in{u} taken")
            act_gates(act)
            for u in range(9, 15):
                split_hi(act, u + 1)
                dst = (mx[:, 6, :], mx[:, 7, :], mixT[:, 0, :], mixT[:, 1, :], mixT[:, 6, :], mixT[:, 7, :])[u - 9]
                act_copy_in(act, u, dst, 32 ** -0.5 if u == 9 else 1.0)
                if u >= 13:
                    act_silu(act, f"gla g{u - 13}", dst, f"in{u} taken")
            act_ecol(act)
            act_gdn_setup(act)
            act_gdn_inverse(act)
            act_gdn_operands(act)
            act_gdn_chunks(act)
            act_gdn_out(act)
            act_gla_gate(act)
            act_la(act, "gla")
            act_la_out(act, "gla", GLA_OUT)
            act.wait_ge(*after("gla inter1 taken"))
            for u in range(15, 23):
                split_hi(act, u + 1)
                i = (u - 15) % 2
                if u in (17, 18):
                    act_hg_gate(act, i)
                    continue
                dst = {0: mx[:, 6 + i, :], 2: mx[:, (0, 17)[i], :], 3: mixT[:, 4 + i, :]}[(u - 15) // 2]
                act_copy_in(act, u, dst)
                if u < 17 or u >= 21:
                    act_silu(act, f"hg {u}", dst, f"in{u} taken")
            for p in range(2):
                act_la(act, f"hg{p}")
            act_la_out(act, "hg", HG_OUT)
            for u in range(23, 29):
                split_hi(act, u + 1)
                act_copy_in(act, u, mx[:, u - 23, :])
            act_fox(act)
            act_mix(act)
            act_residual(act, "w_out", False)
            act_rstd(act, "norm2", D, rs[:, :])
            act_hi(act, "norm2", KT, xhi)
            act_up(act, "ffn1_up", True, h_hi, yg, yu)
            act_residual(act, "ffn1_down", True)
            act_rstd(act, "conv norm", D, rs[:, :])
            act_hi(act, "conv norm", KT, xhi)
            act_conv_in(act, c_hi, bS, cS)
            act_residual(act, "conv_out", False)
            act_rstd(act, "ffn2 norm", D, rs[:, :])
            act_hi(act, "ffn2 norm", KT, xhi)
            act_up(act, "ffn2_up", False, h_hi, yg, yu)
            act_residual(act, "ffn2_down", True)
            act_mla(act)
            act_residual(act, "w_o", False)
            act_rstd(act, "ffn3 norm", D, rs[:, :])
            act_hi(act, "ffn3 norm", KT, xhi)
            act_up(act, "ffn3_up", False, h3_hi, yg3, None)
            act_residual(act, "ffn3_down", True)
            act_final(act)

        @block.vector
        def _(dve):
            dve_load(dve)
            for u in range(9):
                split_lo(dve, u + 1)
                if u == 0:
                    dve_gate_in(dve)
                elif u <= 6:
                    dve_gdn_conv(dve, u - 1)
                    if u >= 2:
                        dve_silu(dve, f"conv{u - 2}", mx[:, u - 2, :])
                else:
                    if u == 7:
                        dve_silu(dve, "conv5", mx[:, 5, :])
                    dve_silu(dve, f"z{u - 7}", mixT[:, u - 5, :])
            dve_gates(dve)
            dve_gcol(dve)
            for u in range(9, 15):
                split_lo(dve, u + 1)
                if u >= 13:
                    dve_silu(dve, f"gla g{u - 13}", mixT[:, u - 7, :])
            dve_gdn_setup(dve)
            dve_gdn_triangles(dve)
            for h in range(4):
                dve_gdn_first(dve, h)
            dve_gdn_inverse(dve)
            dve_gdn_operands(dve)
            dve_gdn_chunks(dve)
            dve_gdn_out(dve)
            dve_gla_gate(dve)
            dve_la(dve, "gla")
            dve_la_out(dve, "gla", "gla_on_g", GLA_OUT)
            for u in range(15, 23):
                split_lo(dve, u + 1)
                i = (u - 15) % 2
                if u < 17:
                    dve_silu(dve, f"hg {u}", mx[:, 6 + i, :], 0.125)
                elif u < 19:
                    dve_hg_gate(dve, i)
                elif u >= 21:
                    dve_silu(dve, f"hg {u}", mixT[:, 4 + i, :])
            for p in range(2):
                dve_la(dve, f"hg{p}")
            dve_la_out(dve, "hg", "hg_on_g", HG_OUT)
            for u in range(23, 29):
                split_lo(dve, u + 1)
            dve_fox(dve)
            dve_mix(dve)
            dve_residual(dve, "w_out", False)
            dve_scale(dve, "norm2", KT, xT, "norm2_g", xhi, xlo, "norm2 rstd", rs[:, :])
            dve_up(dve, "ffn1_up", True, h_hi, h_lo, yg, yu)
            dve_residual(dve, "ffn1_down", True)
            dve_scale(dve, "conv norm", KT, xT, "conv_norm_g_2", xhi, xlo, "conv norm rstd", rs[:, :])
            dve_conv_in(dve, c_hi, c_lo, bS, cS, zS, yS)
            dve_residual(dve, "conv_out", False)
            dve_scale(dve, "ffn2 norm", KT, xT, "conv_ffn_norm_g_2", xhi, xlo, "ffn2 norm rstd", rs[:, :])
            dve_up(dve, "ffn2_up", False, h_hi, h_lo, yg, yu)
            dve_residual(dve, "ffn2_down", True)
            dve_mla(dve)
            dve_residual(dve, "w_o", False)
            dve_scale(dve, "ffn3 norm", KT, xT, "mla_ffn_norm_g_2", xhi, xlo, "ffn3 norm rstd", rs[:, :])
            dve_up(dve, "ffn3_up", False, h3_hi, h3_lo, yg3, None)
            dve_residual(dve, "ffn3_down", True)
            dve_final(dve)

    return S


_OUT = (1, T, D)


def _program(nc, arrays, known):
    aps = {n: nc.dram_tensor(f"in_{n}", a.shape, mybir.dt.from_np(a.dtype), kind="ExternalInput").ap()
           for n, a in arrays.items()}
    out = nc.dram_tensor("out_0", _OUT, F32, kind="ExternalOutput").ap()
    cst = aps.pop("constants")
    flat = {n: (x[0] if len(x.shape) == 3 and n in _WEIGHTS else x) for n, x in aps.items()}
    return build(nc, flat, cst, out, known)


_WEIGHTS = {u[0] for u in UNITS}


def kernel(**inputs):
    import concourse.bacc as bacc
    from concourse.bass_utils import run_bass_kernel_spmd

    arrays = {n: np.ascontiguousarray(a) for n, a in inputs.items()}
    arrays["constants"] = constants()
    numbers = None
    for _ in range(2):
        nc = bacc.Bacc("TRN2", target_bir_lowering=False, num_devices=1)
        numbers = _program(nc, arrays, numbers)
    r = run_bass_kernel_spmd(nc, [{f"in_{n}": a for n, a in arrays.items()}], core_ids=[0])
    return r.results[0]["out_0"]
```

```python
import numpy as np
import concourse.bass as bass
from concourse import mybir
from contextlib import ExitStack

F32 = mybir.dt.float32
F32R = mybir.dt.float32r
I32 = mybir.dt.int32
ALU = mybir.AluOpType
ACT = mybir.ActivationFunctionType
AX = mybir.AxisListType

P = 128
T = 512
D = 1024
KT = D // P
TT = T // P
DH = 64
FF = 2816
FT = FF // P
THIRDS = ((0, 8), (8, 7), (15, 7))
GC = 64
LC = 16
NL = T // LC
NH2 = 8
EPS = 1e-6
UNIT = KT * P
RAW = 4
PARTS = 2

_LEVELS = [1, 2, 4, 8, 16, 32]
_COLS = {}


def _lay():
    at = 0
    sizes = [("ident", P), ("hsum", P), ("ones", P), ("neg", P), ("incl", P)]
    sizes += [(f"lev{b}", P) for b in _LEVELS]
    sizes += [("gla0", P), ("gla1", P), ("perm", P)]
    sizes += [(f"foxrow{h}", P) for h in range(4)] + [(f"gdnrow{h}", P) for h in range(4)]
    sizes += [(f"beta{p}", P) for p in range(2)] + [(f"gpair{p}", P) for p in range(2)]
    sizes += [("cmask", 8), ("hmask", 2), ("qmask", 4), ("freq", 1), ("sign", 1), ("eps", 1)]
    for name, n in sizes:
        _COLS[name] = (at, n)
        at += n
    return at


NCONST = _lay()


def constants():
    c = np.zeros((P, NCONST), np.float32)

    def put(name, a):
        at, n = _COLS[name]
        c[:, at:at + n] = a

    i = np.arange(P)
    s, r = i[:, None], i[None, :]
    put("ident", s == r)
    put("hsum", s // DH == r // DH)
    put("ones", 1.0)
    put("neg", np.where(r > s, -1e30, 0.0))
    put("incl", (s // GC == r // GC) & (s <= r))
    for b in _LEVELS:
        put(f"lev{b}", (s // (2 * b) == r // (2 * b)) & (s % (2 * b) < b) & (r % (2 * b) >= b))
    for w in range(2):
        put(f"gla{w}", s // 32 == 2 * w + r // DH)
    put("perm", (s // 64 == r // 64) & (s % 64 == (r + 32) % 64))
    for h in range(4):
        put(f"foxrow{h}", (s == h) & (r >= 0))
        put(f"gdnrow{h}", (s == 64 + h) & (r >= 0))
    for p in range(2):
        put(f"beta{p}", s == 32 + 2 * p + r // DH)
        put(f"gpair{p}", s == 64 + 2 * p + r // DH)
    put("cmask", i[:, None] // LC == np.arange(8)[None, :])
    put("hmask", i[:, None] // 64 == np.arange(2)[None, :])
    put("qmask", i[:, None] // 32 == np.arange(4)[None, :])
    inv = np.float32(10000.0) ** (-np.arange(0, 64, 2, dtype=np.float32) / np.float32(64))
    put("freq", inv[i % 32][:, None])
    put("sign", np.where(i % 64 < 32, -1.0, 1.0)[:, None])
    put("eps", EPS)
    return c


_ROWS = {}
_row_at = 0
for _name, _n in [("norm1_g", 8), ("norm2_g", 8), ("conv_norm_g_2", 8), ("conv_ffn_norm_g_2", 8), ("kv_norm_g_2", 8),
                  ("mla_norm_g_2", 8), ("mla_ffn_norm_g_2", 8), ("final_norm_g_2", 8), ("kv_latent_norm_g_2", 2),
                  ("mla_q_norm_g_2", 3), ("conv_w_2", 24), ("gdn_conv_w", 24), ("gla_b_gk", 1), ("fox_qn_g", 1),
                  ("fox_kn_g", 1), ("fox_on_g", 1), ("gdn_on_g", 1), ("hg_on_g", 1), ("gla_on_g", 1)]:
    _ROWS[_name] = (_row_at, _n)
    _row_at += _n
NROW0 = _row_at
NCONVW = 3 * 2 * FT
NROW1 = P
NROW2 = NCONVW - P + 2 * FT
NPCOL = NROW0 + NROW1 + NROW2

UNITS = []
FIRST = {}


def _units():
    def add(stage, name, kt, pieces):
        FIRST.setdefault(stage, len(UNITS))
        UNITS.append((name, kt, sum(n for _, _, n in pieces), pieces))

    gdn, z, hg, gla, gk, gg = 772, 1548, 1804, 2828, 3340, 3356
    add("w_in", "w_in", KT, [(0, 768, 32), (0, 1540, 32), (0, 1544, 32), (0, gk, 32)])
    for c in [gdn + P * i for i in range(6)] + [z, z + P]:
        add("w_in", "w_in", KT, [(0, c, P)])
    for c in [gla, gla + P, gla + 2 * P, gla + 3 * P, gg, gg + P]:
        add("w_in", "w_in", KT, [(0, c, P)])
    for i in range(8):
        add("w_in", "w_in", KT, [(0, hg + P * i, P)])
    for i in range(6):
        add("w_in", "w_in", KT, [(0, P * i, P)])
    for i in range(KT):
        add("w_out", "w_out", KT, [(0, P * i, P)])

    def ffn(stage, up, down):
        for i in range(FT):
            add(stage + "_up", up, KT, [(0, P * i, P)])
            add(stage + "_up", up, KT, [(0, FF + P * i, P)])
        for i in range(KT):
            for k0, k in THIRDS:
                add(stage + "_down", down, k, [(k0 * P, P * i, P)])

    ffn("ffn1", "w_up", "w_down")
    for i in range(KT):
        for part in range(3):
            add("conv_in", "conv_w_in_2", KT, [(0, part * D + P * i, P)])
    for i in range(KT):
        add("conv_out", "conv_w_out_2", KT, [(0, P * i, P)])
    ffn("ffn2", "conv_ffn_w13_2", "conv_ffn_w2_2")
    for c in [0, P, P + 64]:
        add("dkv", "w_dkv_2", KT, [(0, c, P)])
    for i in range(3):
        add("dq", "mla_w_dq_2", KT, [(0, P * i, P)])
    for part in range(2):
        for g in range(2):
            add("ukv", "w_ukv_2", 2, [(0, (4 * g + h) * 256 + part * P, P) for h in range(4)])
    for g in range(2):
        for p in range(2):
            add("uq", "mla_w_uq_2", 3, [(0, 192 * (4 * g + 2 * p + h), P) for h in range(2)])
        add("uq", "mla_w_uq_2", 3, [(0, 192 * (4 * g + h) + P, 64) for h in range(4)])
    for i in range(KT):
        add("w_o", "mla_w_o_2", KT, [(0, P * i, P)])
    ffn("ffn3", "mla_ffn_w13_2", "mla_ffn_w2_2")


_units()
LOADED = []
_sum = [0] * RAW
for _u, (_n, _k, _c, _pieces) in enumerate(UNITS):
    _sum[_u % RAW] += 16 * len(_pieces)
    LOADED.append(_sum[_u % RAW])


class Steps:

    def __init__(self, sems, known):
        self.sems, self.known = sems, known
        self.count = dict.fromkeys(sems, 0)
        self.at, self.banks, self.ring, self.last = {}, {}, 0, {}

    def step(self, engine, name):
        assert name not in self.at, name
        self.count[engine] += 1
        self.at[name] = (engine, self.count[engine])
        return self.sems[engine], 1

    def after(self, name):
        if self.known is None:
            return self.sems["dve"], 1
        engine, value = self.known.at[name]
        return self.sems[engine], value

    def take_bank(self, key, n):
        b = self.ring % n
        self.ring += 1
        self.banks[key] = b
        before = self.last.get(b)
        self.last[b] = key
        return b, before

    def bank(self, key):
        return self.known.banks[key] if self.known else 0



TILE0, NORM0, PAIR0, GATED0, XPART0 = {}, {}, {}, {}, {}
_tiles = _pairs = _gates = 0
for _s in ["w_out", "ffn1_up", "ffn1_down", "conv_in", "conv_out", "ffn2_up", "ffn2_down", "w_o", "ffn3_up", "ffn3_down"]:
    TILE0[_s] = _tiles
    if _s == "conv_in" or _s.endswith("_up"):
        _n = KT if _s == "conv_in" else FT
        PAIR0[_s], GATED0[_s] = _pairs, _gates
        _tiles += (3 if _s == "conv_in" else 2) * _n
        _pairs += _n
        _gates += 0 if _s == "conv_in" else _n
    else:
        NORM0[_s] = KT * len(NORM0)
        _tiles += KT
for _s in ["norm2_g", "conv_norm_g_2", "conv_ffn_norm_g_2", "kv_norm_g_2", "mla_norm_g_2", "mla_ffn_norm_g_2"]:
    XPART0[_s] = KT * len(XPART0)




def build(nc, A, cst_d, out_d, known):
    ctx = ExitStack()
    with ctx:
        def sb(name, shape, dt=F32, c=ctx):
            return c.enter_context(nc.sbuf_tensor(name, shape, dt))

        def sem(name):
            return ctx.enter_context(nc.semaphore(name))

        xT = sb("xT", [P, KT, T])
        xhi = sb("xhi", [P, KT, T], F32R)
        xlo = sb("xlo", [P, KT, T], F32R)
        raw = sb("raw", [P, RAW, UNIT])
        whi = sb("whi", [P, PARTS, UNIT], F32R)
        wlo = sb("wlo", [P, PARTS, UNIT], F32R)
        cst = sb("cst", [P, NCONST])
        pcol = sb("pcol", [P, NPCOL])
        gbias = sb("gbias", [P, 4])
        sq = sb("sq", [P, 2, T])
        ssq = sb("ssq", [P, T])
        rs = sb("rs", [P, T])
        xg = sb("xg", [P, 2, T])
        stat = sb("stat", [P, 4, 4])
        credit = sb("credit", [P, 8])
        ps = ctx.enter_context(nc.psum_tensor("ps", [P, 8, T], F32))
        NRING = 6

        def acc(tile):
            return ps[:, tile % 2, :]

        def ring(b):
            return ps[:, 2 + b, :]

        def C(name):
            at, n = _COLS[name]
            return cst[:, at:at + n]

        def par(name, k=0):
            return pcol[:, _ROWS[name][0] + k:_ROWS[name][0] + k + 1]

        def tile_of(buf, m):
            return buf[:, bass.ds(m, 1), :].rearrange("p o t -> p (o t)")

        S = Steps({e: sem(f"{e}_steps") for e in ("pe", "act", "dve", "pool")}, known)
        step, after = S.step, S.after
        unit_loaded = [sem(f"unit_loaded{i}") for i in range(RAW)]
        hi_split, lo_split, unit_used = sem("hi_split"), sem("lo_split"), sem("unit_used")
        acc_free = sem("acc_free")
        x_hi, x_lo, squared, summed = sem("x_hi"), sem("x_lo"), sem("squared"), sem("summed")
        tap_done, tap2_done, conv_done, gated = sem("tap_done"), sem("tap2_done"), sem("conv_done"), sem("gated")
        prod_done, prod_hi, prod_lo = sem("prod_done"), sem("prod_hi"), sem("prod_lo")
        x_loaded = [sem(f"x_loaded{i}") for i in range(TT)]
        cst_loaded, rows_loaded, small_loaded, x_again = (sem(n) for n in
                                                          ("cst_loaded", "rows_loaded", "small_loaded", "x_again"))
        pos_loaded, stored = sem("pos_loaded"), sem("stored")
        v, a, g, t_ = nc.vector, nc.scalar, nc.gpsimd, nc.tensor

        def f32(ap):
            return ap.bitcast(F32)

        def pe_ring(pe, key):
            b, before = S.take_bank(key, NRING)
            if before is not None:
                pe.wait_ge(*after(f"{before} taken"))
            return ring(b)

        def full(eng, key):
            eng.wait_ge(*after(f"{key} full"))
            return ring(S.bank(key))

        def unit_view(buf, u):
            _, kt, n, _ = UNITS[u]
            return buf[:, u % (RAW if buf is raw else PARTS), 0:kt * n].rearrange("p (k c) -> p k c", c=n)

        def is_past(u, i, per):
            return u + (per * i if isinstance(i, int) else 0) >= len(UNITS)

        def in_loop(value, i, per):
            return value if i is None else value + per * i

        def load_unit(sp, u):
            name, kt, n, pieces = UNITS[u]
            if u >= RAW:
                sp.wait_ge(lo_split, u - RAW + 1)
            at = 0
            for r0, c0, m in pieces:
                dst = unit_view(raw, u)[:, :, at:at + m]
                src = A[name][r0:r0 + kt * P, c0:c0 + m].rearrange("(k p) c -> p k c", p=P)
                sp.dma_start(dst, src).then_inc(unit_loaded[u % RAW], 16)
                at += m

        def load_loop(sp, stage, n_units, per, col):
            with sp.Fori(0, n_units // per) as i:
                for j in range(per):
                    u = FIRST[stage] + j
                    name, kt, n, pieces = UNITS[u]
                    r0 = pieces[0][0]
                    sp.wait_ge(lo_split, u - RAW + 1 + per * i)
                    src = A[name][r0:r0 + kt * P, bass.ds(col(i, j), n)].rearrange("(k p) c -> p k c", p=P)
                    sp.dma_start(unit_view(raw, u), src).then_inc(unit_loaded[u % RAW], 16)

        def elements(u, i, per):
            units = [UNITS[u]] + ([UNITS[u + per]] if i is not None and u + per < len(UNITS) else [])
            return max(kt * n for _, kt, n, _ in units)

        def split_hi(act, u, i=None, per=0):
            if is_past(u, i, per):
                return
            n = elements(u, i, per)
            act.wait_ge(unit_loaded[u % RAW], in_loop(LOADED[u], i, 16 * per // RAW))
            if u >= PARTS:
                act.wait_ge(unit_used, in_loop(u - PARTS + 1, i, per))
            a.activation(whi[:, u % PARTS, 0:n], raw[:, u % RAW, 0:n], ACT.Copy).then_inc(hi_split, 1)

        def split_lo(dve, u, i=None, per=0):
            if is_past(u, i, per):
                return
            n = elements(u, i, per)
            dve.wait_ge(hi_split, in_loop(u + 1, i, per))
            v.tensor_tensor(wlo[:, u % PARTS, 0:n], raw[:, u % RAW, 0:n], f32(whi[:, u % PARTS, 0:n]),
                            ALU.subtract).then_inc(lo_split, 1)

        def passes(out, wh, wl, xh, xl, first, last):
            t_.matmul(out, wh, xh, start=first, stop=False)
            t_.matmul(out, wh, xl, start=False, stop=False)
            return t_.matmul(out, wl, xh, start=False, stop=last)

        def product(pe, u, tile, i=None, per=0, x=(xhi, xlo), k0=0, start=True, stop=True, ready=None, cols=0,
                    full=None, order=None, ks=None):
            kt = UNITS[u][1]
            pe.wait_ge(lo_split, in_loop(u + 1, i, per))
            for n, k in list(enumerate(order or range(kt)))[slice(*(ks or (0, kt)))]:
                if ready is not None:
                    ready(pe, k0 + k)
                wh, wl = (unit_view(b, u)[:, k, cols:cols + P] for b in (whi, wlo))
                last = passes(acc(tile), wh, wl, x[0][:, k0 + k, :], x[1][:, k0 + k, :],
                              start and n == 0, stop and n == kt - 1)
            if ks is None or ks[1] == kt:
                last.then_inc(*(step("pe", full) if full else (unit_used, 1)))

        def pe_sum(pe, name, n0):
            out = pe_ring(pe, f"{name} sum")
            pe.wait_ge(summed, n0 + KT + 2)
            t_.matmul(out, C("ones"), ssq[:, :], start=True, stop=True).then_inc(*step("pe", f"{name} sum full"))

        def act_rstd(act, name, width, out):
            key = f"{name} sum"
            a.preload_act_table_set("natural_log_exp_and_others")
            bank = full(act, key)
            a.activation(out, bank, ACT.Ln, scale=1.0 / width, bias=C("eps")).then_inc(*step("act", f"{key} taken"))
            act.wait_ge(*after(f"{key} taken"))
            a.activation(out, out, ACT.Exp, scale=-0.5).then_inc(*step("act", f"{name} rstd"))

        def dve_scale(dve, name, tiles, src, gain, hi, lo, rstd, r, before=None):
            def low(k):
                dve.wait_ge(*after(f"{name} hi{k}"))
                v.tensor_tensor(lo[:, k, :], xg[:, k % 2, :], f32(hi[:, k, :]),
                                ALU.subtract).then_inc(*step("dve", f"{name} lo{k}"))
            dve.wait_ge(*after(rstd))
            if before:
                dve.wait_ge(*after(before))
            for k in range(tiles):
                if k >= 2:
                    dve.wait_ge(*after(f"{name} lo{k - 2}"))
                v.scalar_tensor_tensor(xg[:, k % 2, :], src[:, k, :], par(gain, k), r, ALU.mult,
                                       ALU.mult).then_inc(*step("dve", f"{name} scaled{k}"))
                if k:
                    low(k - 1)
            low(tiles - 1)

        def act_hi(act, name, tiles, hi):
            for k in range(tiles):
                act.wait_ge(*after(f"{name} scaled{k}"))
                a.activation(hi[:, k, :], xg[:, k % 2, :], ACT.Copy).then_inc(*step("act", f"{name} hi{k}"))

        def gain_of(name, k):
            return pcol[:, bass.ds(_ROWS[name][0] + k, 1)]

        def act_gained(act, name, k):
            a.activation(tile_of(xhi, k), tile_of(xT, k), ACT.Copy, scale=gain_of(name, k)).then_inc(x_hi, 1)

        def dve_gained(dve, name, k, n):
            dve.wait_ge(x_hi, n)
            v.scalar_tensor_tensor(tile_of(xlo, k), tile_of(xT, k), gain_of(name, k), f32(tile_of(xhi, k)), ALU.mult,
                                   ALU.subtract).then_inc(x_lo, 1)

        def act_gain_all(act, name, used):
            act.wait_ge(unit_used, used)
            for k in range(KT):
                act_gained(act, name, k)

        def dve_gain_all(dve, name):
            for k in range(KT):
                dve_gained(dve, name, k, XPART0[name] + k + 1)

        def parts_of(name):
            return lambda pe, k: pe.wait_ge(x_lo, XPART0[name] + k + 1)

        def rounds(engine, stage, n, body):
            last = FIRST[stage] + n * 12 == len(UNITS)
            with engine.Fori(0, n - last) as i:
                body(i)
            if last:
                body(n - 1)

        def round_of(thirds):
            per, np_ = (12, 3) if thirds else (4, 1)
            return per, np_, per // np_

        def pe_residual(pe, stage, thirds, x, ready, order=None):
            per, np_, tiles = round_of(thirds)
            parts = THIRDS if thirds else ((0, KT),)
            n0 = TILE0[stage]
            with pe.Fori(0, KT // tiles) as i:
                for j in range(per):
                    m, part = divmod(j, np_)
                    if part == 0:
                        pe.wait_ge(acc_free, n0 + m + 1 + tiles * i)
                    product(pe, FIRST[stage] + j, m, i, per, x, parts[part][0], part == 0, part == np_ - 1,
                            ready if m == 0 else None, order=order)

        def act_residual(act, stage, thirds, gain):
            per, np_, tiles = round_of(thirds)
            r0, n0 = NORM0[stage], TILE0[stage]

            def body(i):
                for j in range(per):
                    split_hi(act, FIRST[stage] + j + 2, i, per)
                    if j % np_ == np_ - 1:
                        m = j // np_
                        act.wait_ge(acc_free, n0 + m + 3 + tiles * i)
                        act.wait_ge(summed, r0 + m + 1 + tiles * i)
                        a.activation(sq[:, m % 2, :], tile_of(xT, m + tiles * i), ACT.Square).then_inc(squared, 1)
                        if gain:
                            act_gained(act, gain, m + tiles * i)
            rounds(act, stage, KT // tiles, body)

        def dve_residual(dve, stage, thirds, gain):
            per, np_, tiles = round_of(thirds)
            n0 = TILE0[stage]

            def body(i):
                for j in range(per):
                    if j % np_ == np_ - 1:
                        m = j // np_
                        dve.wait_ge(unit_used, FIRST[stage] + j + 1 + per * i)
                        x = tile_of(xT, m + tiles * i)
                        v.tensor_tensor(x, acc(m), x, ALU.add).then_inc(acc_free, 1)
                    split_lo(dve, FIRST[stage] + j + 2, i, per)
                    if j % np_ == np_ - 1 and gain:
                        dve.wait_ge(acc_free, n0 + m + 3 + tiles * i)
                        dve_gained(dve, gain, m + tiles * i, XPART0[gain] + m + 1 + tiles * i)
            rounds(dve, stage, KT // tiles, body)

        def pool_residual(pool, stage, reader):
            r0 = NORM0[stage]
            pool.wait_ge(*after(reader))
            g.memset(ssq[:, :], 0.0).then_inc(*step("pool", f"{stage} sum cleared"))
            pool.wait_ge(*after(f"{stage} sum cleared"))
            with pool.Fori(0, KT // 2) as i:
                for m in range(2):
                    pool.wait_ge(squared, r0 + m + 1 + 2 * i)
                    pool.wait_ge(summed, r0 + m + 2 + 2 * i)
                    g.tensor_tensor(ssq[:, :], ssq[:, :], sq[:, m, :], ALU.add).then_inc(summed, 1)

        def ffn_w(k, m):
            return pcol[:, bass.ds(NROW0 + k * 2 * FT + m, 1)]

        def ffn_b(m):
            return pcol[:, bass.ds(NROW0 + NCONVW + m, 1)]

        def pe_up(pe, stage, name, gain, residual):
            n0 = TILE0[stage]

            def body(i, first):
                for j in range(4):
                    pe.wait_ge(acc_free, n0 + j + 1 + 4 * i)
                    product(pe, FIRST[stage] + j, j, i, 4, ready=parts_of(gain) if first and j == 0 else None)
                    if first and j == 0:
                        pe_sum(pe, name, NORM0[residual])
            body(0, True)
            with pe.Fori(1, FT // 2) as i:
                body(i, False)

        def act_up(act, stage, conv, h_hi, zS, yg, yu):
            u0, p0, n0 = FIRST[stage], PAIR0[stage], TILE0[stage]
            a.preload_act_table_set("silu_and_others")
            with act.Fori(0, FT // 2) as i:
                for j in range(4):
                    pair, is_up = j // 2, j % 2
                    m = pair + 2 * i
                    split_hi(act, u0 + j + 2, i, 4)
                    if conv:
                        mt = m + FT * is_up
                        act.wait_ge(prod_done, p0 + pair + 1 + 2 * i)
                        act.wait_ge(acc_free, n0 + j + 3 + 4 * i)
                        a.activation((yu if is_up else yg)[:, pair, :], zS[:, is_up, :], ACT.Identity,
                                     scale=ffn_w(2, mt), bias=ffn_b(mt)).then_inc(tap_done, 1)
                        if is_up:
                            act.wait_ge(conv_done, j + 2 + 4 * i)
                            a.activation(yg[:, pair, :], yg[:, pair, :], ACT.Silu).then_inc(gated, 1)
                    elif not is_up:
                        act.wait_ge(acc_free, n0 + j + 3 + 4 * i)
                        a.activation(yg[:, pair, :], zS[:, 0, :], ACT.Silu).then_inc(gated, 1)
                    if is_up:
                        act.wait_ge(prod_done, p0 + pair + 3 + 2 * i)
                        a.activation(tile_of(h_hi, m), xg[:, pair, :], ACT.Copy).then_inc(prod_hi, 1)

        def dve_up(dve, stage, conv, rstd, zS, yg, yu):
            u0, p0, n0 = FIRST[stage], PAIR0[stage], TILE0[stage]
            dve.wait_ge(*after(rstd))
            with dve.Fori(0, FT // 2) as i:
                for j in range(4):
                    pair, is_up = j // 2, j % 2
                    z = zS[:, is_up, :]
                    dve.wait_ge(unit_used, u0 + j + 1 + 4 * i)
                    if conv:
                        dve.wait_ge(conv_done, j + 1 + 4 * i)
                    else:
                        dve.wait_ge(prod_done, p0 + pair + 2 + 2 * i)
                    v.tensor_tensor(z, acc(j), rs[:, :], ALU.mult).then_inc(acc_free, 1)
                    split_lo(dve, u0 + j + 2, i, 4)
                    dve.wait_ge(acc_free, n0 + j + 3 + 4 * i)
                    if conv:
                        y, mt = (yu if is_up else yg)[:, pair, :], pair + 2 * i + FT * is_up
                        dve.wait_ge(tap_done, j + 1 + 4 * i)
                        v.scalar_tensor_tensor(y[:, 1:T], z[:, 0:T - 1], ffn_w(1, mt), y[:, 1:T], ALU.mult,
                                               ALU.add).then_inc(tap2_done, 1)
                        dve.wait_ge(tap2_done, j + 1 + 4 * i)
                        v.scalar_tensor_tensor(y[:, 2:T], z[:, 0:T - 2], ffn_w(0, mt), y[:, 2:T], ALU.mult,
                                               ALU.add).then_inc(conv_done, 1)
                    if is_up:
                        if conv:
                            dve.wait_ge(conv_done, j + 3 + 4 * i)
                        dve.wait_ge(gated, GATED0[stage] + pair + 1 + 2 * i)
                        dve.wait_ge(prod_lo, p0 + pair + 1 + 2 * i)
                        v.tensor_tensor(xg[:, pair, :], yg[:, pair, :], yu[:, pair, :] if conv else z,
                                        ALU.mult).then_inc(prod_done, 1)

        def pool_products(pool, stage, n, h_hi, h_lo):
            p0 = PAIR0[stage]
            with pool.Fori(0, n // 2) as i:
                for m in range(2):
                    pool.wait_ge(prod_hi, p0 + m + 1 + 2 * i)
                    g.tensor_tensor(tile_of(h_lo, m + 2 * i), xg[:, m, :], f32(tile_of(h_hi, m + 2 * i)),
                                    ALU.subtract).then_inc(prod_lo, 1)

        def pe_conv_in(pe):
            n0 = TILE0["conv_in"]

            def body(i, first):
                for j in range(12):
                    pe.wait_ge(acc_free, n0 + j + 1 + 12 * i)
                    product(pe, FIRST["conv_in"] + j, j, i, 12,
                            ready=parts_of("conv_norm_g_2") if first and j == 0 else None)
                    if first and j == 0:
                        pe_sum(pe, "conv norm", NORM0["ffn1_down"])
            body(0, True)
            with pe.Fori(1, KT // 4) as i:
                body(i, False)

        def act_conv_in(act, h_hi, zS, yS):
            u0, p0 = FIRST["conv_in"], PAIR0["conv_in"]
            with act.Fori(0, KT // 4) as i:
                for j in range(12):
                    m, part = divmod(j, 3)
                    split_hi(act, u0 + j + 2, i, 12)
                    if part == 2:
                        act.wait_ge(acc_free, TILE0["conv_in"] + j + 3 + 12 * i)
                        act.wait_ge(prod_done, p0 + m + 1 + 4 * i)
                        a.activation(yS[:, m % 2, :], zS[:, m % 2, :], ACT.Copy,
                                     scale=gain_of("conv_w_2", 2 * KT + m + 4 * i)).then_inc(tap_done, 1)
                        act.wait_ge(prod_done, p0 + m + 3 + 4 * i)
                        a.activation(tile_of(h_hi, m + 4 * i), xg[:, m % 2, :], ACT.Copy).then_inc(prod_hi, 1)

        def dve_conv_in(dve, bS, cS, zS, yS, r2):
            u0, p0, n0 = FIRST["conv_in"], PAIR0["conv_in"], TILE0["conv_in"]
            dve.wait_ge(*after("conv norm rstd"))
            v.tensor_tensor(r2[:, :], rs[:, :], rs[:, :], ALU.mult).then_inc(*step("dve", "conv norm rstd^2"))
            dve.wait_ge(*after("conv norm rstd^2"))
            with dve.Fori(0, KT // 4) as i:
                for j in range(12):
                    m, part = divmod(j, 3)
                    z, y = zS[:, m % 2, :], yS[:, m % 2, :]
                    dve.wait_ge(unit_used, u0 + j + 1 + 12 * i)
                    if part == 0:
                        dve.wait_ge(prod_done, p0 + m + 1 + 4 * i)
                    if part < 2:
                        v.tensor_tensor((bS, cS)[part][:, m % 2, :], acc(j), (rs, r2)[part][:, :],
                                        ALU.mult).then_inc(acc_free, 1)
                        split_lo(dve, u0 + j + 2, i, 12)
                        continue
                    dve.wait_ge(acc_free, n0 + j + 2 + 12 * i)
                    v.tensor_tensor(z, cS[:, m % 2, :], acc(j), ALU.mult).then_inc(acc_free, 1)
                    split_lo(dve, u0 + j + 2, i, 12)
                    w = [gain_of("conv_w_2", KT * k + m + 4 * i) for k in range(2)]
                    c0 = 2 * FT + 2 * m + 8 * i
                    t0 = 2 * FT + m + 1 + 4 * i
                    dve.wait_ge(acc_free, n0 + j + 3 + 12 * i)
                    dve.wait_ge(tap_done, t0)
                    v.scalar_tensor_tensor(y[:, 1:T], z[:, 0:T - 1], w[1], y[:, 1:T], ALU.mult,
                                           ALU.add).then_inc(tap2_done, 1)
                    dve.wait_ge(tap2_done, c0 + 1)
                    v.scalar_tensor_tensor(y[:, 2:T], z[:, 0:T - 2], w[0], y[:, 2:T], ALU.mult,
                                           ALU.add).then_inc(tap2_done, 1)
                    dve.wait_ge(tap2_done, c0 + 2)
                    dve.wait_ge(prod_lo, p0 + m + 1 + 4 * i)
                    v.tensor_tensor(xg[:, m % 2, :], y, bS[:, m % 2, :], ALU.mult).then_inc(prod_done, 1)

        mixers = ctx.enter_context(ExitStack())
        mx = sb("mx", [P, 36, T], c=mixers)
        mixT = sb("mixT", [P, KT, T], c=mixers)
        graw = sb("graw", [P, T], c=mixers)
        grow = sb("grow", [P, T], c=mixers)
        gcol = sb("gcol", [P, TT, P], c=mixers)
        ecol = sb("ecol", [P, TT, 36], c=mixers)
        lastone = sb("lastone", [P, T], c=mixers)
        vnew = sb("vnew", [P, 2, 4 * DH], c=mixers)
        state = sb("state", [P, 2, P], c=mixers)
        wgk = sb("wgk", [P, P], c=mixers)
        hr = (rs[:, :], ssq[:, :])
        wide = mx[:, :, :].rearrange("p a t -> p (a t)")

        def wtile(k, n):
            return wide[:, k * T:(k + n) * T]

        xtok = wtile(0, 8).rearrange("p (t d) -> p t d", d=D)
        prow = wtile(8, 1).rearrange("p (n c) -> p n c", c=P)
        scanmask = mx[:, 35, :]
        Q, K, V = 0, 2, 4
        KZ, KB, MTt, X_, XT_, AT, Y = 10, 14, 16, 20, 24, 28, 32
        kbg, vb, kout, wT = wtile(10, 2), wtile(12, 2), wtile(4, 2), wtile(14, 2)
        kbg, vb, kout = (b.rearrange("p (t c) -> p t c", t=TT) for b in (kbg, vb, kout))
        wT = wT.rearrange("p (h t) -> p h t", h=2)
        uu, oo = (wtile(k, 2).rearrange("p (t c) -> p t c", t=TT) for k in (32, 34))

        def sp_load_inputs(sp):
            for t in range(TT):
                sp.dma_start(xtok[:, t, :], A["x"][0, t * P:(t + 1) * P, :]).then_inc(x_loaded[t], 16)

        N_SMALL = 4

        def act_load_inputs(act):
            act.dma_start(cst[:, :], cst_d).then_inc(cst_loaded, 16)
            n = 0
            act.wait_ge(*after("rows cleared"))
            for name, (r0, rows) in _ROWS.items():
                src = A[name]
                if src.shape[-1] == DH:
                    row = src if len(src.shape) == 2 else src.rearrange("(o n) -> o n", o=1)
                    for half in range(2):
                        act.dma_start(prow[r0:r0 + 1, 0, half * DH:(half + 1) * DH], row).then_inc(rows_loaded, 16)
                        n += 1
                    continue
                if len(src.shape) == 1:
                    src = src.rearrange("(m c) -> m c", c=P)
                elif len(src.shape) == 2:
                    src = src.rearrange("o (m c) -> (o m) c", c=P)
                else:
                    src = src.rearrange("o k (m c) -> (o k m) c", c=P)
                act.dma_start(prow[r0:r0 + rows, 0, :], src).then_inc(rows_loaded, 16)
                n += 1
            w = A["ffn_conv_w"].rearrange("o k (m c) -> (o k m) c", c=P)
            bias = A["ffn_conv_b"].rearrange("o (m c) -> (o m) c", c=P)
            act.dma_start(prow[:, 1, :], w[0:P, :]).then_inc(rows_loaded, 16)
            act.dma_start(prow[0:NCONVW - P, 2, :], w[P:NCONVW, :]).then_inc(rows_loaded, 16)
            act.dma_start(prow[NCONVW - P:NROW2, 2, :], bias).then_inc(rows_loaded, 16)
            act.wait_ge(*after("small cleared"))
            act.dma_start(gbias[0:4, 0:1], A["fox_b_f"].rearrange("o h -> h o")).then_inc(small_loaded, 16)
            act.dma_start(gbias[64:68, 0:1], A["gdn_dt_bias"].rearrange("o h -> h o")).then_inc(small_loaded, 16)
            act.dma_start(gbias[64:68, 1:2], A["gdn_a_log"].rearrange("o h -> h o")).then_inc(small_loaded, 16)
            act.dma_start(wgk[96:112, :], A["gla_w_gk"][0]).then_inc(small_loaded, 16)
            return n + 3

        N_ROWS = sum(2 if A[n].shape[-1] == DH else 1 for n in _ROWS) + 3

        def pool_init(pool):
            g.memset(prow[:, :, :], 0.0).then_inc(*step("pool", "rows cleared"))
            g.memset(gbias[:, :], 0.0)
            g.memset(wgk[:, :], 0.0).then_inc(*step("pool", "small cleared"))
            for n, s in enumerate((acc_free, summed, prod_done, prod_lo, conv_done)):
                g.memset(credit[:, n:n + 1], 0.0).then_inc(s, 2)
            g.memset(scanmask, 1.0).then_inc(*step("pool", "scanmask ones"))
            pool.wait_ge(*after("scanmask ones"))
            g.memset(scanmask[64:68].rearrange("p (n c) -> p n c", c=GC)[:, :, 0:1], 0.0).then_inc(
                *step("pool", "scanmask"))
            pool.wait_ge(*after("scanmask"))
            g.memset(lastone[:, :], 0.0).then_inc(*step("pool", "lastone zeros"))
            pool.wait_ge(*after("lastone zeros"))
            g.memset(lastone[:, :].rearrange("p (n c) -> p n c", c=LC)[:, :, LC - 1:LC], 1.0)
            g.memset(mx[:, 33, :], 0.0)
            g.memset(vnew[:, :, :], 0.0)
            g.memset(state[:, :, :], 0.0).then_inc(*step("pool", "mixers cleared"))

        def pe_load(pe):
            pe.wait_ge(cst_loaded, 16)
            pe.wait_ge(rows_loaded, 16 * N_ROWS)
            out = pe_ring(pe, "params")
            at = 0
            for n, rows in enumerate((NROW0, NROW1, NROW2)):
                last = t_.transpose(out[:, at:at + rows], prow[0:rows, n, :], C("ident")[0:rows, 0:rows])
                at += rows
            last.then_inc(*step("pe", "params full"))
            for k in range(KT):
                out = pe_ring(pe, f"x{k}")
                for t in range(TT):
                    if k == 0:
                        pe.wait_ge(*after(f"x normed{t}"))
                    last = t_.transpose(out[:, t * P:(t + 1) * P], xtok[:, t, k * P:(k + 1) * P], C("ident"))
                last.then_inc(*step("pe", f"x{k} full"))

        def act_load(act):
            a.preload_act_table_set("natural_log_exp_and_others")
            act.wait_ge(cst_loaded, 16)
            for t in range(TT):
                ss, ln, rstd = (stat[:, t, n:n + 1] for n in range(3))
                act.wait_ge(x_loaded[t], 16)
                a.activation(wtile(10 + 2 * t, 2), xtok[:, t, :], ACT.Square, accum_out=ss).then_inc(
                    *step("act", f"x squares{t}"))
                act.wait_ge(*after(f"x squares{t}"))
                a.activation(ln, ss, ACT.Ln, scale=1.0 / D, bias=C("eps")).then_inc(*step("act", f"x ln{t}"))
                act.wait_ge(*after(f"x ln{t}"))
                a.activation(rstd, ln, ACT.Exp, scale=-0.5).then_inc(*step("act", f"x rstd{t}"))
            split_hi(act, 0)
            split_hi(act, 1)
            act.wait_ge(*after("params taken"))
            for k in range(KT):
                a.activation(xhi[:, k, :], full(act, f"x{k}"), ACT.Copy, scale=par("norm1_g", k)).then_inc(
                    *step("act", f"x hi{k}"))

        def dve_load(dve):
            v.tensor_copy(pcol[:, :], full(dve, "params")[:, 0:NPCOL]).then_inc(*step("dve", "params taken"))
            for t in range(TT):
                dve.wait_ge(*after(f"x rstd{t}"))
                v.tensor_scalar(xtok[:, t, :], xtok[:, t, :], stat[:, t, 2:3], None, ALU.mult).then_inc(
                    *step("dve", f"x normed{t}"))
            split_lo(dve, 0)
            split_lo(dve, 1)
            for k in range(KT):
                dve.wait_ge(*after(f"x hi{k}"))
                v.scalar_tensor_tensor(xlo[:, k, :], full(dve, f"x{k}"), par("norm1_g", k), f32(xhi[:, k, :]), ALU.mult,
                                       ALU.subtract).then_inc(*step("dve", f"x{k} taken"))

        xagain = wtile(27, 8).rearrange("p (t d) -> p t d", d=D)

        def act_load_again(act):
            for m in (4, 5):
                act.wait_ge(*after(f"mix{m}"))
            for t in range(TT):
                act.dma_start(xagain[:, t, :], A["x"][0, t * P:(t + 1) * P, :]).then_inc(x_again, 16)

        def pe_x_again(pe, ks):
            pe.wait_ge(x_again, 16 * TT)
            for k in ks:
                out = pe_ring(pe, f"xT{k}")
                for t in range(TT):
                    last = t_.transpose(out[:, t * P:(t + 1) * P], xagain[:, t, k * P:(k + 1) * P], C("ident"))
                last.then_inc(*step("pe", f"xT{k} full"))

        def act_x_again(act, ks):
            for k in ks:
                a.activation(xT[:, k, :], full(act, f"xT{k}"), ACT.Copy).then_inc(*step("act", f"xT{k} taken"))

        def pe_in(pe, u, ks=None):
            if u >= 2:
                pe.wait_ge(*after(f"in{u - 2} taken"))
            product(pe, u, u, ready=(lambda pe, k: pe.wait_ge(*after(f"x{k} taken"))) if u == 0 else None, ks=ks)

        def act_copy_in(act, u, dst, scale=1.0):
            act.wait_ge(unit_used, u + 1)
            a.activation(dst, acc(u), ACT.Copy, scale=scale).then_inc(*step("act", f"in{u} taken"))

        silu_n = {"act": 0, "dve": 0}

        def act_sigmoid(act, name, x, e, sign):
            a.activation(e, x, ACT.Exp, scale=-sign).then_inc(*step("act", f"{name} exp"))
            act.wait_ge(*after(f"{name} exp"))
            a.activation(e, e, ACT.Ln, bias=1.0).then_inc(*step("act", f"{name} ln"))
            act.wait_ge(*after(f"{name} ln"))
            a.activation(e, e, ACT.Exp, scale=-1.0).then_inc(*step("act", f"{name} sigmoid"))

        def act_silu(act, name, x, ready):
            n = silu_n["act"]
            silu_n["act"] += 1
            act.wait_ge(*after(ready))
            if n >= 2:
                act.wait_ge(*after(f"silu{n - 2} used"))
            act_sigmoid(act, name, x, xg[:, n % 2, :], 1.0)

        def dve_silu(dve, name, x, scale=1.0):
            n = silu_n["dve"]
            silu_n["dve"] += 1
            dve.wait_ge(*after(f"{name} sigmoid"))
            v.scalar_tensor_tensor(x, x, scale, xg[:, n % 2, :], ALU.mult, ALU.mult).then_inc(
                *step("dve", f"silu{n} used"))

        def act_head_norm(act, name, src, ready, scale, n=0):
            for i, x in enumerate(src):
                act.wait_ge(*after(ready[i]))
                if i >= 2:
                    act.wait_ge(*after(f"{name} sum{i - 2} full"))
                a.activation(sq[:, i % 2, :], x, ACT.Square).then_inc(*step("act", f"{name} square{i}"))
                if i:
                    act_head_rs(act, name, i - 1, scale)
            act_head_rs(act, name, len(src) - 1, scale)

        def act_head_rs(act, name, i, scale):
            key = f"{name} sum{i}"
            if i >= 2:
                act.wait_ge(*after(f"{name} {i - 2}"))
            r = hr[i % 2]
            a.activation(r, full(act, key), ACT.Ln, scale=scale, bias=C("eps")).then_inc(*step("act", f"{key} taken"))
            act.wait_ge(*after(f"{key} taken"))
            a.activation(r, r, ACT.Exp, scale=-0.5).then_inc(*step("act", f"{name} rs{i}"))

        def pe_head_norm(pe, name, n):
            for i in range(n):
                out = pe_ring(pe, f"{name} sum{i}")
                pe.wait_ge(*after(f"{name} square{i}"))
                t_.matmul(out, C("hsum"), sq[:, i % 2, :], start=True, stop=True).then_inc(
                    *step("pe", f"{name} sum{i} full"))

        def dve_head_norm(dve, name, src, gain):
            for i, x in enumerate(src):
                dve.wait_ge(*after(f"{name} rs{i}"))
                v.scalar_tensor_tensor(x, x, gain[i], hr[i % 2], ALU.mult,
                                       ALU.mult).then_inc(*step("dve", f"{name} {i}"))

        def pe_transpose(pe, key, x, ready):
            out = pe_ring(pe, key)
            if ready:
                pe.wait_ge(*after(ready))
            for t in range(TT):
                last = t_.transpose(out[:, t * P:(t + 1) * P], x[:, t * P:(t + 1) * P], C("ident"))
            last.then_inc(*step("pe", f"{key} full"))

        LS, LG = mx[:, 32, :], mx[:, 34, :]
        D1 = mx[:, 33, :]

        def dve_gate_in(dve):
            dve.wait_ge(small_loaded, 16 * N_SMALL)
            dve.wait_ge(unit_used, 1)
            v.tensor_scalar(graw[:, :], acc(0), gbias[:, 0:1], None, ALU.add).then_inc(*step("dve", "in0 taken"))

        def act_gates(act):
            act.wait_ge(*after("in0 taken"))
            a.activation(gbias[64:68, 2:3], gbias[64:68, 1:2], ACT.Exp).then_inc(*step("act", "exp a_log"))
            a.activation(LG, graw[:, :], ACT.Abs).then_inc(*step("act", "gate abs"))
            act.wait_ge(*after("gate abs"))
            a.activation(LG, LG, ACT.Exp, scale=-1.0).then_inc(*step("act", "gate exp"))
            act.wait_ge(*after("gate exp"))
            a.activation(LG, LG, ACT.Ln, bias=1.0).then_inc(*step("act", "gate ln"))
            act.wait_ge(*after("gate scan"))
            a.activation(grow[32:36, :], LS[32:36, :], ACT.Exp).then_inc(*step("act", "beta"))

        def dve_gates(dve):
            dve.wait_ge(*after("gate ln"))
            dve.wait_ge(*after("mixers cleared"))
            v.scalar_tensor_tensor(LS, graw[:, :], 0.0, LG, ALU.min, ALU.subtract).then_inc(*step("dve", "log sigmoid"))
            dve.wait_ge(*after("log sigmoid"))
            v.tensor_scalar(D1[0:4], LS[0:4], -1.0, None, ALU.mult)
            v.tensor_tensor(D1[64:68], LS[64:68], graw[64:68, :], ALU.subtract).then_inc(*step("dve", "-softplus"))
            dve.wait_ge(*after("-softplus"))
            v.tensor_scalar(D1[64:68], D1[64:68], gbias[64:68, 2:3], None, ALU.mult).then_inc(*step("dve", "decay"))
            dve.wait_ge(*after("decay"))
            v.tensor_tensor_scan(grow[:, :], scanmask, D1, 0.0, ALU.mult, ALU.add).then_inc(*step("dve", "gate scan"))
            dve.wait_ge(*after("gate scan"))
            G3 = grow[64:68, :].rearrange("p (n c) -> p n c", c=GC)
            v.tensor_tensor(grow[96:100, :].rearrange("p (n c) -> p n c", c=GC),
                            G3[:, :, GC - 1:GC].to_broadcast([4, T // GC, GC]), G3,
                            ALU.subtract).then_inc(*step("dve", "to chunk end"))

        def pe_gates(pe):
            pe.wait_ge(*after("beta"))
            pe_transpose(pe, "gcol", grow[:, :], "to chunk end")

        def dve_gcol(dve):
            v.tensor_copy(gcol[:, :, :].rearrange("p t c -> p (t c)"),
                          full(dve, "gcol")).then_inc(*step("dve", "gcol taken"))

        def act_ecol(act):
            act.wait_ge(*after("gcol taken"))
            a.activation(ecol[:, :, :], gcol[:, :, 64:100], ACT.Exp).then_inc(*step("act", "ecol"))

        def act_gdn_tap(act, i):
            act.wait_ge(unit_used, i + 2)
            if i == 0:
                act.wait_ge(*after("x7 taken"))
            a.activation(mx[:, i, :], acc(i + 1), ACT.Identity,
                         scale=par("gdn_conv_w", 18 + i)).then_inc(*step("act", f"gdn tap{i}"))

        def dve_gdn_conv(dve, i):
            y = mx[:, i, :]
            dve.wait_ge(*after(f"gdn tap{i}"))
            for back in (1, 2, 3):
                name = f"in{i + 1} taken" if back == 3 else f"gdn tap{i} {back}"
                v.scalar_tensor_tensor(y[:, back:T], acc(i + 1)[:, 0:T - back], par("gdn_conv_w", 6 * (3 - back) + i),
                                       y[:, back:T], ALU.mult, ALU.add).then_inc(*step("dve", name))
                if back < 3:
                    dve.wait_ge(*after(name))

        GDN_QK = [mx[:, i, :] for i in range(4)]

        def pe_gdn_setup(pe):
            pe_head_norm(pe, "gdn qk", 4)
            for p in range(2):
                out = pe_ring(pe, f"beta{p}")
                t_.matmul(out, C(f"beta{p}"), grow[:, :], start=True, stop=True).then_inc(
                    *step("pe", f"beta{p} full"))
            for h in range(4):
                out = pe_ring(pe, f"gdn G{h}")
                t_.matmul(out, C(f"gdnrow{h}"), grow[:, :], start=True, stop=True).then_inc(
                    *step("pe", f"gdn G{h} full"))

        def pool_gdn(pool):
            for h in range(4):
                pool.wait_ge(*after(f"gdn qk {2 + h // 2}"))
                g.tensor_scalar(mx[:, KZ + h, :], mx[:, K + h // 2, :], C("hmask")[:, h % 2:h % 2 + 1], None,
                                ALU.mult).then_inc(*step("pool", f"gdn kz{h}"))

        def act_gdn_setup(act):
            act_head_norm(act, "gdn qk", GDN_QK, [f"silu{i} used" for i in range(4)], 1.0)
            for h in range(4):
                act.wait_ge(*after(f"gdn G{h} taken"))
                a.activation(mx[:, Y + h, :], mx[:, Y + h, :], ACT.Exp).then_inc(*step("act", f"gdn decay{h}"))

        def dve_gdn_setup(dve):
            gains = [0.125, 0.125, 1.0, 1.0]
            dve_head_norm(dve, "gdn qk", GDN_QK, gains)
            for p in range(2):
                dve.wait_ge(*after(f"gdn qk {2 + p}"))
                v.tensor_tensor(mx[:, KB + p, :], mx[:, K + p, :], full(dve, f"beta{p}"),
                                ALU.mult).then_inc(*step("dve", f"beta{p} taken"))
            for h in range(4):
                bank = full(dve, f"gdn G{h}")
                if h == 0:
                    dve.wait_ge(*after("gcol taken"))
                    dve.wait_ge(*after("beta"))
                for t in range(TT):
                    blk = slice(t * P, (t + 1) * P)
                    last = t == TT - 1
                    v.tensor_scalar(mx[:, Y + h, blk], bank[:, blk], gcol[:, t, 64 + h:65 + h], 0.0, ALU.subtract,
                                    ALU.min).then_inc(*step("dve", f"gdn G{h} taken" if last else f"gdn exponent{h} {t}"))
            for h in range(4):
                e = mx[:, Y + h, :].rearrange("p (t r) -> p t r", r=P)
                dve.wait_ge(*after(f"gdn decay{h}"))
                v.tensor_tensor(e, e, C("incl").unsqueeze(1).to_broadcast([P, TT, P]),
                                ALU.mult).then_inc(*step("dve", f"gdn masked{h}"))

        def blocks(tile):
            return mx[:, tile, :].rearrange("p (t r) -> p t r", r=P)

        def pe_block_products(pe, key, lhs, rhs):
            out = pe_ring(pe, key)
            for t in range(TT):
                blk = slice(t * P, (t + 1) * P)
                last = t_.matmul(out[:, blk], lhs[:, blk], rhs[:, blk], start=True, stop=True)
            last.then_inc(*step("pe", f"{key} full"))

        def pe_gdn_triangles(pe):
            for h in range(4):
                pe.wait_ge(*after(f"gdn kz{h}"))
                pe.wait_ge(*after(f"beta{h // 2} taken"))
                pe_block_products(pe, f"gdn M{h}", mx[:, KZ + h, :], mx[:, KB + h // 2, :])
                pe_block_products(pe, f"gdn A{h}", mx[:, KZ + h, :], mx[:, Q + h // 2, :])

        def dve_gdn_triangles(dve):
            for h in range(4):
                dve.wait_ge(*after(f"gdn masked{h}"))
                v.tensor_tensor(mx[:, MTt + h, :], full(dve, f"gdn M{h}"), mx[:, Y + h, :],
                                ALU.mult).then_inc(*step("dve", f"gdn M{h} taken"))
                v.tensor_tensor(mx[:, AT + h, :], full(dve, f"gdn A{h}"), mx[:, Y + h, :],
                                ALU.mult).then_inc(*step("dve", f"gdn A{h} taken"))

        def bmask(b):
            return C(f"lev{b}").unsqueeze(1).to_broadcast([P, TT, P])

        def pool_gdn_level(pool, b, h):
            if b == 2:
                pool.wait_ge(*after(f"gdn A{h} taken"))
            else:
                pool.wait_ge(*after(f"gdn Y{b // 2} {h} full"))
            g.tensor_tensor(blocks(Y + h), blocks(MTt + h), bmask(b), ALU.mult).then_inc(
                *step("pool", f"gdn O{b} {h}"))

        def dve_gdn_first(dve, h):
            dve.wait_ge(*after(f"gdn M{h} taken"))
            v.tensor_tensor(blocks(XT_ + h), blocks(MTt + h), bmask(1), ALU.mult).then_inc(*step("dve", f"gdn O1 {h}"))
            dve.wait_ge(*after(f"gdn O1 {h}"))
            v.tensor_tensor(blocks(XT_ + h), C("ident").unsqueeze(1).to_broadcast([P, TT, P]), blocks(XT_ + h),
                            ALU.subtract).then_inc(*step("dve", f"gdn XT1 {h}"))

        def pe_gdn_inverse(pe):
            for h in range(4):
                pe_transpose(pe, f"gdn X1 {h}", mx[:, XT_ + h, :], f"gdn XT1 {h}")
            for b in _LEVELS[1:]:
                for h in range(4):
                    pe.wait_ge(*after(f"gdn O{b} {h}"))
                    pe.wait_ge(*after(f"gdn X1 {h} taken" if b == 2 else f"gdn XOX{b // 2} {h} taken"))
                    pe_block_products(pe, f"gdn Y{b} {h}", mx[:, Y + h, :], mx[:, X_ + h, :])
                for h in range(4):
                    pe.wait_ge(*after(f"gdn Y{b} {h} taken"))
                    if b > 2:
                        pe.wait_ge(*after(f"gdn XOXT{b // 2} {h} taken"))
                    if b < 32:
                        pe_block_products(pe, f"gdn XOX{b} {h}", mx[:, XT_ + h, :], mx[:, OX + h, :])
                    pe_block_products(pe, f"gdn XOXT{b} {h}", mx[:, OX + h, :], mx[:, XT_ + h, :])

        OX = KZ

        def act_gdn_inverse(act):
            for h in range(4):
                a.activation(mx[:, X_ + h, :], full(act, f"gdn X1 {h}"), ACT.Copy).then_inc(
                    *step("act", f"gdn X1 {h} taken"))
            for b in _LEVELS[1:]:
                for h in range(4):
                    if b == 2:
                        act.wait_ge(*after(f"gdn A{h} full"))
                    else:
                        act.wait_ge(*after(f"gdn XOXT{b // 2} {h} full"))
                    a.activation(mx[:, OX + h, :], full(act, f"gdn Y{b} {h}"), ACT.Copy).then_inc(
                        *step("act", f"gdn Y{b} {h} taken"))

        def dve_gdn_inverse(dve):
            for b in _LEVELS[1:]:
                for h in range(4):
                    dve.wait_ge(*after(f"gdn XOXT{b} {h} full"))
                    if b < 32:
                        v.tensor_tensor(mx[:, X_ + h, :], mx[:, X_ + h, :], full(dve, f"gdn XOX{b} {h}"),
                                        ALU.subtract).then_inc(*step("dve", f"gdn XOX{b} {h} taken"))
                    v.tensor_tensor(mx[:, XT_ + h, :], mx[:, XT_ + h, :], full(dve, f"gdn XOXT{b} {h}"),
                                    ALU.subtract).then_inc(*step("dve", f"gdn XOXT{b} {h} taken"))

        def pe_gdn_operands(pe):
            for p in range(2):
                pe_transpose(pe, f"gdn kT{p}", mx[:, K + p, :], f"gdn qk {2 + p}")
            for p in range(2):
                pe_transpose(pe, f"gdn vT{p}", mx[:, V + p, :], f"silu{4 + p} used")
            for p in range(2):
                out = pe_ring(pe, f"gdn Gp{p}")
                t_.matmul(out, C(f"gpair{p}"), grow[:, :], start=True, stop=True).then_inc(
                    *step("pe", f"gdn Gp{p} full"))
            for h in range(4):
                out = pe_ring(pe, f"gdn w{h}")
                pe.wait_ge(*after(f"gdn kbg {h}"))
                pe.wait_ge(*after(f"gdn XOXT32 {h} taken"))
                for t in range(TT):
                    last = t_.matmul(out[:, t * P:(t + 1) * P], kbg[:, t, P * (h // 2):P * (h // 2) + P],
                                     blocks(XT_ + h)[:, t, :], start=True, stop=True)
                last.then_inc(*step("pe", f"gdn w{h} full"))
            for i in range(2):
                out = pe_ring(pe, f"gdn u{i}")
                pe.wait_ge(*after("gdn vT1 taken"))
                for t in (2 * i, 2 * i + 1):
                    for h in range(4):
                        at = (t % 2) * 4 * DH + h * DH
                        last = t_.matmul(out[:, at:at + DH], blocks(XT_ + h)[:, t, :], vb[:, t, h * DH:(h + 1) * DH],
                                         start=True, stop=True)
                last.then_inc(*step("pe", f"gdn u{i} full"))

        def head_cols(buf, p):
            return buf[:, :, P * p:P * (p + 1)].rearrange("p t (h c) -> p t h c", h=2)

        def dve_gdn_operands(dve):
            dve.wait_ge(*after("ecol"))
            dve.wait_ge(*after("gdn XOXT32 3 full"))
            for p in range(2):
                bank = full(dve, f"gdn kT{p}").rearrange("p (t h c) -> p t h c", t=TT, h=2)
                for hh in range(2):
                    h = 2 * p + hh
                    dst = kbg[:, :, h * DH:(h + 1) * DH]
                    v.tensor_tensor(dst, bank[:, :, hh, :], gcol[:, :, 32 + h:33 + h].to_broadcast([P, TT, DH]),
                                    ALU.mult).then_inc(*step("dve", f"gdn kb {h}"))
                    dve.wait_ge(*after(f"gdn kb {h}"))
                    v.tensor_tensor(dst, dst, ecol[:, :, h:h + 1].to_broadcast([P, TT, DH]),
                                    ALU.mult).then_inc(*step("dve", f"gdn kbg {h}"))
            for p in range(2):
                bank = full(dve, f"gdn vT{p}").rearrange("p (t h c) -> p t h c", t=TT, h=2)
                for hh in range(2):
                    h = 2 * p + hh
                    v.tensor_tensor(vb[:, :, h * DH:(h + 1) * DH], bank[:, :, hh, :],
                                    gcol[:, :, 32 + h:33 + h].to_broadcast([P, TT, DH]),
                                    ALU.mult).then_inc(*step("dve", f"gdn vT{p} taken" if hh else f"gdn vb {h}"))
            for p in range(2):
                bank = full(dve, f"gdn kT{p}").rearrange("p (t h c) -> p t h c", t=TT, h=2)
                if p == 0:
                    dve.wait_ge(*after("gdn vT1 full"))
                for hh in range(2):
                    h = 2 * p + hh
                    v.tensor_tensor(kout[:, :, h * DH:(h + 1) * DH], bank[:, :, hh, :],
                                    ecol[:, :, 32 + h:33 + h].to_broadcast([P, TT, DH]),
                                    ALU.mult).then_inc(*step("dve", f"gdn kT{p} taken" if hh else f"gdn ko {h}"))
            for p in range(2):
                dve.wait_ge(*after(f"gdn Gp{p} taken"))
                v.tensor_tensor(mx[:, Q + p, :], mx[:, Q + p, :], mx[:, 8 + p, :],
                                ALU.mult).then_inc(*step("dve", f"gdn q_in{p}"))
            for i in range(2):
                v.tensor_copy(uu[:, 2 * i:2 * i + 2, :].rearrange("p t c -> p (t c)"),
                              full(dve, f"gdn u{i}")).then_inc(*step("dve", f"gdn u{i} taken"))

        def act_gdn_operands(act):
            for p in range(2):
                a.activation(mx[:, 8 + p, :], full(act, f"gdn Gp{p}"), ACT.Exp).then_inc(
                    *step("act", f"gdn Gp{p} taken"))
            for h in range(4):
                rows = slice(64 * (h % 2), 64 * (h % 2) + 64)
                a.activation(wT[rows, h // 2, :], full(act, f"gdn w{h}")[rows, :], ACT.Copy).then_inc(
                    *step("act", f"gdn w{h} taken"))

        def pe_gdn_chunks(pe, unit):
            for c in range(T // GC):
                t, par_ = c // 2, c % 2
                blk = slice(t * P, (t + 1) * P)
                out = pe_ring(pe, f"gdn wS{c}")
                if c == 0:
                    pe.wait_ge(*after("gdn w3 taken"))
                    pe.wait_ge(*after("mixers cleared"))
                    pe.wait_ge(*after("gdn q_in1"))
                else:
                    pe.wait_ge(*after(f"gdn kv{c - 1} taken"))
                for p in range(2):
                    last = t_.matmul(out[:, P * p:P * (p + 1)], wT[:, p, blk], state[:, p, :], start=True, stop=True)
                last.then_inc(*step("pe", f"gdn wS{c} full"))
                pe_in(pe, unit + c, (0, KT // 2))
                outo = pe_ring(pe, f"gdn o{c}")
                outk = pe_ring(pe, f"gdn kv{c}")
                pe.wait_ge(*after(f"gdn wS{c} taken"))
                for p in range(2):
                    last = t_.matmul(outk[:, P * p:P * (p + 1)], kout[:, t, P * p:P * (p + 1)],
                                     vnew[:, par_, P * p:P * (p + 1)], start=True, stop=True)
                last.then_inc(*step("pe", f"gdn kv{c} full"))
                for p in range(2):
                    for hh in range(2):
                        h = 2 * p + hh
                        cols = slice(h * DH, (h + 1) * DH)
                        t_.matmul(outo[:, cols], mx[:, Q + p, blk], state[:, p, hh * DH:(hh + 1) * DH], start=True,
                                  stop=False)
                        last = t_.matmul(outo[:, cols], blocks(AT + h)[:, t, :], vnew[:, par_, cols], start=False,
                                         stop=True)
                last.then_inc(*step("pe", f"gdn o{c} full"))
                pe_in(pe, unit + c, (KT // 2, KT))

        def dve_gdn_chunks(dve, unit):
            for c in range(T // GC):
                t, rows = c // 2, slice(64 * (c % 2), 64 * (c % 2) + 64)
                bank = full(dve, f"gdn wS{c}")
                if c == 0:
                    dve.wait_ge(*after("gdn u1 taken"))
                if c >= 2:
                    dve.wait_ge(*after(f"gdn o{c - 2} full"))
                v.tensor_tensor(vnew[rows, c % 2, :], uu[rows, t, :], bank[rows, 0:4 * DH],
                                ALU.subtract).then_inc(*step("dve", f"gdn wS{c} taken"))
                bank = full(dve, f"gdn kv{c}")
                dve.wait_ge(*after(f"gdn o{c} full"))
                for h in range(4):
                    p, r = h // 2, slice(64 * (h % 2), 64 * (h % 2) + 64)
                    end = GC * c + GC - 1
                    st = state[r, p, r]
                    v.scalar_tensor_tensor(st, st, mx[r, 8 + p, end:end + 1], bank[r, P * p + r.start:P * p + r.stop],
                                           ALU.mult, ALU.add).then_inc(
                                               *step("dve", f"gdn kv{c} taken" if h == 3 else f"gdn state{c} {h}"))
                unit(c)

        def act_gdn_chunks(act, unit):
            for c in range(T // GC):
                t, rows = c // 2, slice(64 * (c % 2), 64 * (c % 2) + 64)
                a.activation(oo[rows, t, :], full(act, f"gdn o{c}")[rows, 0:4 * DH], ACT.Copy).then_inc(
                    *step("act", f"gdn o{c} taken"))
                unit(c)

        GDN_O = [mx[:, K + p, :] for p in range(2)]

        def pe_gdn_out(pe):
            for p in range(2):
                out = pe_ring(pe, f"gdn oT{p}")
                pe.wait_ge(*after("gdn o7 taken"))
                for t in range(TT):
                    last = t_.transpose(out[:, t * P:(t + 1) * P], oo[:, t, P * p:P * (p + 1)], C("ident"))
                last.then_inc(*step("pe", f"gdn oT{p} full"))
            pe_head_norm(pe, "gdn out", 2)

        def act_gdn_out(act):
            for p in range(2):
                a.activation(GDN_O[p], full(act, f"gdn oT{p}"), ACT.Copy).then_inc(*step("act", f"gdn oT{p} taken"))
            act_head_norm(act, "gdn out", GDN_O, [f"gdn oT{p} taken" for p in range(2)], 1.0 / DH)

        def dve_gdn_out(dve):
            dve_head_norm(dve, "gdn out", GDN_O, [par("gdn_on_g")] * 2)
            for p in range(2):
                dve.wait_ge(*after(f"gdn out {p}"))
                v.tensor_tensor(mixT[:, 2 + p, :], mixT[:, 2 + p, :], GDN_O[p], ALU.mult).then_inc(
                    *step("dve", f"mix{2 + p}"))

        A0, PP, SF, AM, KO, KOT, VT, VX, KV, AX_, O_, QI = 0, 1, 2, 3, 14, 15, 16, 18, 20, 24, 32, 34
        TJ, PROD, TMP, QZ = (5, 35), (8, 9), (28, 29, 30, 31), 10

        def chunks(x):
            return x.rearrange("p (n c) -> p n c", c=LC)

        LA = {"gla": dict(q=mx[:, 6, :], k=mx[:, 7, :], a=mx[:, A0, :], v=[mixT[:, 0, :], mixT[:, 1, :]],
                          o=[mx[:, O_, :], mx[:, O_ + 1, :]], red=["gla0", "gla1"], dk=32, mask="qmask")}
        for p in range(2):
            LA[f"hg{p}"] = dict(q=xT[:, p, :], k=xT[:, 4 + p, :], a=xT[:, 2 + p, :], v=[xT[:, 6 + p, :]],
                                o=[mx[:, O_ + p, :]], red=["hsum"], dk=64, mask="hmask")
        am = wtile(AM, 2)
        KVw, AXw = wtile(KV, 4), wtile(AX_, 4)
        for L in LA.values():
            L["heads"] = [(L["dk"] * h, h // 2, 64 * (h % 2)) for h in range(P // L["dk"])]
        cm = C("cmask").unsqueeze(2).to_broadcast([P, 8, DH])
        GROUP = 8

        def la_spread(eng, e, nm, n, engine):
            h, t = divmod(n, TT)
            _, vi, r0 = LA[nm]["heads"][h]
            eng.wait_ge(*after(f"{nm} v{vi} taken"))
            if n >= 2:
                eng.wait_ge(*after(f"{nm} kv{n - 2} full"))
            src = mx[:, VT + vi, t * P + r0:t * P + r0 + DH].unsqueeze(1).to_broadcast([P, 8, DH])
            e.tensor_tensor(mx[:, VX + n % 2, :].rearrange("p (c d) -> p c d", d=DH), src, cm,
                            ALU.mult).then_inc(*step(engine, f"{nm} spread{n}"))

        def la_add(eng, e, nm, j, vi, engine):
            L = LA[nm]
            n, m = LC - j, (j - 1) * len(L["v"]) + vi
            eng.wait_ge(*after(f"{nm} intra{j} {vi} taken"))
            eng.wait_ge(*after(f"{nm} o{j - 1} {vi}" if j >= 2 else f"{nm} intra0 {vi} taken"))
            o3 = chunks(L["o"][vi])[:, :, j:LC]
            e.tensor_tensor(o3, o3, mx[:, TMP[m % 4], 0:NL * n].rearrange("p (n c) -> p n c", c=n),
                            ALU.add).then_inc(*step(engine, f"{nm} o{j} {vi}"))

        def pool_la(pool, nm, before=None):
            L = LA[nm]
            ax = chunks(L["a"])
            if before:
                pool.wait_ge(*after(f"{before} prod{LC - 1}"))
            pool.wait_ge(*after(f"{nm} am copy"))
            g.memset(mx[:, VX, :], 0.0).then_inc(*step("pool", f"{nm} d1 zeros"))
            g.memset(AXw.rearrange("p (d c) -> p d c", c=NL)[:, :, 0:1], 0.0).then_inc(*step("pool", f"{nm} ax zeros"))
            g.memset(chunks(am[:, 0:T])[:, :, 0:1], 0.0)
            g.memset(am[:, T:T + 1], 0.0)
            pool.wait_ge(*after(f"{nm} d1 zeros"))
            g.tensor_copy(chunks(mx[:, VX, :])[:, :, 0:1], ax[:, :, 0:1]).then_inc(*step("pool", f"{nm} scan inputs"))

            def t_next(j):
                prev = chunks(L["q"] if j == 1 else mx[:, TJ[(j - 1) % 2], :])
                if j >= 3:
                    pool.wait_ge(*after(f"{nm} prod{j - 2}"))
                if j >= 2:
                    pool.wait_ge(*after(f"{nm} t{j - 1}"))
                g.tensor_tensor(chunks(mx[:, TJ[j % 2], :])[:, :, j:LC], prev[:, :, j:LC], ax[:, :, 1:LC + 1 - j],
                                ALU.mult).then_inc(*step("pool", f"{nm} t{j}"))
            t_next(1)
            t_next(2)
            for n in range(1, 4 * len(L["heads"]), 2):
                la_spread(pool, g, nm, n, "pool")
            for j in range(1, LC):
                if 2 < j + 1 < LC:
                    t_next(j + 1)
                if len(L["v"]) == 2:
                    la_add(pool, g, nm, j, 1, "pool")

        def act_la(act, nm, ready, unit=None):
            L = LA[nm]
            for r in ready:
                act.wait_ge(*after(r))
            a.activation(am[:, 0:T], L["a"], ACT.Copy).then_inc(*step("act", f"{nm} am copy"))
            for vi in range(len(L["v"])):
                a.activation(mx[:, VT + vi, :], full(act, f"{nm} v{vi}"), ACT.Copy).then_inc(
                    *step("act", f"{nm} v{vi} taken"))
            a.activation(mx[:, KOT, :], full(act, f"{nm} ko"), ACT.Copy).then_inc(*step("act", f"{nm} ko taken"))
            act.wait_ge(*after(f"{nm} prefix"))
            act.wait_ge(*after(f"{nm} ax zeros"))
            A3 = AXw.rearrange("p (d c) -> p d c", c=NL)
            a.activation(A3[:, :, 1:NL], chunks(mx[:, PP, :])[:, 1:NL, LC - 1].unsqueeze(1).to_broadcast([P, DH, NL - 1]),
                         ACT.Copy).then_inc(*step("act", f"{nm} chunk decays"))
            n = 0
            for h, (row, vi, r0) in enumerate(L["heads"]):
                rows = slice(row, row + L["dk"])
                dst = KVw.rearrange("p (d c) -> p c d", c=NL)
                for t in range(TT):
                    bank = full(act, f"{nm} kv{n}").rearrange("p (c d) -> p c d", d=DH)
                    a.activation(dst[rows, 8 * t:8 * t + 8, :], bank[rows, :, :], ACT.Copy).then_inc(
                        *step("act", f"{nm} kv{n} taken"))
                    n += 1
            act.wait_ge(*after(f"{nm} q_in"))
            for h in range(len(L["heads"])):
                a.activation(mx[:, QZ + h, :], mx[:, QI, :], ACT.Copy, scale=C(L["mask"])[:, h:h + 1]).then_inc(
                    *step("act", f"{nm} qz{h}"))
            if unit:
                for n in range(3):
                    unit(n)

        def pe_la(pe, nm, vready, unit=None):
            L = LA[nm]
            n_heads = len(L["heads"])
            for vi, x in enumerate(L["v"]):
                pe_transpose(pe, f"{nm} v{vi}", x, vready[vi])
            pe_transpose(pe, f"{nm} ko", mx[:, KO, :], f"{nm} k_out")
            n = 0
            for h in range(n_heads):
                for t in range(TT):
                    out = pe_ring(pe, f"{nm} kv{n}")
                    pe.wait_ge(*after(f"{nm} spread{n}"))
                    pe.wait_ge(*after(f"{nm} ko taken"))
                    t_.matmul(out, mx[:, KOT, t * P:(t + 1) * P], mx[:, VX + n % 2, :], start=True,
                              stop=True).then_inc(*step("pe", f"{nm} kv{n} full"))
                    n += 1
            for j in range(LC):
                pe.wait_ge(*after(f"{nm} prod{j}"))
                n = NL * (LC - j)
                for vi, red in enumerate(L["red"]):
                    out = pe_ring(pe, f"{nm} intra{j} {vi}")
                    t_.matmul(out[:, 0:n], C(red), mx[:, PROD[j % 2], 0:n], start=True,
                              stop=True).then_inc(*step("pe", f"{nm} intra{j} {vi} full"))
                if unit and j < 12:
                    pe_in(pe, unit + j // 4, (2 * (j % 4), 2 * (j % 4) + 2))
            S3 = KVw.rearrange("p (d c) -> p d c", c=NL)
            qz = mx[:, QZ:QZ + n_heads, :]
            pe.wait_ge(*after(f"{nm} states"))
            pe.wait_ge(*after(f"{nm} qz{n_heads - 1}"))
            for gr in range(NL // GROUP):
                out = pe_ring(pe, f"{nm} inter{gr}")
                for c in range(max(GROUP * gr, 1), GROUP * (gr + 1)):
                    at = (c - GROUP * gr) * n_heads * LC
                    last = t_.matmul(out[0:DH, at:at + n_heads * LC].rearrange("p (h t) -> p h t", h=n_heads),
                                     S3[:, :, c - 1], qz[:, :, LC * c:LC * c + LC], start=True, stop=True)
                last.then_inc(*step("pe", f"{nm} inter{gr} full"))

        def dve_la(dve, nm, unit=None):
            L = LA[nm]
            n_heads, nv = len(L["heads"]), len(L["v"])
            dve.wait_ge(*after(f"{nm} scan inputs"))
            v.tensor_tensor_scan(mx[:, SF, ::-1], am[:, 1:T + 1][:, ::-1], lastone[:, ::-1], 0.0, ALU.mult,
                                 ALU.add).then_inc(*step("dve", f"{nm} suffix"))
            v.tensor_tensor_scan(mx[:, PP, :], am[:, 0:T], mx[:, VX, :], 0.0, ALU.mult,
                                 ALU.add).then_inc(*step("dve", f"{nm} prefix"))
            dve.wait_ge(*after(f"{nm} suffix"))
            v.tensor_tensor(mx[:, KO, :], L["k"], mx[:, SF, :], ALU.mult).then_inc(*step("dve", f"{nm} k_out"))
            dve.wait_ge(*after(f"{nm} prefix"))
            v.tensor_tensor(mx[:, QI, :], L["q"], mx[:, PP, :], ALU.mult).then_inc(*step("dve", f"{nm} q_in"))
            for n in range(0, 4 * n_heads, 2):
                la_spread(dve, v, nm, n, "dve")
            for j in range(LC + 2):
                if j == 3:
                    dve.wait_ge(*after(f"{nm} chunk decays"))
                    dve.wait_ge(*after(f"{nm} kv{4 * n_heads - 1} taken"))
                    v.tensor_tensor_scan(KVw, AXw, KVw, 0.0, ALU.mult, ALU.add).then_inc(*step("dve", f"{nm} states"))
                if j < LC:
                    n = LC - j
                    if j:
                        dve.wait_ge(*after(f"{nm} t{j}"))
                    if j >= 2:
                        dve.wait_ge(*after(f"{nm} intra{j - 2} {nv - 1} full"))
                    tj = chunks(L["q"] if j == 0 else mx[:, TJ[j % 2], :])
                    v.tensor_tensor(mx[:, PROD[j % 2], 0:NL * n].rearrange("p (n c) -> p n c", c=n), tj[:, :, j:LC],
                                    chunks(L["k"])[:, :, 0:n], ALU.mult).then_inc(*step("dve", f"{nm} prod{j}"))
                if j >= 3:
                    la_add(dve, v, nm, j - 2, 0, "dve")
                if 0 < j <= LC:
                    jj, n = j - 1, LC - j + 1
                    for vi in range(nv):
                        bank = full(dve, f"{nm} intra{jj} {vi}")[:, 0:NL * n].rearrange("p (n c) -> p n c", c=n)
                        if jj == 0:
                            dst = chunks(L["o"][vi])
                        else:
                            m = (jj - 1) * nv + vi
                            if m >= 4:
                                jb, vb_ = divmod(m - 4, nv)
                                dve.wait_ge(*after(f"{nm} o{jb + 1} {vb_}"))
                            dst = mx[:, TMP[m % 4], 0:NL * n].rearrange("p (n c) -> p n c", c=n)
                        v.tensor_tensor(dst, bank, chunks(L["v"][vi])[:, :, 0:n],
                                        ALU.mult).then_inc(*step("dve", f"{nm} intra{jj} {vi} taken"))
                if unit and j in (5, 9, 13):
                    unit((j - 5) // 4)
            for vi in range(nv):
                dve.wait_ge(*after(f"{nm} o{LC - 1} {vi}"))
            for gr in range(NL // GROUP):
                bank = full(dve, f"{nm} inter{gr}")[0:DH, 0:GROUP * n_heads * LC]
                bank = bank.rearrange("p (c h t) -> p c h t", c=GROUP, h=n_heads)
                first = int(gr == 0)
                for h, (_, vi, r0) in enumerate(L["heads"]):
                    o = chunks(L["o"][vi][r0:r0 + DH, :])[:, GROUP * gr + first:GROUP * (gr + 1), :]
                    last = h == n_heads - 1
                    v.tensor_tensor(o, o, bank[:, first:, h, :], ALU.add).then_inc(
                        *step("dve", f"{nm} inter{gr} taken" if last else f"{nm} inter{gr} {h}"))

        def act_la_out(act, nm, outs):
            act_head_norm(act, f"{nm} out", [o for o, _, _ in outs], [r for _, r, _ in outs], 1.0 / DH)

        def dve_la_out(dve, nm, gain, outs):
            dve_head_norm(dve, f"{nm} out", [o for o, _, _ in outs], [par(gain)] * len(outs))
            for i, (o, _, m) in enumerate(outs):
                dve.wait_ge(*after(f"{nm} out {i}"))
                v.tensor_tensor(mixT[:, m, :], mixT[:, m, :], o, ALU.mult).then_inc(*step("dve", f"mix{m}"))

        GLA_OUT = [(mx[:, O_ + i, :], "gla inter3 taken", 6 + i) for i in range(2)]
        HG_OUT = [(mx[:, O_ + i, :], f"hg{i} inter3 taken", 4 + i) for i in range(2)]

        def pe_gla_gate(pe):
            out = pe_ring(pe, "gla gate")
            pe.wait_ge(small_loaded, 16 * N_SMALL)
            pe.wait_ge(*after("in0 taken"))
            t_.matmul(out, wgk[:, :], graw[:, :], start=True, stop=True).then_inc(*step("pe", "gla gate full"))

        def act_gla_gate(act):
            z, e = mx[:, 1, :], mx[:, 2, :]
            act.wait_ge(*after("gdn o7 full"))
            a.activation(z, full(act, "gla gate"), ACT.Identity, bias=par("gla_b_gk")).then_inc(
                *step("act", "gla gate taken"))
            act.wait_ge(*after("gla gate taken"))
            act.wait_ge(*after("mix3"))
            a.activation(e, z, ACT.Abs).then_inc(*step("act", "gla abs"))
            act.wait_ge(*after("gla abs"))
            a.activation(e, e, ACT.Exp, scale=-1.0).then_inc(*step("act", "gla exp"))
            act.wait_ge(*after("gla exp"))
            a.activation(e, e, ACT.Ln, bias=1.0).then_inc(*step("act", "gla ln"))
            act.wait_ge(*after("gla log sigmoid"))
            a.activation(mx[:, A0, :], z, ACT.Exp, scale=1.0 / 16).then_inc(*step("act", "gla decay"))

        def dve_gla_gate(dve):
            dve.wait_ge(*after("gla ln"))
            v.scalar_tensor_tensor(mx[:, 1, :], mx[:, 1, :], 0.0, mx[:, 2, :], ALU.min,
                                   ALU.subtract).then_inc(*step("dve", "gla log sigmoid"))

        def act_hg_unit(act, n):
            u, p = 15 + n, n % 2
            if n // 2 != 1:
                dst = {0: xT[:, p, :], 2: xT[:, 6 + p, :], 3: mixT[:, 4 + p, :]}[n // 2]
                act_copy_in(act, u, dst)
                split_hi(act, u + 2)
                if n // 2 != 2:
                    act_silu(act, f"hg {u}", dst, f"in{u} taken")
                return
            act.wait_ge(unit_used, u + 1)
            forget, into = xT[:, 2 + p, :], xT[:, 4 + p, :]
            for x, sign, name in ((forget, -1.0, f"hg exp(-f) {p}"), (into, 1.0, f"in{u} taken")):
                a.activation(x, acc(u), ACT.Exp, scale=sign).then_inc(*step("act", name))
            split_hi(act, u + 2)
            for x, name in ((forget, "a"), (into, "k")):
                act.wait_ge(*after(f"in{u} taken"))
                a.activation(x, x, ACT.Ln, bias=1.0).then_inc(*step("act", f"hg ln {name}{p}"))
                act.wait_ge(*after(f"hg ln {name}{p}"))
                a.activation(x, x, ACT.Exp, scale=-1.0).then_inc(*step("act", f"hg {name}{p}"))

        def dve_hg_unit(dve, n):
            u, p = 15 + n, n % 2
            split_lo(dve, u + 2)
            if n // 2 == 0:
                dve_silu(dve, f"hg {u}", xT[:, p, :], 0.125)
            elif n // 2 == 3:
                dve_silu(dve, f"hg {u}", mixT[:, 4 + p, :])

        PB = {}
        LAG = 2

        def attn_pe(pe, tag, heads, logits, values, PT, ready):
            n_all = heads * TT
            for n in range(n_all + LAG + 1):
                if n < n_all:
                    h, i = divmod(n, TT)
                    out = pe_ring(pe, f"{tag} L{n}")
                    if i == 0:
                        ready(pe, h)
                    logits(out[:, 0:P * (i + 1)], h, i).then_inc(*step("pe", f"{tag} L{n} full"))
                m = n - LAG
                if 0 <= m < n_all:
                    i = m % TT
                    out = pe_ring(pe, f"{tag} T{m}")
                    pe.wait_ge(*after(f"{tag} P{m}"))
                    for k in range(i + 1):
                        last = t_.transpose(out[:, k * P:(k + 1) * P], PB[tag][:, m % 3, k * P:(k + 1) * P],
                                            C("ident"))
                    last.then_inc(*step("pe", f"{tag} T{m} full"))
                m -= 1
                if 0 <= m and m % TT == TT - 1:
                    h = m // TT
                    out = pe_ring(pe, f"{tag} O{h}")
                    pe.wait_ge(*after(f"{tag} T{m} taken"))
                    for k in range(TT):
                        last = t_.matmul(out[:, k * P:T], values(k, h), PT[:, h % 2, k, k * P:T], start=k == 0,
                                         stop=k == TT - 1)
                    last.then_inc(*step("pe", f"{tag} O{h} full"))

        def attn_act(act, tag, heads, PT, each=None, start=None):
            n_all = heads * TT
            for n in range(n_all + LAG):
                if n < n_all:
                    i = n % TT
                    W = P * (i + 1)
                    if start and i == 0:
                        start(n // TT)
                    act.wait_ge(*after(f"{tag} max{n}"))
                    if n >= 3:
                        act.wait_ge(*after(f"{tag} T{n - 3} full"))
                    a.activation(PB[tag][:, n % 3, 0:W], full(act, f"{tag} L{n}")[:, 0:W], ACT.Exp,
                                 bias=stat[:, n % 4, 0:1],
                                 accum_out=stat[:, n % 4, 1:2]).then_inc(*step("act", f"{tag} L{n} taken"))
                m = n - LAG
                if m >= 0:
                    h, i = divmod(m, TT)
                    W = P * (i + 1)
                    bank = full(act, f"{tag} T{m}")
                    if h >= 2 and i == 0:
                        act.wait_ge(*after(f"{tag} O{h - 2} full"))
                    a.activation(PT[:, h % 2, 0:i + 1, i * P:(i + 1) * P],
                                 bank[:, 0:W].rearrange("p (k q) -> p k q", q=P),
                                 ACT.Copy).then_inc(*step("act", f"{tag} T{m} taken"))
                    if each and i == 1 and h:
                        each(h - 1)
            if each:
                each(heads - 1)

        def attn_dve(dve, tag, heads, each):
            n_all = heads * TT
            for n in range(n_all + 1):
                if n < n_all:
                    i = n % TT
                    bank = full(dve, f"{tag} L{n}")
                    diag = bank[:, i * P:(i + 1) * P]
                    v.tensor_tensor(diag, diag, C("neg"), ALU.add).then_inc(*step("dve", f"{tag} masked{n}"))
                    dve.wait_ge(*after(f"{tag} masked{n}"))
                    v.tensor_reduce(stat[:, n % 4, 0:1], bank[:, 0:P * (i + 1)], AX.X, ALU.max,
                                    negate=True).then_inc(*step("dve", f"{tag} max{n}"))
                if n:
                    m = n - 1
                    W = P * (m % TT + 1)
                    dve.wait_ge(*after(f"{tag} L{m} taken"))
                    v.reciprocal(stat[:, m % 4, 2:3], stat[:, m % 4, 1:2]).then_inc(*step("dve", f"{tag} 1/sum{m}"))
                    dve.wait_ge(*after(f"{tag} 1/sum{m}"))
                    pm = PB[tag][:, m % 3, 0:W]
                    v.tensor_scalar(pm, pm, stat[:, m % 4, 2:3], None, ALU.mult).then_inc(*step("dve", f"{tag} P{m}"))
                    if m % TT == LAG and m > TT:
                        each(m // TT - 1)
            each(heads - 1)

        FZ, FVT, FO = 0, 4, 8
        FOX_IN = [mx[:, 6, :], mx[:, 7, :], mx[:, 12, :], mx[:, 13, :], mixT[:, 0, :], mixT[:, 1, :]]
        PB["fox"] = mx[:, 14:17, :]
        fox_PT = wtile(17, 8).rearrange("p (b k t) -> p b k t", b=2, t=T)
        FOX_QK = FOX_IN[0:4]
        FOX_O = [mx[:, FO + p, :] for p in range(2)]
        X_AGAIN = ((0, 1, 2), (3, 4, 5), (6, 7))

        def act_fox_unit(act, n):
            act_copy_in(act, 23 + n, FOX_IN[n])
            split_hi(act, 25 + n)

        def pe_fox(pe):
            pe_head_norm(pe, "fox qk", 4)
            for p in range(2):
                pe_transpose(pe, f"fox v{p}", FOX_IN[4 + p], f"in{27 + p} taken")

            def ready(pe, h):
                pe.wait_ge(*after(f"fox kz{h}"))
                pe.wait_ge(*after(f"fox v{h // 2} taken"))
                if h:
                    pe_x_again(pe, X_AGAIN[h - 1])

            def logits(out, h, i):
                W = P * (i + 1)
                t_.matmul(out, FOX_QK[h // 2][:, i * P:(i + 1) * P], mx[:, FZ + h, 0:W], start=True, stop=False)
                return t_.matmul(out, C(f"foxrow{h}"), grow[:, 0:W], start=False, stop=True)

            attn_pe(pe, "fox", 4, logits, lambda k, h: mx[:, FVT + h // 2, k * P:(k + 1) * P], fox_PT, ready)
            pe_head_norm(pe, "fox out", 2)

        def act_fox(act):
            act_load_again(act)
            act_head_norm(act, "fox qk", FOX_QK, [f"in{23 + i} taken" for i in range(4)], 1.0 / DH)
            for p in range(2):
                a.activation(mx[:, FVT + p, :], full(act, f"fox v{p}"), ACT.Copy).then_inc(
                    *step("act", f"fox v{p} taken"))
            attn_act(act, "fox", 4, fox_PT, start=lambda h: act_x_again(act, X_AGAIN[h - 1]) if h else None)
            act_head_norm(act, "fox out", FOX_O, ["fox O1 taken", "fox O3 taken"], 1.0 / DH)

        def dve_fox(dve):
            v.tensor_scalar(gbias[:, 3:4], par("fox_qn_g"), 0.125, None, ALU.mult).then_inc(*step("dve", "fox q gain"))
            dve.wait_ge(*after("fox q gain"))
            dve_head_norm(dve, "fox qk", FOX_QK, [gbias[:, 3:4]] * 2 + [par("fox_kn_g")] * 2)

            def out(h):
                rows = slice(64 * (h % 2), 64 * (h % 2) + 64)
                v.tensor_copy(FOX_O[h // 2][rows, :], full(dve, f"fox O{h}")[rows, :]).then_inc(
                    *step("dve", f"fox O{h} taken"))
            attn_dve(dve, "fox", 4, out)
            for i in range(2):
                dve.wait_ge(*after(f"fox out rs{i}"))
                v.scalar_tensor_tensor(mixT[:, i, :], FOX_O[i], par("fox_on_g"), hr[i], ALU.mult,
                                       ALU.mult).then_inc(*step("dve", f"mix{i}"))

        def pool_fox(pool):
            for h in range(4):
                pool.wait_ge(*after(f"fox qk {2 + h // 2}"))
                g.tensor_scalar(mx[:, FZ + h, :], FOX_QK[2 + h // 2], C("hmask")[:, h % 2:h % 2 + 1], None,
                                ALU.mult).then_inc(*step("pool", f"fox kz{h}"))

        MIX_ORDER = (2, 3, 6, 7, 4, 5, 0, 1)

        def act_mix(act):
            act.wait_ge(unit_used, FIRST["w_out"])
            for m in MIX_ORDER:
                act.wait_ge(*after(f"mix{m}"))
                a.activation(xhi[:, m, :], mixT[:, m, :], ACT.Copy).then_inc(*step("act", f"mix hi{m}"))

        def dve_mix(dve):
            for m in MIX_ORDER:
                dve.wait_ge(*after(f"mix hi{m}"))
                v.tensor_tensor(xlo[:, m, :], mixT[:, m, :], f32(xhi[:, m, :]),
                                ALU.subtract).then_inc(*step("dve", f"mix lo{m}"))

        mixers.close()
        ffn = ctx.enter_context(ExitStack())
        h_hi = sb("h_hi", [P, FT, T], F32R, ffn)
        h_lo = sb("h_lo", [P, FT, T], F32R, ffn)
        zS, yg, yu = (sb(n, [P, 2, T], F32, ffn) for n in ("zS", "yg", "yu"))
        ffn.close()
        conv = ctx.enter_context(ExitStack())
        c_hi = sb("c_hi", [P, KT, T], F32R, conv)
        c_lo = sb("c_lo", [P, KT, T], F32R, conv)
        bS, cS, vS, yS = (sb(n, [P, 2, T], F32, conv) for n in ("bS", "cS", "vS", "yS"))
        r2 = sb("r2", [P, T], c=conv)
        conv.close()
        mla = ctx.enter_context(ExitStack())
        kn = sb("kn", [P, NH2, T], c=mla)
        qn = sb("qn", [P, NH2, T], c=mla)
        qp = sb("qp", [P, NH2 // 2, T], c=mla)
        kpz = sb("kpz", [P, 2, T], c=mla)
        vtok = sb("vtok", [P, TT, D], c=mla)
        rot = sb("rot", [P, 2, T], c=mla)
        latent = ctx.enter_context(ExitStack())
        lhi, llo = (sb(n, [P, 2, T], F32R, latent) for n in ("lhi", "llo"))
        chi, clo = (sb(n, [P, 3, T], F32R, latent) for n in ("chi", "clo"))
        lat = sb("lat", [P, 3, T], c=latent)
        kraw = sb("kraw", [P, T], c=latent)
        rl = sb("rl", [P, T], c=latent)
        ang = sb("ang", [P, 2, T], c=latent)
        turns = sb("turns", [P, T], I32, latent)
        latent.close()
        attn = ctx.enter_context(ExitStack())
        PB["mla"] = sb("mla_P", [P, 3, T], c=attn)
        mla_PT = sb("mla_PT", [P, 2, TT, T], c=attn)
        attn.close()
        mla.close()
        ffn3 = ctx.enter_context(ExitStack())
        h3_hi = sb("h3_hi", [P, FT, T], F32R, ffn3)
        h3_lo = sb("h3_lo", [P, FT, T], F32R, ffn3)
        zS3, yg3 = (sb(n, [P, 2, T], F32, ffn3) for n in ("zS3", "yg3"))
        ffn3.close()
        fin = sb("fin", [P, KT, T])

        MLA_TILES = [f"dkv{i}" for i in range(3)] + [f"dq{i}" for i in range(3)] + [f"kn{h}" for h in range(NH2)]
        MLA_TILES += [f"v{g}{t}" for g in range(2) for t in range(TT)]
        for _g in range(2):
            MLA_TILES += [f"qn{4 * _g + h}" for h in range(4)] + [f"qp{2 * _g + p}" for p in range(2)]
        tile_no = {n: i for i, n in enumerate(MLA_TILES)}

        def mla_acc(name):
            return acc(tile_no[name])

        def pe_mla_wait(pe, name):
            if tile_no[name] >= 2:
                pe.wait_ge(*after(f"{MLA_TILES[tile_no[name] - 2]} taken"))

        def pe_latent_sum(pe, name, n):
            out = pe_ring(pe, f"{name} sum")
            for k in range(n):
                pe.wait_ge(*after(f"{name} square{k}"))
                t_.matmul(out, C("ones"), sq[:, k % 2, :], start=k == 0, stop=k == n - 1).then_inc(
                    *step("pe", f"{name} sum full" if k == n - 1 else f"{name} add{k}"))

        def act_latent(act, name, n, hi):
            for k in range(n):
                if k >= 2:
                    act.wait_ge(*after(f"{name} add{k - 2}"))
                act.wait_ge(*after(f"{('dkv', 'dq')[name == 'cq']}{k} taken"))
                a.activation(sq[:, k % 2, :], lat[:, k, :], ACT.Square).then_inc(*step("act", f"{name} square{k}"))
            act_rstd(act, name, n * P, rl[:, :])
            act_hi(act, name, n, hi)

        def pe_mla(pe):
            u = FIRST["dkv"]
            for i in range(3):
                pe_mla_wait(pe, f"dkv{i}")
                product(pe, u + i, tile_no[f"dkv{i}"], ready=parts_of("kv_norm_g_2") if i == 0 else None)
                if i == 0:
                    pe_sum(pe, "mla norm", NORM0["ffn2_down"])
            pe_latent_sum(pe, "lat", 2)
            u = FIRST["dq"]
            for i in range(3):
                pe_mla_wait(pe, f"dq{i}")
                product(pe, u + i, tile_no[f"dq{i}"], ready=parts_of("mla_norm_g_2") if i == 0 else None)
            out = pe_ring(pe, "k swapped")
            pe.wait_ge(*after("dkv2 taken"))
            t_.matmul(out, C("perm"), kraw[:, :], start=True, stop=True).then_inc(*step("pe", "k swapped full"))
            u = FIRST["ukv"]
            for h in range(NH2):
                pe_mla_wait(pe, f"kn{h}")
                product(pe, u + h // 4, tile_no[f"kn{h}"], x=(lhi, llo), ready=(lambda pe, k: pe.wait_ge(*after(f"lat lo{k}"))) if h == 0 else None,
                        cols=P * (h % 4), full=f"kn{h} full" if h % 4 < 3 else None)
            for gr in range(2):
                pe.wait_ge(lo_split, u + 2 + gr + 1)
                wh, wl = (unit_view(b, u + 2 + gr) for b in (whi, wlo))
                for t in range(TT):
                    pe_mla_wait(pe, f"v{gr}{t}")
                    blk = slice(t * P, (t + 1) * P)
                    for k in range(2):
                        last = passes(mla_acc(f"v{gr}{t}"), lhi[:, k, blk], llo[:, k, blk], wh[:, k, :], wl[:, k, :],
                                      k == 0, k == 1)
                    last.then_inc(*(step("pe", f"v{gr}{t} full") if t < TT - 1 else (unit_used, 1)))
            pe_latent_sum(pe, "cq", 3)
            u = FIRST["uq"]
            for gr in range(2):
                for p in range(2):
                    for hh in range(2):
                        name = f"qn{4 * gr + 2 * p + hh}"
                        pe_mla_wait(pe, name)
                        product(pe, u + 3 * gr + p, tile_no[name], x=(chi, clo), ready=(lambda pe, k: pe.wait_ge(*after(f"cq lo{k}"))) if name == "qn0" else None,
                                cols=P * hh, full=f"{name} full" if hh == 0 else None)
                for p in range(2):
                    name = f"qp{2 * gr + p}"
                    pe_mla_wait(pe, name)
                    product(pe, u + 3 * gr + 2, tile_no[name], x=(chi, clo), cols=P * p, full=f"{name} full" if p == 0 else None)
                for p in range(2):
                    i = 2 * gr + p
                    out = pe_ring(pe, f"q swapped{i}")
                    pe.wait_ge(*after(f"qp{i} taken"))
                    t_.matmul(out, C("perm"), qp[:, i, :], start=True, stop=True).then_inc(
                        *step("pe", f"q swapped{i} full"))

            def ready(pe, h):
                if h == 0:
                    pe.wait_ge(*after("kpz1"))
                    pe.wait_ge(*after("kpz0"))
                    pe.wait_ge(*after(f"kn{NH2 - 1} taken"))
                    pe.wait_ge(*after("v13 taken"))
                pe.wait_ge(*after(f"qn{h} taken"))
                pe.wait_ge(*after(f"rotated{h // 2}"))

            def logits(out, h, i):
                blk = slice(i * P, (i + 1) * P)
                W = P * (i + 1)
                t_.matmul(out, qn[:, h, blk], kn[:, h, 0:W], start=True, stop=False)
                return t_.matmul(out, qp[:, h // 2, blk], kpz[:, h % 2, 0:W], start=False, stop=True)

            attn_pe(pe, "mla", NH2, logits, lambda k, h: vtok[:, k, h * P:(h + 1) * P], mla_PT, ready)

        QSCALE = float((128 + 64) ** -0.5)

        def act_mla(act):
            act_rstd(act, "mla norm", D, rs[:, :])
            act_positions(act)
            u = FIRST["dkv"]
            for i in range(3):
                split_hi(act, u + i + 2)
            act_gain_all(act, "mla_norm_g_2", FIRST["dq"])
            act_latent(act, "lat", 2, lhi)
            u = FIRST["dq"]
            for i in range(3):
                split_hi(act, u + i + 2)
            u = FIRST["ukv"]
            for h in range(NH2):
                act.wait_ge(*after(f"kn{h} full") if h % 4 < 3 else (unit_used, u + h // 4 + 1))
                a.activation(kn[:, h, :], mla_acc(f"kn{h}"), ACT.Copy).then_inc(*step("act", f"kn{h} taken"))
                if h % 4 == 3:
                    split_hi(act, u + h // 4 + 2)
            for n in ("sin", "cos"):
                act.wait_ge(*after(f"{n} reduced"))
                a.activation(rot[:, n == "sin", :], ang[:, n == "cos", :], ACT.Sin).then_inc(*step("act", n))
            for gr in range(2):
                split_hi(act, u + 2 + gr + 2)
            act_latent(act, "cq", 3, chi)
            u = FIRST["uq"]
            for gr in range(2):
                for p in range(2):
                    for hh in range(2):
                        h = 4 * gr + 2 * p + hh
                        act.wait_ge(*after(f"qn{h} full") if hh == 0 else (unit_used, u + 3 * gr + p + 1))
                        a.activation(qn[:, h, :], mla_acc(f"qn{h}"), ACT.Copy, scale=QSCALE).then_inc(
                            *step("act", f"qn{h} taken"))
                    split_hi(act, u + 3 * gr + p + 2)
                for p in range(2):
                    i = 2 * gr + p
                    act.wait_ge(*after(f"qp{i} full") if p == 0 else (unit_used, u + 3 * gr + 3))
                    a.activation(qp[:, i, :], mla_acc(f"qp{i}"), ACT.Copy, scale=QSCALE).then_inc(
                        *step("act", f"qp{i} taken"))
                split_hi(act, u + 3 * gr + 4)

            def each(h):
                a.activation(xhi[:, h, :], full(act, f"mla O{h}"), ACT.Copy).then_inc(*step("act", f"mla hi{h}"))
            attn_act(act, "mla", NH2, mla_PT, each)

        def pool_mla(pool):
            pool.wait_ge(x_lo, XPART0["mla_norm_g_2"])
            g.memset(kpz[:, :, :], 0.0).then_inc(*step("pool", "kpz zeros"))

        def act_positions(act):
            act.dma_start(turns[:, :], A["positions_2"][0].partition_broadcast(P)).then_inc(pos_loaded, 16)

        TWO_PI = 2 * np.pi
        TURN = [6.28125, 0.0019350051879882812, float(TWO_PI - 6.28125 - 0.0019350051879882812)]

        def dve_angles(dve):
            n = [0]

            def did(ins, name=None):
                n[0] += 1
                name = name or f"angle{n[0]}"
                ins.then_inc(*step("dve", name))
                dve.wait_ge(*after(name))

            s, c, w = ang[:, 0, :], ang[:, 1, :], rl[:, :]
            dve.wait_ge(pos_loaded, 16)
            dve.wait_ge(*after("lat lo1"))
            did(v.tensor_copy(s, turns[:, :]))
            did(v.tensor_scalar(s, s, C("freq"), None, ALU.mult))
            did(v.tensor_scalar(turns[:, :], s, float(1 / TWO_PI), None, ALU.mult))
            did(v.tensor_copy(w, turns[:, :]))
            for part in TURN:
                did(v.scalar_tensor_tensor(s, w, -part, s, ALU.mult, ALU.add))

            def wrap(x):
                for side, op in ((1.0, ALU.is_gt), (-1.0, ALU.is_lt)):
                    did(v.tensor_scalar(w, x, side * float(np.pi), -side * float(TWO_PI), op, ALU.mult))
                    did(v.tensor_tensor(x, x, w, ALU.add))

            wrap(s)
            did(v.tensor_scalar(c, s, float(np.pi / 2), None, ALU.add))
            wrap(c)
            for x, name in ((s, "sin"), (c, "cos")):
                did(v.tensor_scalar(x, x, 3.1415925, -3.1415925, ALU.min, ALU.max), f"{name} reduced")

        def dve_rotate(dve, key, x, name, before):
            w = xg[:, 0, :]
            dve.wait_ge(*after(before))
            v.tensor_tensor(w, full(dve, key), rot[:, 1, :], ALU.mult).then_inc(*step("dve", f"{key} taken"))
            v.tensor_tensor(x, x, rot[:, 0, :], ALU.mult).then_inc(*step("dve", f"{name} cos"))
            dve.wait_ge(*after(f"{name} cos"))
            v.tensor_tensor(x, x, w, ALU.add).then_inc(*step("dve", name))

        def dve_mla(dve):
            dve.wait_ge(*after("mla norm rstd"))
            u = FIRST["dkv"]
            for i in range(3):
                dve.wait_ge(unit_used, u + i + 1)
                v.tensor_tensor(lat[:, i, :] if i < 2 else kraw[:, :], mla_acc(f"dkv{i}"), rs[:, :], ALU.mult).then_inc(
                    *step("dve", f"dkv{i} taken"))
                split_lo(dve, u + i + 2)
            dve_gain_all(dve, "mla_norm_g_2")
            dve_scale(dve, "lat", 2, lat, "kv_latent_norm_g_2", lhi, llo, "lat rstd", rl[:, :])
            u = FIRST["dq"]
            for i in range(3):
                dve.wait_ge(unit_used, u + i + 1)
                if i == 0:
                    dve.wait_ge(*after("lat lo1"))
                v.tensor_tensor(lat[:, i, :], mla_acc(f"dq{i}"), rs[:, :], ALU.mult).then_inc(
                    *step("dve", f"dq{i} taken"))
                split_lo(dve, u + i + 2)
            dve_angles(dve)
            u = FIRST["ukv"]
            for i in range(2):
                split_lo(dve, u + i + 2)
            dve.wait_ge(*after("cos"))
            s = rot[:, 1, :]
            v.tensor_scalar(s, s, C("sign"), None, ALU.mult).then_inc(*step("dve", "signed sin"))
            dve.wait_ge(*after("signed sin"))
            dve_rotate(dve, "k swapped", kraw[:, :], "k rotated", "lat lo1")
            dve.wait_ge(*after("k rotated"))
            dve.wait_ge(*after("kpz zeros"))
            for half in range(2):
                v.tensor_copy(kpz[64 * half:64 * half + 64, half, :], kraw[64:P, :]).then_inc(
                    *step("dve", f"kpz{half}"))
            for gr in range(2):
                for t in range(TT):
                    dve.wait_ge(*after(f"v{gr}{t} full") if t < TT - 1 else (unit_used, u + 2 + gr + 1))
                    v.tensor_copy(vtok[:, t, 4 * P * gr:4 * P * (gr + 1)], mla_acc(f"v{gr}{t}")).then_inc(
                        *step("dve", f"v{gr}{t} taken"))
                split_lo(dve, u + 2 + gr + 2)
            dve_scale(dve, "cq", 3, lat, "mla_q_norm_g_2", chi, clo, "cq rstd", rl[:, :], "k rotated")
            u = FIRST["uq"]
            for gr in range(2):
                for p in range(3):
                    split_lo(dve, u + 3 * gr + p + 2)
                for p in range(2):
                    i = 2 * gr + p
                    dve_rotate(dve, f"q swapped{i}", qp[:, i, :], f"rotated{i}", f"rotated{i - 1}" if i else "cq lo2")

            def each(h):
                dve.wait_ge(*after(f"mla hi{h}"))
                v.tensor_tensor(xlo[:, h, :], full(dve, f"mla O{h}"), f32(xhi[:, h, :]),
                                ALU.subtract).then_inc(*step("dve", f"mla O{h} taken"))
            attn_dve(dve, "mla", NH2, each)

        def pe_final(pe):
            pe_sum(pe, "final norm", NORM0["ffn3_down"])
            for k in range(KT):
                pe.wait_ge(*after(f"final{k}"))
                out = pe_ring(pe, f"final{k}")
                for t in range(TT):
                    last = t_.transpose(out[:, t * P:(t + 1) * P], xg[:, k % 2, t * P:(t + 1) * P], C("ident"))
                last.then_inc(*step("pe", f"final{k} full"))

        def act_final(act):
            act_rstd(act, "final norm", D, rs[:, :])
            for k in range(KT):
                a.activation(fin[:, k, :], full(act, f"final{k}"), ACT.Copy).then_inc(*step("act", f"final{k} taken"))

        def dve_final(dve):
            dve.wait_ge(*after("final norm rstd"))
            for k in range(KT):
                if k >= 2:
                    dve.wait_ge(*after(f"final{k - 2} full"))
                v.scalar_tensor_tensor(xg[:, k % 2, :], xT[:, k, :], par("final_norm_g_2", k), rs[:, :], ALU.mult,
                                       ALU.mult).then_inc(*step("dve", f"final{k}"))

        def sp_final(sp):
            for k in range(KT):
                sp.wait_ge(*after(f"final{k} taken"))
                dst = out_d[0, :, k * P:(k + 1) * P].rearrange("(t p) c -> p t c", p=P)
                sp.dma_start(dst, fin[:, k, :].rearrange("p (t c) -> p t c", c=P)).then_inc(stored, 16)
            sp.wait_ge(stored, 16 * KT)

        GLA_READY = ["gla decay", "mix3"]

        def hg_ready(p):
            return [f"silu{10 + p} used", f"hg a{p}", f"hg k{p}", f"in{19 + p} taken"]

        block = ctx.enter_context(nc.Block())

        @block.sync
        def _(sp):
            sp_load_inputs(sp)
            for u in range(FIRST["w_out"]):
                load_unit(sp, u)
            def up(i, j):
                return (j % 2) * FF + (j // 2) * P + 2 * P * i
            def one(i, j):
                return j * P + 4 * P * i
            def thirds(i, j):
                return (j // 3) * P + 4 * P * i
            load_loop(sp, "w_out", KT, 4, one)
            load_loop(sp, "ffn1_up", 2 * FT, 4, up)
            load_loop(sp, "ffn1_down", 3 * KT, 12, thirds)
            load_loop(sp, "conv_in", 3 * KT, 12, lambda i, j: (j % 3) * D + (j // 3) * P + 4 * P * i)
            load_loop(sp, "conv_out", KT, 4, one)
            load_loop(sp, "ffn2_up", 2 * FT, 4, up)
            load_loop(sp, "ffn2_down", 3 * KT, 12, thirds)
            for u in range(FIRST["dkv"], FIRST["w_o"]):
                load_unit(sp, u)
            load_loop(sp, "w_o", KT, 4, one)
            load_loop(sp, "ffn3_up", 2 * FT, 4, up)
            load_loop(sp, "ffn3_down", 3 * KT, 12, thirds)
            sp_final(sp)

        @block.gpsimd
        def _(pool):
            pool_init(pool)
            pool_gdn(pool)
            for b in _LEVELS[1:]:
                for h in range(4):
                    pool_gdn_level(pool, b, h)
            pool_la(pool, "gla")
            for p in range(2):
                pool_la(pool, f"hg{p}", ("gla", "hg0")[p])
            pool_fox(pool)
            pool_residual(pool, "w_out", "mix1")
            pool_products(pool, "ffn1_up", FT, h_hi, h_lo)
            pool_residual(pool, "ffn1_down", "norm2 sum full")
            pool_products(pool, "conv_in", KT, c_hi, c_lo)
            pool_residual(pool, "conv_out", "conv norm sum full")
            pool_products(pool, "ffn2_up", FT, h_hi, h_lo)
            pool_residual(pool, "ffn2_down", "ffn2 norm sum full")
            pool_mla(pool)
            pool_residual(pool, "w_o", "mla norm sum full")
            pool_products(pool, "ffn3_up", FT, h3_hi, h3_lo)
            pool_residual(pool, "ffn3_down", "ffn3 norm sum full")

        @block.tensor
        def _(pe):
            pe_load(pe)
            for u in range(9):
                pe_in(pe, u)
            pe_gates(pe)
            for u in range(9, 15):
                pe_in(pe, u)
            pe_gdn_setup(pe)
            pe_gdn_triangles(pe)
            pe_gdn_inverse(pe)
            pe_gdn_operands(pe)
            pe_gdn_chunks(pe, 15)
            pe_gdn_out(pe)
            pe_gla_gate(pe)
            pe_la(pe, "gla", ["in11 taken", "in12 taken"])
            pe_head_norm(pe, "gla out", 2)
            for p in range(2):
                pe_la(pe, f"hg{p}", [f"in{19 + p} taken"], 23 + 3 * p)
            pe_head_norm(pe, "hg out", 2)
            pe_fox(pe)

            pe_residual(pe, "w_out", False, (xhi, xlo), lambda pe, k: pe.wait_ge(*after(f"mix lo{k}")), MIX_ORDER)
            pe_up(pe, "ffn1_up", "norm2", "norm2_g", "w_out")

            def products(stage):
                return lambda pe, k: pe.wait_ge(prod_lo, PAIR0[stage] + k + 3)
            pe_residual(pe, "ffn1_down", True, (h_hi, h_lo), products("ffn1_up"))
            pe_conv_in(pe)
            pe_residual(pe, "conv_out", False, (c_hi, c_lo), products("conv_in"))
            pe_up(pe, "ffn2_up", "ffn2 norm", "conv_ffn_norm_g_2", "conv_out")
            pe_residual(pe, "ffn2_down", True, (h_hi, h_lo), products("ffn2_up"))
            pe_mla(pe)
            pe_residual(pe, "w_o", False, (xhi, xlo), lambda pe, k: pe.wait_ge(*after(f"mla O{k} taken")))
            pe_up(pe, "ffn3_up", "ffn3 norm", "mla_ffn_norm_g_2", "w_o")
            pe_residual(pe, "ffn3_down", True, (h3_hi, h3_lo), products("ffn3_up"))
            pe_final(pe)

        @block.scalar
        def _(act):
            act_load_inputs(act)
            act_load(act)
            for u in range(9):
                if 1 <= u <= 6:
                    act_gdn_tap(act, u - 1)
                    if u >= 2:
                        act_silu(act, f"conv{u - 2}", mx[:, u - 2, :], f"in{u - 1} taken")
                elif u >= 7:
                    act_copy_in(act, u, mixT[:, u - 5, :])
                    if u == 7:
                        act_silu(act, "conv5", mx[:, 5, :], "in6 taken")
                    act_silu(act, f"z{u - 7}", mixT[:, u - 5, :], f"in{u} taken")
                split_hi(act, u + 2)
            act_gates(act)
            for u in range(9, 15):
                dst = (mx[:, 6, :], mx[:, 7, :], mixT[:, 0, :], mixT[:, 1, :], mixT[:, 6, :], mixT[:, 7, :])[u - 9]
                act_copy_in(act, u, dst, 32 ** -0.5 if u == 9 else 1.0)
                if u >= 13:
                    act_silu(act, f"gla g{u - 13}", dst, f"in{u} taken")
                split_hi(act, u + 2)
            act_ecol(act)
            act_gdn_setup(act)
            act_gdn_inverse(act)
            act_gdn_operands(act)
            act_gdn_chunks(act, lambda c: act_hg_unit(act, c))
            act_gdn_out(act)
            act_gla_gate(act)
            act_la(act, "gla", GLA_READY)
            act_la_out(act, "gla", GLA_OUT)
            for p in range(2):
                act_la(act, f"hg{p}", hg_ready(p), lambda n, p=p: act_fox_unit(act, 3 * p + n))
            act_la_out(act, "hg", HG_OUT)
            act_fox(act)
            act_mix(act)
            act_residual(act, "w_out", False, None)
            act_gain_all(act, "norm2_g", FIRST["ffn1_up"])
            act_rstd(act, "norm2", D, rs[:, :])
            act_up(act, "ffn1_up", True, h_hi, zS, yg, yu)
            act_residual(act, "ffn1_down", True, "conv_norm_g_2")
            act_rstd(act, "conv norm", D, rs[:, :])
            act_conv_in(act, c_hi, vS, yS)
            act_residual(act, "conv_out", False, "conv_ffn_norm_g_2")
            act_rstd(act, "ffn2 norm", D, rs[:, :])
            act_up(act, "ffn2_up", False, h_hi, zS, yg, yu)
            act_residual(act, "ffn2_down", True, "kv_norm_g_2")
            act_mla(act)
            act_residual(act, "w_o", False, None)
            act_gain_all(act, "mla_ffn_norm_g_2", FIRST["ffn3_up"])
            act_rstd(act, "ffn3 norm", D, rs[:, :])
            act_up(act, "ffn3_up", False, h3_hi, zS3, yg3, None)
            act_residual(act, "ffn3_down", True, None)
            act_final(act)

        @block.vector
        def _(dve):
            dve_load(dve)
            for u in range(9):
                if u == 0:
                    dve_gate_in(dve)
                elif u <= 6:
                    dve_gdn_conv(dve, u - 1)
                    if u >= 2:
                        dve_silu(dve, f"conv{u - 2}", mx[:, u - 2, :])
                else:
                    if u == 7:
                        dve_silu(dve, "conv5", mx[:, 5, :])
                    dve_silu(dve, f"z{u - 7}", mixT[:, u - 5, :])
                split_lo(dve, u + 2)
            dve_gates(dve)
            dve_gcol(dve)
            for u in range(9, 15):
                if u >= 13:
                    dve_silu(dve, f"gla g{u - 13}", mixT[:, u - 7, :])
                split_lo(dve, u + 2)
            dve_gdn_setup(dve)
            dve_gdn_triangles(dve)
            for h in range(4):
                dve_gdn_first(dve, h)
            dve_gdn_inverse(dve)
            dve_gdn_operands(dve)
            dve_gdn_chunks(dve, lambda c: dve_hg_unit(dve, c))
            dve_gdn_out(dve)
            dve_gla_gate(dve)
            dve_la(dve, "gla")
            dve_la_out(dve, "gla", "gla_on_g", GLA_OUT)
            for p in range(2):
                dve_la(dve, f"hg{p}", lambda n, p=p: split_lo(dve, 25 + 3 * p + n))
            dve_la_out(dve, "hg", "hg_on_g", HG_OUT)
            dve_fox(dve)
            dve_mix(dve)
            dve_residual(dve, "w_out", False, None)
            dve_gain_all(dve, "norm2_g")
            dve_up(dve, "ffn1_up", True, "norm2 rstd", zS, yg, yu)
            dve_residual(dve, "ffn1_down", True, "conv_norm_g_2")
            dve_conv_in(dve, bS, cS, vS, yS, r2)
            dve_residual(dve, "conv_out", False, "conv_ffn_norm_g_2")
            dve_up(dve, "ffn2_up", False, "ffn2 norm rstd", zS, yg, yu)
            dve_residual(dve, "ffn2_down", True, "kv_norm_g_2")
            dve_mla(dve)
            dve_residual(dve, "w_o", False, None)
            dve_gain_all(dve, "mla_ffn_norm_g_2")
            dve_up(dve, "ffn3_up", False, "ffn3 norm rstd", zS3, yg3, None)
            dve_residual(dve, "ffn3_down", True, None)
            dve_final(dve)

    return S


_OUT = (1, T, D)


def _program(nc, arrays, known):
    aps = {n: nc.dram_tensor(f"in_{n}", a.shape, mybir.dt.from_np(a.dtype), kind="ExternalInput").ap()
           for n, a in arrays.items()}
    out = nc.dram_tensor("out_0", _OUT, F32, kind="ExternalOutput").ap()
    cst = aps.pop("constants")
    flat = {n: (x[0] if len(x.shape) == 3 and n in _WEIGHTS else x) for n, x in aps.items()}
    return build(nc, flat, cst, out, known)


_WEIGHTS = {u[0] for u in UNITS}


def kernel(**inputs):
    import concourse.bacc as bacc
    from concourse.bass_utils import run_bass_kernel_spmd

    arrays = {n: np.ascontiguousarray(a) for n, a in inputs.items()}
    arrays["constants"] = constants()
    numbers = None
    for _ in range(2):
        nc = bacc.Bacc("TRN2", target_bir_lowering=False, num_devices=1)
        numbers = _program(nc, arrays, numbers)
    r = run_bass_kernel_spmd(nc, [{f"in_{n}": a for n, a in arrays.items()}], core_ids=[0])
    return r.results[0]["out_0"]
```

```python
import numpy as np
import concourse.bass as bass
from concourse import mybir
from contextlib import ExitStack

F32 = mybir.dt.float32
F32R = mybir.dt.float32r
I32 = mybir.dt.int32
ALU = mybir.AluOpType
ACT = mybir.ActivationFunctionType
AX = mybir.AxisListType

P = 128
T = 512
D = 1024
KT = D // P
TT = T // P
DH = 64
FF = 2816
FT = FF // P
THIRDS = ((0, 8), (8, 7), (15, 7))
GC = 64
LC = 16
NL = T // LC
NH2 = 8
EPS = 1e-6
UNIT = KT * P
RAW = 4
PARTS = 2

_LEVELS = [1, 2, 4, 8, 16, 32]
_COLS = {}


def _lay():
    at = 0
    sizes = [("ident", P), ("eps", 1), ("hsum", P), ("ones", P), ("neg", P), ("incl", P)]
    sizes += [(f"lev{b}", P) for b in _LEVELS]
    sizes += [("gla0", P), ("gla1", P), ("perm", P)]
    sizes += [(f"foxrow{h}", P) for h in range(4)] + [(f"gdnrow{h}", P) for h in range(4)]
    sizes += [(f"beta{p}", P) for p in range(2)] + [(f"gpair{p}", P) for p in range(2)]
    sizes += [("cmask", 8), ("hmask", 2), ("qmask", 4), ("freq", 1), ("sign", 1)]
    for name, n in sizes:
        _COLS[name] = (at, n)
        at += n
    return at


NCONST = _lay()
NCONST0 = P + 1


def constants():
    c = np.zeros((P, NCONST), np.float32)

    def put(name, a):
        at, n = _COLS[name]
        c[:, at:at + n] = a

    i = np.arange(P)
    s, r = i[:, None], i[None, :]
    put("ident", s == r)
    put("hsum", s // DH == r // DH)
    put("ones", 1.0)
    put("neg", np.where(r > s, -1e30, 0.0))
    put("incl", (s // GC == r // GC) & (s <= r))
    for b in _LEVELS:
        put(f"lev{b}", (s // (2 * b) == r // (2 * b)) & (s % (2 * b) < b) & (r % (2 * b) >= b))
    for w in range(2):
        put(f"gla{w}", s // 32 == 2 * w + r // DH)
    put("perm", (s // 64 == r // 64) & (s % 64 == (r + 32) % 64))
    for h in range(4):
        put(f"foxrow{h}", (s == h) & (r >= 0))
        put(f"gdnrow{h}", (s == 64 + h) & (r >= 0))
    for p in range(2):
        put(f"beta{p}", s == 32 + 2 * p + r // DH)
        put(f"gpair{p}", s == 64 + 2 * p + r // DH)
    put("cmask", i[:, None] // LC == np.arange(8)[None, :])
    put("hmask", i[:, None] // 64 == np.arange(2)[None, :])
    put("qmask", i[:, None] // 32 == np.arange(4)[None, :])
    inv = np.float32(10000.0) ** (-np.arange(0, 64, 2, dtype=np.float32) / np.float32(64))
    put("freq", inv[i % 32][:, None])
    put("sign", np.where(i % 64 < 32, -1.0, 1.0)[:, None])
    put("eps", EPS)
    return c


_ROWS = {}
_row_at = 0
for _name, _n in [("norm1_g", 8), ("norm2_g", 8), ("conv_norm_g_2", 8), ("conv_ffn_norm_g_2", 8), ("kv_norm_g_2", 8),
                  ("mla_norm_g_2", 8), ("mla_ffn_norm_g_2", 8), ("final_norm_g_2", 8), ("kv_latent_norm_g_2", 2),
                  ("mla_q_norm_g_2", 3), ("conv_w_2", 24), ("gdn_conv_w", 24), ("gla_b_gk", 1), ("fox_qn_g", 1),
                  ("fox_kn_g", 1), ("fox_on_g", 1), ("gdn_on_g", 1), ("hg_on_g", 1), ("gla_on_g", 1)]:
    _ROWS[_name] = (_row_at, _n)
    _row_at += _n
NROW0 = _row_at
NCONVW = 3 * 2 * FT
NROW1 = P
NROW2 = NCONVW - P + 2 * FT
NPCOL = NROW0 + NROW1 + NROW2
PARAM_COLS = 4 * P + 4

UNITS = []
FIRST = {}


def _units():
    def add(stage, name, kt, pieces):
        FIRST.setdefault(stage, len(UNITS))
        UNITS.append((name, kt, sum(n for _, _, n in pieces), pieces))

    gdn, z, hg, gla, gk, gg = 772, 1548, 1804, 2828, 3340, 3356
    add("w_in", "w_in", KT, [(0, 768, 32), (0, 1540, 32), (0, 1544, 32), (0, gk, 32)])
    for c in [gdn + P * i for i in range(6)] + [z, z + P]:
        add("w_in", "w_in", KT, [(0, c, P)])
    for c in [gla, gla + P, gla + 2 * P, gla + 3 * P, gg, gg + P]:
        add("w_in", "w_in", KT, [(0, c, P)])
    for i in range(8):
        add("w_in", "w_in", KT, [(0, hg + P * i, P)])
    for i in (2, 3, 0, 1, 4, 5):
        add("w_in", "w_in", KT, [(0, P * i, P)])
    for i in range(KT):
        add("w_out", "w_out", KT, [(0, P * i, P)])

    def ffn(stage, up, down):
        for i in range(FT):
            add(stage + "_up", up, KT, [(0, P * i, P)])
            add(stage + "_up", up, KT, [(0, FF + P * i, P)])
        for i in range(KT):
            for k0, k in THIRDS:
                add(stage + "_down", down, k, [(k0 * P, P * i, P)])

    ffn("ffn1", "w_up", "w_down")
    for i in range(KT):
        for part in range(3):
            add("conv_in", "conv_w_in_2", KT, [(0, part * D + P * i, P)])
    for i in range(KT):
        add("conv_out", "conv_w_out_2", KT, [(0, P * i, P)])
    ffn("ffn2", "conv_ffn_w13_2", "conv_ffn_w2_2")
    for c in [0, P, P + 64]:
        add("dkv", "w_dkv_2", KT, [(0, c, P)])
    for i in range(3):
        add("dq", "mla_w_dq_2", KT, [(0, P * i, P)])
    for part in range(2):
        for g in range(2):
            add("ukv", "w_ukv_2", 2, [(0, (4 * g + h) * 256 + part * P, P) for h in range(4)])
    for g in range(2):
        add("uq", "mla_w_uq_2", 3, [(0, 192 * (4 * g + h) + P, 64) for h in range(4)])
        for p in range(2):
            add("uq", "mla_w_uq_2", 3, [(0, 192 * (4 * g + 2 * p + h), P) for h in range(2)])
    for i in range(KT):
        add("w_o", "mla_w_o_2", KT, [(0, P * i, P)])
    ffn("ffn3", "mla_ffn_w13_2", "mla_ffn_w2_2")


_units()
LOADED = []
_sum = [0] * RAW
for _u, (_n, _k, _c, _pieces) in enumerate(UNITS):
    _sum[_u % RAW] += 16 * len(_pieces)
    LOADED.append(_sum[_u % RAW])


class Steps:

    def __init__(self, sems, known):
        self.sems, self.known = sems, known
        self.count = dict.fromkeys(sems, 0)
        self.at, self.banks, self.ring, self.last = {}, {}, 0, {}

    def step(self, engine, name):
        assert name not in self.at, name
        self.count[engine] += 1
        self.at[name] = (engine, self.count[engine])
        return self.sems[engine], 1

    def after(self, name):
        if self.known is None:
            return self.sems["dve"], 1
        engine, value = self.known.at[name]
        return self.sems[engine], value

    def take_bank(self, key, n):
        b = self.ring % n
        self.ring += 1
        self.banks[key] = b
        before = self.last.get(b)
        self.last[b] = key
        return b, before

    def bank(self, key):
        return self.known.banks[key] if self.known else 0



TILE0, NORM0, PAIR0, GATED0, XPART0 = {}, {}, {}, {}, {}
_tiles = _pairs = _gates = 0
for _s in ["w_out", "ffn1_up", "ffn1_down", "conv_in", "conv_out", "ffn2_up", "ffn2_down", "w_o", "ffn3_up", "ffn3_down"]:
    TILE0[_s] = _tiles
    if _s == "conv_in" or _s.endswith("_up"):
        _n = KT if _s == "conv_in" else FT
        PAIR0[_s], GATED0[_s] = _pairs, _gates
        _tiles += (3 if _s == "conv_in" else 2) * _n
        _pairs += _n
        _gates += 0 if _s == "conv_in" else _n
    else:
        NORM0[_s] = KT * len(NORM0)
        _tiles += KT
for _s in ["norm2_g", "conv_norm_g_2", "conv_ffn_norm_g_2", "kv_norm_g_2", "mla_norm_g_2", "mla_ffn_norm_g_2",
           "final_norm_g_2"]:
    XPART0[_s] = KT * len(XPART0)




def build(nc, A, cst_d, out_d, known):
    ctx = ExitStack()
    with ctx:
        def sb(name, shape, dt=F32, c=ctx):
            return c.enter_context(nc.sbuf_tensor(name, shape, dt))

        def sem(name):
            return ctx.enter_context(nc.semaphore(name))

        xT = sb("xT", [P, KT, T])
        xhi = sb("xhi", [P, KT, T], F32R)
        xlo = sb("xlo", [P, KT, T], F32R)
        raw = sb("raw", [P, RAW, UNIT])
        whi = sb("whi", [P, PARTS, UNIT], F32R)
        wlo = sb("wlo", [P, PARTS, UNIT], F32R)
        cst = sb("cst", [P, NCONST])
        pcol = sb("pcol", [P, NPCOL])
        gbias = sb("gbias", [P, 4])
        sq = sb("sq", [P, 2, T])
        ssq = sb("ssq", [P, T])
        rs = sb("rs", [P, T])
        xg = sb("xg", [P, 2, T])
        stat = sb("stat", [P, 4, 4])
        credit = sb("credit", [P, 8])
        ps = ctx.enter_context(nc.psum_tensor("ps", [P, 8, T], F32))
        NRING = 6

        def acc(tile):
            return ps[:, tile % 2, :]

        def ring(b):
            return ps[:, 2 + b, :]

        def C(name):
            at, n = _COLS[name]
            return cst[:, at:at + n]

        def par(name, k=0):
            return pcol[:, _ROWS[name][0] + k:_ROWS[name][0] + k + 1]

        def tile_of(buf, m):
            return buf[:, bass.ds(m, 1), :].rearrange("p o t -> p (o t)")

        S = Steps({e: sem(f"{e}_steps") for e in ("pe", "act", "dve", "pool")}, known)
        step, after = S.step, S.after
        unit_loaded = [sem(f"unit_loaded{i}") for i in range(RAW)]
        hi_split, lo_split, unit_used = sem("hi_split"), sem("lo_split"), sem("unit_used")
        acc_free = sem("acc_free")
        x_hi, x_lo, squared, summed = sem("x_hi"), sem("x_lo"), sem("squared"), sem("summed")
        tap_done, tap2_done, conv_done, gated = sem("tap_done"), sem("tap2_done"), sem("conv_done"), sem("gated")
        prod_done, prod_hi, prod_lo = sem("prod_done"), sem("prod_hi"), sem("prod_lo")
        x_loaded = [sem(f"x_loaded{i}") for i in range(TT)]
        cst0_loaded, cst_loaded = sem("cst0_loaded"), sem("cst_loaded")
        rows_loaded, small_loaded, x_again = sem("rows_loaded"), sem("small_loaded"), sem("x_again")
        pos_loaded, stored = sem("pos_loaded"), sem("stored")
        v, a, g, t_ = nc.vector, nc.scalar, nc.gpsimd, nc.tensor

        def f32(ap):
            return ap.bitcast(F32)

        def pe_ring(pe, key):
            b, before = S.take_bank(key, NRING)
            if before is not None:
                pe.wait_ge(*after(f"{before} taken"))
            return ring(b)

        def full(eng, key):
            eng.wait_ge(*after(f"{key} full"))
            return ring(S.bank(key))

        def unit_view(buf, u):
            _, kt, n, _ = UNITS[u]
            return buf[:, u % (RAW if buf is raw else PARTS), 0:kt * n].rearrange("p (k c) -> p k c", c=n)

        def is_past(u, i, per):
            return u + (per * i if isinstance(i, int) else 0) >= len(UNITS)

        def in_loop(value, i, per):
            return value if i is None else value + per * i

        def load_unit(sp, u):
            name, kt, n, pieces = UNITS[u]
            if u >= RAW:
                sp.wait_ge(lo_split, u - RAW + 1)
            at = 0
            for r0, c0, m in pieces:
                dst = unit_view(raw, u)[:, :, at:at + m]
                src = A[name][r0:r0 + kt * P, c0:c0 + m].rearrange("(k p) c -> p k c", p=P)
                sp.dma_start(dst, src).then_inc(unit_loaded[u % RAW], 16)
                at += m

        def load_loop(sp, stage, n_units, per, col):
            with sp.Fori(0, n_units // per) as i:
                for j in range(per):
                    u = FIRST[stage] + j
                    name, kt, n, pieces = UNITS[u]
                    r0 = pieces[0][0]
                    sp.wait_ge(lo_split, u - RAW + 1 + per * i)
                    src = A[name][r0:r0 + kt * P, bass.ds(col(i, j), n)].rearrange("(k p) c -> p k c", p=P)
                    sp.dma_start(unit_view(raw, u), src).then_inc(unit_loaded[u % RAW], 16)

        def elements(u, i, per):
            units = [UNITS[u]] + ([UNITS[u + per]] if i is not None and u + per < len(UNITS) else [])
            return max(kt * n for _, kt, n, _ in units)

        def split_hi(act, u, i=None, per=0):
            if is_past(u, i, per):
                return
            n = elements(u, i, per)
            act.wait_ge(unit_loaded[u % RAW], in_loop(LOADED[u], i, 16 * per // RAW))
            if u >= PARTS:
                act.wait_ge(unit_used, in_loop(u - PARTS + 1, i, per))
            a.activation(whi[:, u % PARTS, 0:n], raw[:, u % RAW, 0:n], ACT.Copy).then_inc(hi_split, 1)

        def split_lo(dve, u, i=None, per=0, e=v):
            if is_past(u, i, per):
                return
            n = elements(u, i, per)
            dve.wait_ge(hi_split, in_loop(u + 1, i, per))
            e.tensor_tensor(wlo[:, u % PARTS, 0:n], raw[:, u % RAW, 0:n], f32(whi[:, u % PARTS, 0:n]),
                            ALU.subtract).then_inc(lo_split, 1)

        def passes(out, wh, wl, xh, xl, first, last):
            t_.matmul(out, wh, xh, start=first, stop=False)
            t_.matmul(out, wh, xl, start=False, stop=False)
            return t_.matmul(out, wl, xh, start=False, stop=last)

        def product(pe, u, tile, i=None, per=0, x=(xhi, xlo), k0=0, start=True, stop=True, ready=None, cols=0,
                    full=None, order=None, ks=None):
            kt = UNITS[u][1]
            pe.wait_ge(lo_split, in_loop(u + 1, i, per))
            for n, k in list(enumerate(order or range(kt)))[slice(*(ks or (0, kt)))]:
                if ready is not None:
                    ready(pe, k0 + k)
                wh, wl = (unit_view(b, u)[:, k, cols:cols + P] for b in (whi, wlo))
                last = passes(acc(tile), wh, wl, x[0][:, k0 + k, :], x[1][:, k0 + k, :],
                              start and n == 0, stop and n == kt - 1)
            if ks is None or ks[1] == kt:
                last.then_inc(*(step("pe", full) if full else (unit_used, 1)))

        def pe_sum(pe, name, n0):
            out = pe_ring(pe, f"{name} sum")
            pe.wait_ge(summed, n0 + KT + 2)
            t_.matmul(out, C("ones"), ssq[:, :], start=True, stop=True).then_inc(*step("pe", f"{name} sum full"))

        def act_rstd(act, name, width, out, columns=T, table=True):
            key = f"{name} sum"
            if table:
                a.preload_act_table_set("natural_log_exp_and_others")
            bank = full(act, key)[:, 0:columns]
            a.activation(out, bank, ACT.Ln, scale=1.0 / width, bias=C("eps")).then_inc(*step("act", f"{key} taken"))
            act.wait_ge(*after(f"{key} taken"))
            a.activation(out, out, ACT.Exp, scale=-0.5).then_inc(*step("act", f"{name} rstd"))

        def dve_scale(dve, name, tiles, src, gain, hi, lo, rstd, r, before=None):
            def low(k):
                dve.wait_ge(*after(f"{name} hi{k}"))
                v.tensor_tensor(lo[:, k, :], xg[:, k % 2, :], f32(hi[:, k, :]),
                                ALU.subtract).then_inc(*step("dve", f"{name} lo{k}"))
            dve.wait_ge(*after(rstd))
            if before:
                dve.wait_ge(*after(before))
            for k in range(tiles):
                if k >= 2:
                    dve.wait_ge(*after(f"{name} lo{k - 2}"))
                v.scalar_tensor_tensor(xg[:, k % 2, :], src[:, k, :], par(gain, k), r, ALU.mult,
                                       ALU.mult).then_inc(*step("dve", f"{name} scaled{k}"))
                if k:
                    low(k - 1)
            low(tiles - 1)

        def act_hi(act, name, tiles, hi):
            for k in range(tiles):
                act.wait_ge(*after(f"{name} scaled{k}"))
                a.activation(hi[:, k, :], xg[:, k % 2, :], ACT.Copy).then_inc(*step("act", f"{name} hi{k}"))

        def gain_of(name, k):
            return pcol[:, bass.ds(_ROWS[name][0] + k, 1)]

        def act_gained(act, name, k):
            a.activation(tile_of(xT if name == "final_norm_g_2" else xhi, k), tile_of(xT, k), ACT.Copy,
                         scale=gain_of(name, k)).then_inc(x_hi, 1)

        def dve_gained(dve, name, k, n):
            dve.wait_ge(x_hi, n)
            v.scalar_tensor_tensor(tile_of(xlo, k), tile_of(xT, k), gain_of(name, k), f32(tile_of(xhi, k)), ALU.mult,
                                   ALU.subtract).then_inc(x_lo, 1)

        def act_gain_all(act, name, used, tiles=range(KT)):
            act.wait_ge(unit_used, used)
            for k in tiles:
                act_gained(act, name, k)

        def dve_gain_all(dve, name):
            for k in range(KT):
                dve_gained(dve, name, k, XPART0[name] + k + 1)

        def parts_of(name):
            return lambda pe, k: pe.wait_ge(x_lo, XPART0[name] + k + 1)

        def rounds(engine, stage, n, body, following):
            last = bool(following) or FIRST[stage] + n * 12 == len(UNITS)
            with engine.Fori(0, n - last) as i:
                body(i, None)
            if last:
                body(n - 1, following)

        def round_of(thirds):
            per, np_ = (12, 3) if thirds else (4, 1)
            return per, np_, per // np_

        def pe_residual(pe, stage, thirds, x, ready, order=None):
            per, np_, tiles = round_of(thirds)
            parts = THIRDS if thirds else ((0, KT),)
            n0 = TILE0[stage]
            with pe.Fori(0, KT // tiles) as i:
                for j in range(per):
                    m, part = divmod(j, np_)
                    if part == 0:
                        pe.wait_ge(acc_free, n0 + m + 1 + tiles * i)
                    product(pe, FIRST[stage] + j, m, i, per, x, parts[part][0], part == 0, part == np_ - 1,
                            ready if m == 0 else None, order=order)

        def act_residual(act, stage, thirds, gain, following=None):
            per, np_, tiles = round_of(thirds)
            r0, n0 = NORM0[stage], TILE0[stage]

            def square(i, m):
                act.wait_ge(acc_free, n0 + m + 3 + tiles * i)
                act.wait_ge(summed, r0 + m + 1 + tiles * i)
                a.activation(sq[:, m % 2, :], tile_of(xT, m + tiles * i), ACT.Square).then_inc(squared, 1)

            def body(i, begun):
                for j in range(per):
                    m = j // np_
                    if begun and j == per - 1:
                        used = FIRST[stage] + KT // tiles * per
                        act_gain_all(act, begun, used, range(KT // 2))
                        square(i, m)
                        act_gain_all(act, begun, used, range(KT // 2, KT))
                    split_hi(act, FIRST[stage] + j + 2, i, per)
                    if j % np_ == np_ - 1 and not (begun and j == per - 1):
                        square(i, m)
                        if gain:
                            act.wait_ge(squared, r0 + m + 1 + tiles * i)
                            act_gained(act, gain, m + tiles * i)
            rounds(act, stage, KT // tiles, body, following)

        def dve_residual(dve, stage, thirds, gain, following=None):
            per, np_, tiles = round_of(thirds)
            n0 = TILE0[stage]

            def body(i, begun):
                for j in range(per):
                    if j % np_ == np_ - 1:
                        m = j // np_
                        dve.wait_ge(unit_used, FIRST[stage] + j + 1 + per * i)
                        x = tile_of(xT, m + tiles * i)
                        v.tensor_tensor(x, acc(m), x, ALU.add).then_inc(acc_free, 1)
                    if begun and j == per - 1:
                        dve_gain_all(dve, begun)
                    split_lo(dve, FIRST[stage] + j + 2, i, per)
                    if j % np_ == np_ - 1 and gain:
                        dve.wait_ge(acc_free, n0 + m + 3 + tiles * i)
                        dve_gained(dve, gain, m + tiles * i, XPART0[gain] + m + 1 + tiles * i)
            rounds(dve, stage, KT // tiles, body, following)

        def pool_residual(pool, stage, reader):
            r0 = NORM0[stage]
            pool.wait_ge(*after(reader))
            g.memset(ssq[:, :], 0.0).then_inc(*step("pool", f"{stage} sum cleared"))
            pool.wait_ge(*after(f"{stage} sum cleared"))
            with pool.Fori(0, KT // 2) as i:
                for m in range(2):
                    pool.wait_ge(squared, r0 + m + 1 + 2 * i)
                    pool.wait_ge(summed, r0 + m + 2 + 2 * i)
                    g.tensor_tensor(ssq[:, :], ssq[:, :], sq[:, m, :], ALU.add).then_inc(summed, 1)

        def ffn_w(k, m):
            return pcol[:, bass.ds(NROW0 + k * 2 * FT + m, 1)]

        def ffn_b(m):
            return pcol[:, bass.ds(NROW0 + NCONVW + m, 1)]

        def pe_up(pe, stage, name, gain, residual):
            n0 = TILE0[stage]

            def body(i, first):
                for j in range(4):
                    pe.wait_ge(acc_free, n0 + j + 1 + 4 * i)
                    product(pe, FIRST[stage] + j, j, i, 4, ready=parts_of(gain) if first and j == 0 else None)
                    if first and j == 0:
                        pe_sum(pe, name, NORM0[residual])
            body(0, True)
            with pe.Fori(1, FT // 2) as i:
                body(i, False)

        def act_up(act, stage, conv, h_hi, zS, yg, yu):
            u0, p0, n0 = FIRST[stage], PAIR0[stage], TILE0[stage]
            a.preload_act_table_set("silu_and_others")
            with act.Fori(0, FT // 2) as i:
                for j in range(4):
                    pair, is_up = j // 2, j % 2
                    m = pair + 2 * i
                    split_hi(act, u0 + j + 2, i, 4)
                    if conv:
                        mt = m + FT * is_up
                        act.wait_ge(prod_done, p0 + pair + 1 + 2 * i)
                        act.wait_ge(acc_free, n0 + j + 3 + 4 * i)
                        a.activation((yu if is_up else yg)[:, pair, :], zS[:, is_up, :], ACT.Identity,
                                     scale=ffn_w(2, mt), bias=ffn_b(mt)).then_inc(tap_done, 1)
                        if is_up:
                            act.wait_ge(conv_done, j + 2 + 4 * i)
                            a.activation(yg[:, pair, :], yg[:, pair, :], ACT.Silu).then_inc(gated, 1)
                    elif not is_up:
                        act.wait_ge(acc_free, n0 + j + 3 + 4 * i)
                        a.activation(yg[:, pair, :], zS[:, 0, :], ACT.Silu).then_inc(gated, 1)
                    if is_up:
                        act.wait_ge(prod_done, p0 + pair + 3 + 2 * i)
                        a.activation(tile_of(h_hi, m), xg[:, pair, :], ACT.Copy).then_inc(prod_hi, 1)

        def dve_up(dve, stage, conv, rstd, zS, yg, yu):
            u0, p0, n0 = FIRST[stage], PAIR0[stage], TILE0[stage]
            dve.wait_ge(*after(rstd))
            with dve.Fori(0, FT // 2) as i:
                for j in range(4):
                    pair, is_up = j // 2, j % 2
                    z = zS[:, is_up, :]
                    dve.wait_ge(unit_used, u0 + j + 1 + 4 * i)
                    if conv:
                        dve.wait_ge(conv_done, j + 1 + 4 * i)
                    else:
                        dve.wait_ge(prod_done, p0 + pair + 2 + 2 * i)
                    v.tensor_tensor(z, acc(j), rs[:, :], ALU.mult).then_inc(acc_free, 1)
                    split_lo(dve, u0 + j + 2, i, 4)
                    dve.wait_ge(acc_free, n0 + j + 3 + 4 * i)
                    if conv:
                        y, mt = (yu if is_up else yg)[:, pair, :], pair + 2 * i + FT * is_up
                        dve.wait_ge(tap_done, j + 1 + 4 * i)
                        v.scalar_tensor_tensor(y[:, 1:T], z[:, 0:T - 1], ffn_w(1, mt), y[:, 1:T], ALU.mult,
                                               ALU.add).then_inc(tap2_done, 1)
                        dve.wait_ge(tap2_done, j + 1 + 4 * i)
                        v.scalar_tensor_tensor(y[:, 2:T], z[:, 0:T - 2], ffn_w(0, mt), y[:, 2:T], ALU.mult,
                                               ALU.add).then_inc(conv_done, 1)
                    if is_up:
                        if conv:
                            dve.wait_ge(conv_done, j + 3 + 4 * i)
                        dve.wait_ge(gated, GATED0[stage] + pair + 1 + 2 * i)
                        dve.wait_ge(prod_lo, p0 + pair + 1 + 2 * i)
                        v.tensor_tensor(xg[:, pair, :], yg[:, pair, :], yu[:, pair, :] if conv else z,
                                        ALU.mult).then_inc(prod_done, 1)

        def pool_products(pool, stage, n, h_hi, h_lo):
            p0 = PAIR0[stage]
            with pool.Fori(0, n // 2) as i:
                for m in range(2):
                    pool.wait_ge(prod_hi, p0 + m + 1 + 2 * i)
                    g.tensor_tensor(tile_of(h_lo, m + 2 * i), xg[:, m, :], f32(tile_of(h_hi, m + 2 * i)),
                                    ALU.subtract).then_inc(prod_lo, 1)

        def pe_conv_in(pe):
            n0 = TILE0["conv_in"]

            def body(i, first):
                for j in range(12):
                    pe.wait_ge(acc_free, n0 + j + 1 + 12 * i)
                    product(pe, FIRST["conv_in"] + j, j, i, 12,
                            ready=parts_of("conv_norm_g_2") if first and j == 0 else None)
                    if first and j == 0:
                        pe_sum(pe, "conv norm", NORM0["ffn1_down"])
            body(0, True)
            with pe.Fori(1, KT // 4) as i:
                body(i, False)

        def act_conv_in(act, h_hi, zS, yS):
            u0, p0 = FIRST["conv_in"], PAIR0["conv_in"]
            with act.Fori(0, KT // 4) as i:
                for j in range(12):
                    m, part = divmod(j, 3)
                    split_hi(act, u0 + j + 2, i, 12)
                    if part == 2:
                        act.wait_ge(acc_free, TILE0["conv_in"] + j + 3 + 12 * i)
                        act.wait_ge(prod_done, p0 + m + 1 + 4 * i)
                        a.activation(yS[:, m % 2, :], zS[:, m % 2, :], ACT.Copy,
                                     scale=gain_of("conv_w_2", 2 * KT + m + 4 * i)).then_inc(tap_done, 1)
                        act.wait_ge(prod_done, p0 + m + 3 + 4 * i)
                        a.activation(tile_of(h_hi, m + 4 * i), xg[:, m % 2, :], ACT.Copy).then_inc(prod_hi, 1)

        def dve_conv_in(dve, bS, cS, zS, yS, r2):
            u0, p0, n0 = FIRST["conv_in"], PAIR0["conv_in"], TILE0["conv_in"]
            dve.wait_ge(*after("conv norm rstd"))
            v.tensor_tensor(r2[:, :], rs[:, :], rs[:, :], ALU.mult).then_inc(*step("dve", "conv norm rstd^2"))
            dve.wait_ge(*after("conv norm rstd^2"))
            with dve.Fori(0, KT // 4) as i:
                for j in range(12):
                    m, part = divmod(j, 3)
                    z, y = zS[:, m % 2, :], yS[:, m % 2, :]
                    dve.wait_ge(unit_used, u0 + j + 1 + 12 * i)
                    if part == 0:
                        dve.wait_ge(prod_done, p0 + m + 1 + 4 * i)
                    if part < 2:
                        v.tensor_tensor((bS, cS)[part][:, m % 2, :], acc(j), (rs, r2)[part][:, :],
                                        ALU.mult).then_inc(acc_free, 1)
                        split_lo(dve, u0 + j + 2, i, 12)
                        continue
                    dve.wait_ge(acc_free, n0 + j + 2 + 12 * i)
                    v.tensor_tensor(z, cS[:, m % 2, :], acc(j), ALU.mult).then_inc(acc_free, 1)
                    split_lo(dve, u0 + j + 2, i, 12)
                    w = [gain_of("conv_w_2", KT * k + m + 4 * i) for k in range(2)]
                    c0 = 2 * FT + 2 * m + 8 * i
                    t0 = 2 * FT + m + 1 + 4 * i
                    dve.wait_ge(acc_free, n0 + j + 3 + 12 * i)
                    dve.wait_ge(tap_done, t0)
                    v.scalar_tensor_tensor(y[:, 1:T], z[:, 0:T - 1], w[1], y[:, 1:T], ALU.mult,
                                           ALU.add).then_inc(tap2_done, 1)
                    dve.wait_ge(tap2_done, c0 + 1)
                    v.scalar_tensor_tensor(y[:, 2:T], z[:, 0:T - 2], w[0], y[:, 2:T], ALU.mult,
                                           ALU.add).then_inc(tap2_done, 1)
                    dve.wait_ge(tap2_done, c0 + 2)
                    dve.wait_ge(prod_lo, p0 + m + 1 + 4 * i)
                    v.tensor_tensor(xg[:, m % 2, :], y, bS[:, m % 2, :], ALU.mult).then_inc(prod_done, 1)

        mixers = ctx.enter_context(ExitStack())
        mx = sb("mx", [P, 36, T], c=mixers)
        mixT = sb("mixT", [P, KT, T], c=mixers)
        graw = sb("graw", [P, T], c=mixers)
        grow = sb("grow", [P, T], c=mixers)
        gcol = sb("gcol", [P, TT, P], c=mixers)
        ecol = sb("ecol", [P, TT, 36], c=mixers)
        lastone = sb("lastone", [P, T], c=mixers)
        vnew = sb("vnew", [P, 2, 4 * DH], c=mixers)
        state = sb("state", [P, 2, P], c=mixers)
        wgk = sb("wgk", [P, P], c=mixers)
        hr = (rs[:, :], ssq[:, :])
        wide = mx[:, :, :].rearrange("p a t -> p (a t)")

        def wtile(k, n):
            return wide[:, k * T:(k + n) * T]

        xtok = wtile(0, 8).rearrange("p (t d) -> p t d", d=D)
        prow = wtile(8, 1).rearrange("p (n c) -> p n c", c=P)
        scanmask = mx[:, 35, :]
        Q, K, V = 0, 2, 4
        KZ, KB, MTt, X_, XT_, AT, Y = 10, 14, 16, 20, 24, 28, 32
        kbg, vb, kout, wT = wtile(10, 2), wtile(12, 2), wtile(4, 2), wtile(14, 2)
        kbg, vb, kout = (b.rearrange("p (t c) -> p t c", t=TT) for b in (kbg, vb, kout))
        wT = wT.rearrange("p (h t) -> p h t", h=2)
        uu, oo = (wtile(k, 2).rearrange("p (t c) -> p t c", t=TT) for k in (32, 34))

        def sp_load_inputs(sp):
            for t in range(TT):
                sp.dma_start(xtok[:, t, :], A["x"][0, t * P:(t + 1) * P, :]).then_inc(x_loaded[t], 16)

        def load_rows(q):
            q.dma_start(prow[:, 0:3, :].rearrange("p n c -> p (n c)"), A["params"][:, 0:3 * P]).then_inc(rows_loaded, 16)

        def load_small(q):
            q.dma_start(wgk[:, :], A["params"][:, 3 * P:4 * P]).then_inc(small_loaded, 16)
            q.dma_start(gbias[:, :], A["params"][:, 4 * P:PARAM_COLS]).then_inc(small_loaded, 16)
        N_SMALL = 2

        def pool_init(pool):
            for n, s in enumerate((acc_free, summed, prod_done, prod_lo, conv_done)):
                g.memset(credit[:, n:n + 1], 0.0).then_inc(s, 2)
            g.memset(scanmask, 1.0).then_inc(*step("pool", "scanmask ones"))
            pool.wait_ge(*after("scanmask ones"))
            g.memset(scanmask[64:68].rearrange("p (n c) -> p n c", c=GC)[:, :, 0:1], 0.0).then_inc(
                *step("pool", "scanmask"))
            pool.wait_ge(*after("scanmask"))
            g.memset(lastone[:, :], 0.0).then_inc(*step("pool", "lastone zeros"))
            pool.wait_ge(*after("lastone zeros"))
            g.memset(lastone[:, :].rearrange("p (n c) -> p n c", c=LC)[:, :, LC - 1:LC], 1.0)
            g.memset(mx[:, 33, :], 0.0)
            g.memset(vnew[:, :, :], 0.0)
            g.memset(state[:, :, :], 0.0).then_inc(*step("pool", "mixers cleared"))

        def pe_load(pe):
            pe.wait_ge(cst0_loaded, 16)
            pe.wait_ge(rows_loaded, 16)
            out = pe_ring(pe, "params")
            at = 0
            for n, rows in enumerate((NROW0, NROW1, NROW2)):
                last = t_.transpose(out[:, at:at + rows], prow[0:rows, n, :], C("ident")[0:rows, 0:rows])
                at += rows
            last.then_inc(*step("pe", "params full"))
            for k in range(KT):
                out = pe_ring(pe, f"x{k}")
                for t in range(TT):
                    if k == 0:
                        pe.wait_ge(*after(f"x normed{t}"))
                    last = t_.transpose(out[:, t * P:(t + 1) * P], xtok[:, t, k * P:(k + 1) * P], C("ident"))
                last.then_inc(*step("pe", f"x{k} full"))

        def act_load(act):
            a.preload_act_table_set("natural_log_exp_and_others")
            act.wait_ge(cst0_loaded, 16)
            for t in range(TT):
                ss, ln, rstd = (stat[:, t, n:n + 1] for n in range(3))
                act.wait_ge(x_loaded[t], 16)
                a.activation(wtile(10 + 2 * t, 2), xtok[:, t, :], ACT.Square, accum_out=ss).then_inc(
                    *step("act", f"x squares{t}"))
                act.wait_ge(*after(f"x squares{t}"))
                a.activation(ln, ss, ACT.Ln, scale=1.0 / D, bias=C("eps")).then_inc(*step("act", f"x ln{t}"))
                act.wait_ge(*after(f"x ln{t}"))
                a.activation(rstd, ln, ACT.Exp, scale=-0.5).then_inc(*step("act", f"x rstd{t}"))
            split_hi(act, 0)
            split_hi(act, 1)
            act.wait_ge(*after("params taken"))
            for k in range(KT):
                a.activation(xhi[:, k, :], full(act, f"x{k}"), ACT.Copy, scale=par("norm1_g", k)).then_inc(
                    *step("act", f"x hi{k}"))

        def dve_load(dve):
            v.tensor_copy(pcol[:, :], full(dve, "params")[:, 0:NPCOL]).then_inc(*step("dve", "params taken"))
            for t in range(TT):
                dve.wait_ge(*after(f"x rstd{t}"))
                v.tensor_scalar(xtok[:, t, :], xtok[:, t, :], stat[:, t, 2:3], None, ALU.mult).then_inc(
                    *step("dve", f"x normed{t}"))
            split_lo(dve, 0)
            split_lo(dve, 1)
            for k in range(KT):
                dve.wait_ge(*after(f"x hi{k}"))
                v.scalar_tensor_tensor(xlo[:, k, :], full(dve, f"x{k}"), par("norm1_g", k), f32(xhi[:, k, :]), ALU.mult,
                                       ALU.subtract).then_inc(*step("dve", f"x{k} taken"))

        xagain = wtile(28, 8).rearrange("p (t d) -> p t d", d=D)

        def pool_load_again(pool):
            for m in (4, 5):
                pool.wait_ge(*after(f"mix{m}"))
            for t in range(TT):
                pool.dma_start(xagain[:, t, :], A["x"][0, t * P:(t + 1) * P, :]).then_inc(x_again, 16)

        def pe_x_again(pe, ks):
            pe.wait_ge(x_again, 16 * TT)
            for k in ks:
                out = pe_ring(pe, f"xT{k}")
                for t in range(TT):
                    last = t_.transpose(out[:, t * P:(t + 1) * P], xagain[:, t, k * P:(k + 1) * P], C("ident"))
                last.then_inc(*step("pe", f"xT{k} full"))

        def act_x_again(act, ks):
            for k in ks:
                a.activation(xT[:, k, :], full(act, f"xT{k}"), ACT.Copy).then_inc(*step("act", f"xT{k} taken"))

        def pe_in(pe, u, ks=None):
            if u >= 2:
                pe.wait_ge(*after(f"in{u - 2} taken"))
            product(pe, u, u, ready=(lambda pe, k: pe.wait_ge(*after(f"x{k} taken"))) if u == 0 else None, ks=ks)

        def act_copy_in(act, u, dst, scale=1.0):
            act.wait_ge(unit_used, u + 1)
            a.activation(dst, acc(u), ACT.Copy, scale=scale).then_inc(*step("act", f"in{u} taken"))

        silu_n = {"act": 0, "dve": 0}

        def act_sigmoid(act, name, x, e, sign):
            a.activation(e, x, ACT.Exp, scale=-sign).then_inc(*step("act", f"{name} exp"))
            act.wait_ge(*after(f"{name} exp"))
            a.activation(e, e, ACT.Ln, bias=1.0).then_inc(*step("act", f"{name} ln"))
            act.wait_ge(*after(f"{name} ln"))
            a.activation(e, e, ACT.Exp, scale=-1.0).then_inc(*step("act", f"{name} sigmoid"))

        def act_silu(act, name, x, ready):
            n = silu_n["act"]
            silu_n["act"] += 1
            act.wait_ge(*after(ready))
            if n >= 2:
                act.wait_ge(*after(f"silu{n - 2} used"))
            act_sigmoid(act, name, x, xg[:, n % 2, :], 1.0)

        def dve_silu(dve, name, x, scale=1.0):
            n = silu_n["dve"]
            silu_n["dve"] += 1
            dve.wait_ge(*after(f"{name} sigmoid"))
            v.scalar_tensor_tensor(x, x, scale, xg[:, n % 2, :], ALU.mult, ALU.mult).then_inc(
                *step("dve", f"silu{n} used"))

        def act_head_norm(act, name, src, ready, scale, n=0):
            for i, x in enumerate(src):
                act.wait_ge(*after(ready[i]))
                if i >= 2:
                    act.wait_ge(*after(f"{name} sum{i - 2} full"))
                a.activation(sq[:, i % 2, :], x, ACT.Square).then_inc(*step("act", f"{name} square{i}"))
                if i:
                    act_head_rs(act, name, i - 1, scale)
            act_head_rs(act, name, len(src) - 1, scale)

        def act_head_rs(act, name, i, scale):
            key = f"{name} sum{i}"
            if i >= 2:
                act.wait_ge(*after(f"{name} {i - 2}"))
            r = hr[i % 2]
            a.activation(r, full(act, key), ACT.Ln, scale=scale, bias=C("eps")).then_inc(*step("act", f"{key} taken"))
            act.wait_ge(*after(f"{key} taken"))
            a.activation(r, r, ACT.Exp, scale=-0.5).then_inc(*step("act", f"{name} rs{i}"))

        def pe_head_norm(pe, name, which):
            for i in which:
                out = pe_ring(pe, f"{name} sum{i}")
                pe.wait_ge(*after(f"{name} square{i}"))
                t_.matmul(out, C("hsum"), sq[:, i % 2, :], start=True, stop=True).then_inc(
                    *step("pe", f"{name} sum{i} full"))

        def dve_head_norm(dve, name, src, gain, which=None):
            for i in which or range(len(src)):
                x = src[i]
                dve.wait_ge(*after(f"{name} rs{i}"))
                v.scalar_tensor_tensor(x, x, gain[i], hr[i % 2], ALU.mult,
                                       ALU.mult).then_inc(*step("dve", f"{name} {i}"))

        def pe_transpose(pe, key, x, ready):
            out = pe_ring(pe, key)
            if ready:
                pe.wait_ge(*after(ready))
            for t in range(TT):
                last = t_.transpose(out[:, t * P:(t + 1) * P], x[:, t * P:(t + 1) * P], C("ident"))
            last.then_inc(*step("pe", f"{key} full"))

        LS, LG = mx[:, 32, :], mx[:, 34, :]
        D1 = mx[:, 33, :]

        def dve_gate_in(dve):
            dve.wait_ge(small_loaded, 16 * N_SMALL)
            dve.wait_ge(unit_used, 1)
            v.tensor_scalar(graw[:, :], acc(0), gbias[:, 0:1], None, ALU.add).then_inc(*step("dve", "in0 taken"))

        def act_gates(act):
            act.wait_ge(*after("in0 taken"))
            a.activation(gbias[64:68, 2:3], gbias[64:68, 1:2], ACT.Exp).then_inc(*step("act", "exp a_log"))
            a.activation(LG, graw[:, :], ACT.Abs).then_inc(*step("act", "gate abs"))
            act.wait_ge(*after("gate abs"))
            a.activation(LG, LG, ACT.Exp, scale=-1.0).then_inc(*step("act", "gate exp"))
            act.wait_ge(*after("gate exp"))
            a.activation(LG, LG, ACT.Ln, bias=1.0).then_inc(*step("act", "gate ln"))
            act.wait_ge(*after("gate scan"))
            a.activation(grow[32:36, :], LS[32:36, :], ACT.Exp).then_inc(*step("act", "beta"))

        def dve_gates(dve):
            dve.wait_ge(*after("gate ln"))
            dve.wait_ge(*after("mixers cleared"))
            v.scalar_tensor_tensor(LS, graw[:, :], 0.0, LG, ALU.min, ALU.subtract).then_inc(*step("dve", "log sigmoid"))
            dve.wait_ge(*after("log sigmoid"))
            v.tensor_scalar(D1[0:4], LS[0:4], -1.0, None, ALU.mult)
            v.tensor_tensor(D1[64:68], LS[64:68], graw[64:68, :], ALU.subtract).then_inc(*step("dve", "-softplus"))
            dve.wait_ge(*after("-softplus"))
            v.tensor_scalar(D1[64:68], D1[64:68], gbias[64:68, 2:3], None, ALU.mult).then_inc(*step("dve", "decay"))
            dve.wait_ge(*after("decay"))
            v.tensor_tensor_scan(grow[:, :], scanmask, D1, 0.0, ALU.mult, ALU.add).then_inc(*step("dve", "gate scan"))
            dve.wait_ge(*after("gate scan"))
            G3 = grow[64:68, :].rearrange("p (n c) -> p n c", c=GC)
            v.tensor_tensor(grow[96:100, :].rearrange("p (n c) -> p n c", c=GC),
                            G3[:, :, GC - 1:GC].to_broadcast([4, T // GC, GC]), G3,
                            ALU.subtract).then_inc(*step("dve", "to chunk end"))

        def pe_gates(pe):
            pe.wait_ge(*after("beta"))
            pe_transpose(pe, "gcol", grow[:, :], "to chunk end")

        def dve_gcol(dve):
            v.tensor_copy(gcol[:, :, :].rearrange("p t c -> p (t c)"),
                          full(dve, "gcol")).then_inc(*step("dve", "gcol taken"))

        def act_ecol(act):
            act.wait_ge(*after("gcol taken"))
            a.activation(ecol[:, :, :], gcol[:, :, 64:100], ACT.Exp).then_inc(*step("act", "ecol"))

        def act_gdn_tap(act, i):
            act.wait_ge(unit_used, i + 2)
            if i == 0:
                act.wait_ge(*after("x7 taken"))
            a.activation(mx[:, i, :], acc(i + 1), ACT.Identity,
                         scale=par("gdn_conv_w", 18 + i)).then_inc(*step("act", f"gdn tap{i}"))

        def dve_gdn_conv(dve, i):
            y = mx[:, i, :]
            dve.wait_ge(*after(f"gdn tap{i}"))
            for back in (1, 2, 3):
                name = f"in{i + 1} taken" if back == 3 else f"gdn tap{i} {back}"
                v.scalar_tensor_tensor(y[:, back:T], acc(i + 1)[:, 0:T - back], par("gdn_conv_w", 6 * (3 - back) + i),
                                       y[:, back:T], ALU.mult, ALU.add).then_inc(*step("dve", name))
                if back < 3:
                    dve.wait_ge(*after(name))

        GDN_QK = [mx[:, i, :] for i in range(4)]

        def pe_gdn_setup(pe):
            for p in range(2):
                out = pe_ring(pe, f"beta{p}")
                t_.matmul(out, C(f"beta{p}"), grow[:, :], start=True, stop=True).then_inc(
                    *step("pe", f"beta{p} full"))
            for h in range(4):
                out = pe_ring(pe, f"gdn G{h}")
                t_.matmul(out, C(f"gdnrow{h}"), grow[:, :], start=True, stop=True).then_inc(
                    *step("pe", f"gdn G{h} full"))

        def pool_gdn(pool):
            for h in range(4):
                pool.wait_ge(*after(f"gdn qk {2 + h // 2}"))
                g.tensor_scalar(mx[:, KZ + h, :], mx[:, K + h // 2, :], C("hmask")[:, h % 2:h % 2 + 1], None,
                                ALU.mult).then_inc(*step("pool", f"gdn kz{h}"))

        def act_gdn_norm(act):
            act_head_norm(act, "gdn qk", GDN_QK, [f"silu{i} used" for i in range(4)], 1.0)

        def act_gdn_setup(act):
            for h in range(4):
                act.wait_ge(*after(f"gdn G{h} taken"))
                a.activation(mx[:, Y + h, :], mx[:, Y + h, :], ACT.Exp).then_inc(*step("act", f"gdn decay{h}"))

        def dve_gdn_norm(dve):
            dve_head_norm(dve, "gdn qk", GDN_QK, [0.125, 0.125, 1.0, 1.0])

        def dve_gdn_setup(dve):
            for p in range(2):
                dve.wait_ge(*after(f"gdn qk {2 + p}"))
                v.tensor_tensor(mx[:, KB + p, :], mx[:, K + p, :], full(dve, f"beta{p}"),
                                ALU.mult).then_inc(*step("dve", f"beta{p} taken"))
            for h in range(4):
                bank = full(dve, f"gdn G{h}")
                if h == 0:
                    dve.wait_ge(*after("gcol taken"))
                    dve.wait_ge(*after("beta"))
                for t in range(TT):
                    blk = slice(t * P, (t + 1) * P)
                    last = t == TT - 1
                    v.tensor_scalar(mx[:, Y + h, blk], bank[:, blk], gcol[:, t, 64 + h:65 + h], 0.0, ALU.subtract,
                                    ALU.min).then_inc(*step("dve", f"gdn G{h} taken" if last else f"gdn exponent{h} {t}"))

        def blocks(tile):
            return mx[:, tile, :].rearrange("p (t r) -> p t r", r=P)

        def pe_block_products(pe, key, lhs, rhs):
            out = pe_ring(pe, key)
            for t in range(TT):
                blk = slice(t * P, (t + 1) * P)
                last = t_.matmul(out[:, blk], lhs[:, blk], rhs[:, blk], start=True, stop=True)
            last.then_inc(*step("pe", f"{key} full"))

        def halves(x, b, second):
            return x.rearrange("p (n two b) -> p n two b", two=2, b=b)[:, :, int(second), :]

        def pe_half_products(pe, key, lhs, rhs, b, second):
            out = pe_ring(pe, key)
            for t in range(TT):
                blk = slice(t * P, (t + 1) * P)
                last = t_.matmul(out[:, t * 64:(t + 1) * 64].rearrange("p (n b) -> p n b", b=b), lhs[:, blk],
                                 halves(rhs[:, blk], b, second), start=True, stop=True)
            last.then_inc(*step("pe", f"{key} full"))

        def pe_gdn_triangles(pe):
            for h in range(4):
                pe.wait_ge(*after(f"gdn kz{h}"))
                pe.wait_ge(*after(f"beta{h // 2} taken"))
                pe_block_products(pe, f"gdn M{h}", mx[:, KZ + h, :], mx[:, KB + h // 2, :])

        def dve_gdn_triangles(dve):
            for h in range(4):
                dve.wait_ge(*after(f"gdn decay{h}"))
                v.tensor_tensor(mx[:, MTt + h, :], full(dve, f"gdn M{h}"), mx[:, Y + h, :],
                                ALU.mult).then_inc(*step("dve", f"gdn M{h} taken"))
                dve_gdn_first(dve, h)
            for h in range(4):
                v.tensor_tensor(mx[:, AT + h, :], full(dve, f"gdn A{h}"), mx[:, Y + h, :],
                                ALU.mult).then_inc(*step("dve", f"gdn A{h} taken"))

        def pool_gdn_triangle(pool, h):
            pool.wait_ge(*after(f"gdn A{h} taken"))
            g.tensor_tensor(blocks(AT + h), blocks(AT + h), C("incl").unsqueeze(1).to_broadcast([P, TT, P]),
                            ALU.mult).then_inc(*step("pool", f"gdn triangle{h}"))

        def bmask(b):
            return C(f"lev{b}").unsqueeze(1).to_broadcast([P, TT, P])

        def o_tile(b, h):
            return (8, 9, KB, KB + 1)[h] if b == 2 else Y + h

        def pool_gdn_level(pool, b, h):
            if b == 2:
                pool.wait_ge(*after(f"gdn M{h} taken"))
            elif b == 4:
                pool.wait_ge(*after(f"gdn A{h} taken"))
            else:
                pool.wait_ge(*after(f"gdn Y{b // 2} {h} full"))
            g.tensor_tensor(blocks(o_tile(b, h)), blocks(MTt + h), bmask(b), ALU.mult).then_inc(
                *step("pool", f"gdn O{b} {h}"))

        def dve_gdn_first(dve, h):
            dve.wait_ge(*after(f"gdn M{h} taken"))
            v.tensor_tensor(blocks(XT_ + h), blocks(MTt + h), bmask(1), ALU.mult).then_inc(*step("dve", f"gdn O1 {h}"))
            dve.wait_ge(*after(f"gdn O1 {h}"))
            v.tensor_tensor(blocks(XT_ + h), C("ident").unsqueeze(1).to_broadcast([P, TT, P]), blocks(XT_ + h),
                            ALU.subtract).then_inc(*step("dve", f"gdn XT1 {h}"))

        def pe_gdn_inverse(pe):
            for h in range(4):
                pe_transpose(pe, f"gdn X1 {h}", mx[:, XT_ + h, :], f"gdn XT1 {h}")
            for h in range(4):
                pe_block_products(pe, f"gdn A{h}", mx[:, KZ + h, :], mx[:, Q + h // 2, :])
            for b in _LEVELS[1:]:
                for h in range(4):
                    pe.wait_ge(*after(f"gdn O{b} {h}"))
                    pe.wait_ge(*after(f"gdn X1 {h} taken" if b == 2 else f"gdn XOX{b // 2} {h} taken"))
                    pe_block_products(pe, f"gdn Y{b} {h}", mx[:, o_tile(b, h), :], mx[:, X_ + h, :])
                for h in range(4):
                    pe.wait_ge(*after(f"gdn Y{b} {h} taken"))
                    if b > 2:
                        pe.wait_ge(*after(f"gdn XOXT{b // 2} {h} taken"))
                    if b < 32:
                        pe_half_products(pe, f"gdn XOX{b} {h}", mx[:, XT_ + h, :], mx[:, OX + h, :], b, False)
                    pe_half_products(pe, f"gdn XOXT{b} {h}", mx[:, OX + h, :], mx[:, XT_ + h, :], b, True)

        OX = KZ

        def act_gdn_inverse(act):
            for h in range(4):
                a.activation(mx[:, X_ + h, :], full(act, f"gdn X1 {h}"), ACT.Copy).then_inc(
                    *step("act", f"gdn X1 {h} taken"))
            for b in _LEVELS[1:]:
                for h in range(4):
                    if b == 2:
                        act.wait_ge(*after(f"gdn A{h} full"))
                    else:
                        act.wait_ge(*after(f"gdn XOXT{b // 2} {h} full"))
                    a.activation(mx[:, OX + h, :], full(act, f"gdn Y{b} {h}"), ACT.Copy).then_inc(
                        *step("act", f"gdn Y{b} {h} taken"))

        def dve_gdn_inverse(dve):
            for b in _LEVELS[1:]:
                for h in range(4):
                    dve.wait_ge(*after(f"gdn XOXT{b} {h} full"))
                    if b < 32:
                        x, bank = halves(mx[:, X_ + h, :], b, False), full(dve, f"gdn XOX{b} {h}")[:, 0:T // 2]
                        v.tensor_tensor(x, x, bank.rearrange("p (n b) -> p n b", b=b), ALU.subtract).then_inc(
                            *step("dve", f"gdn XOX{b} {h} taken"))
                    x, bank = halves(mx[:, XT_ + h, :], b, True), full(dve, f"gdn XOXT{b} {h}")[:, 0:T // 2]
                    v.tensor_tensor(x, x, bank.rearrange("p (n b) -> p n b", b=b), ALU.subtract).then_inc(
                        *step("dve", f"gdn XOXT{b} {h} taken"))

        def pe_gdn_operands(pe):
            for p in range(2):
                pe_transpose(pe, f"gdn kT{p}", mx[:, K + p, :], f"gdn qk {2 + p}")
            for p in range(2):
                pe_transpose(pe, f"gdn vT{p}", mx[:, V + p, :], f"silu{4 + p} used")
            for p in range(2):
                out = pe_ring(pe, f"gdn Gp{p}")
                t_.matmul(out, C(f"gpair{p}"), grow[:, :], start=True, stop=True).then_inc(
                    *step("pe", f"gdn Gp{p} full"))
            for h in range(4):
                out = pe_ring(pe, f"gdn w{h}")
                pe.wait_ge(*after(f"gdn kbg {h}"))
                pe.wait_ge(*after(f"gdn XOXT32 {h} taken"))
                for t in range(TT):
                    last = t_.matmul(out[:, t * P:(t + 1) * P], kbg[:, t, P * (h // 2):P * (h // 2) + P],
                                     blocks(XT_ + h)[:, t, :], start=True, stop=True)
                last.then_inc(*step("pe", f"gdn w{h} full"))
            for i in range(2):
                out = pe_ring(pe, f"gdn u{i}")
                pe.wait_ge(*after("gdn vT1 taken"))
                for t in (2 * i, 2 * i + 1):
                    for h in range(4):
                        at = (t % 2) * 4 * DH + h * DH
                        last = t_.matmul(out[:, at:at + DH], blocks(XT_ + h)[:, t, :], vb[:, t, h * DH:(h + 1) * DH],
                                         start=True, stop=True)
                last.then_inc(*step("pe", f"gdn u{i} full"))

        def head_cols(buf, p):
            return buf[:, :, P * p:P * (p + 1)].rearrange("p t (h c) -> p t h c", h=2)

        def dve_gdn_operands(dve):
            dve.wait_ge(*after("ecol"))
            dve.wait_ge(*after("gdn XOXT32 3 full"))
            for p in range(2):
                bank = full(dve, f"gdn kT{p}").rearrange("p (t h c) -> p t h c", t=TT, h=2)
                for hh in range(2):
                    h = 2 * p + hh
                    dst = kbg[:, :, h * DH:(h + 1) * DH]
                    v.tensor_tensor(dst, bank[:, :, hh, :], gcol[:, :, 32 + h:33 + h].to_broadcast([P, TT, DH]),
                                    ALU.mult).then_inc(*step("dve", f"gdn kb {h}"))
                    dve.wait_ge(*after(f"gdn kb {h}"))
                    v.tensor_tensor(dst, dst, ecol[:, :, h:h + 1].to_broadcast([P, TT, DH]),
                                    ALU.mult).then_inc(*step("dve", f"gdn kbg {h}"))
            for p in range(2):
                bank = full(dve, f"gdn vT{p}").rearrange("p (t h c) -> p t h c", t=TT, h=2)
                for hh in range(2):
                    h = 2 * p + hh
                    v.tensor_tensor(vb[:, :, h * DH:(h + 1) * DH], bank[:, :, hh, :],
                                    gcol[:, :, 32 + h:33 + h].to_broadcast([P, TT, DH]),
                                    ALU.mult).then_inc(*step("dve", f"gdn vT{p} taken" if hh else f"gdn vb {h}"))
            for p in range(2):
                bank = full(dve, f"gdn kT{p}").rearrange("p (t h c) -> p t h c", t=TT, h=2)
                if p == 0:
                    dve.wait_ge(*after("gdn vT1 full"))
                for hh in range(2):
                    h = 2 * p + hh
                    v.tensor_tensor(kout[:, :, h * DH:(h + 1) * DH], bank[:, :, hh, :],
                                    ecol[:, :, 32 + h:33 + h].to_broadcast([P, TT, DH]),
                                    ALU.mult).then_inc(*step("dve", f"gdn kT{p} taken" if hh else f"gdn ko {h}"))
            for p in range(2):
                dve.wait_ge(*after(f"gdn Gp{p} taken"))
                v.tensor_tensor(mx[:, Q + p, :], mx[:, Q + p, :], mx[:, 8 + p, :],
                                ALU.mult).then_inc(*step("dve", f"gdn q_in{p}"))
            for i in range(2):
                v.tensor_copy(uu[:, 2 * i:2 * i + 2, :].rearrange("p t c -> p (t c)"),
                              full(dve, f"gdn u{i}")).then_inc(*step("dve", f"gdn u{i} taken"))

        def act_gdn_operands(act):
            for p in range(2):
                a.activation(mx[:, 8 + p, :], full(act, f"gdn Gp{p}"), ACT.Exp).then_inc(
                    *step("act", f"gdn Gp{p} taken"))
            for h in range(4):
                rows = slice(64 * (h % 2), 64 * (h % 2) + 64)
                a.activation(wT[rows, h // 2, :], full(act, f"gdn w{h}")[rows, :], ACT.Copy).then_inc(
                    *step("act", f"gdn w{h} taken"))

        def pe_gdn_chunks(pe, unit, also):
            for c in range(T // GC):
                t, par_ = c // 2, c % 2
                blk = slice(t * P, (t + 1) * P)
                out = pe_ring(pe, f"gdn wS{c}")
                if c == 0:
                    pe.wait_ge(*after("gdn w3 taken"))
                    pe.wait_ge(*after("mixers cleared"))
                    pe.wait_ge(*after("gdn q_in1"))
                else:
                    pe.wait_ge(*after(f"gdn kv{c - 1} taken"))
                for p in range(2):
                    last = t_.matmul(out[:, P * p:P * (p + 1)], wT[:, p, blk], state[:, p, :], start=True, stop=True)
                last.then_inc(*step("pe", f"gdn wS{c} full"))
                pe_in(pe, unit + c, (0, KT // 2))
                outo = pe_ring(pe, f"gdn o{c}")
                outk = pe_ring(pe, f"gdn kv{c}")
                pe.wait_ge(*after(f"gdn wS{c} taken"))
                for p in range(2):
                    last = t_.matmul(outk[:, P * p:P * (p + 1)], kout[:, t, P * p:P * (p + 1)],
                                     vnew[:, par_, P * p:P * (p + 1)], start=True, stop=True)
                last.then_inc(*step("pe", f"gdn kv{c} full"))
                for p in range(2):
                    for hh in range(2):
                        h = 2 * p + hh
                        cols = slice(h * DH, (h + 1) * DH)
                        t_.matmul(outo[:, cols], mx[:, Q + p, blk], state[:, p, hh * DH:(hh + 1) * DH], start=True,
                                  stop=False)
                        last = t_.matmul(outo[:, cols], blocks(AT + h)[:, t, :], vnew[:, par_, cols], start=False,
                                         stop=True)
                last.then_inc(*step("pe", f"gdn o{c} full"))
                pe_in(pe, unit + c, (KT // 2, KT))
                also(c)

        def dve_gdn_chunks(dve, unit, also):
            for c in range(T // GC):
                t, rows = c // 2, slice(64 * (c % 2), 64 * (c % 2) + 64)
                bank = full(dve, f"gdn wS{c}")
                if c == 0:
                    dve.wait_ge(*after("gdn u1 taken"))
                if c >= 2:
                    dve.wait_ge(*after(f"gdn o{c - 2} full"))
                v.tensor_tensor(vnew[rows, c % 2, :], uu[rows, t, :], bank[rows, 0:4 * DH],
                                ALU.subtract).then_inc(*step("dve", f"gdn wS{c} taken"))
                if c:
                    split_lo(dve, unit + c + 1)
                bank = full(dve, f"gdn kv{c}")
                dve.wait_ge(*after(f"gdn o{c} full"))
                for h in range(4):
                    p, r = h // 2, slice(64 * (h % 2), 64 * (h % 2) + 64)
                    end = GC * c + GC - 1
                    st = state[r, p, r]
                    v.scalar_tensor_tensor(st, st, mx[r, 8 + p, end:end + 1], bank[r, P * p + r.start:P * p + r.stop],
                                           ALU.mult, ALU.add).then_inc(
                                               *step("dve", f"gdn kv{c} taken" if h == 3 else f"gdn state{c} {h}"))
                also(c)

        def act_gdn_chunks(act, unit, also):
            for c in range(T // GC):
                t, rows = c // 2, slice(64 * (c % 2), 64 * (c % 2) + 64)
                if c:
                    unit(c - 1)
                a.activation(oo[rows, t, :], full(act, f"gdn o{c}")[rows, 0:4 * DH], ACT.Copy).then_inc(
                    *step("act", f"gdn o{c} taken"))
                also(c)
            unit(T // GC - 1)

        GDN_O = [mx[:, Q + p, :] for p in range(2)]

        def pe_gdn_oT(pe):
            for p in range(2):
                out = pe_ring(pe, f"gdn oT{p}")
                pe.wait_ge(*after("gdn o7 taken"))
                for t in range(TT):
                    last = t_.transpose(out[:, t * P:(t + 1) * P], oo[:, t, P * p:P * (p + 1)], C("ident"))
                last.then_inc(*step("pe", f"gdn oT{p} full"))

        def act_gdn_oT(act):
            for p in range(2):
                a.activation(GDN_O[p], full(act, f"gdn oT{p}"), ACT.Copy).then_inc(*step("act", f"gdn oT{p} taken"))

        def act_gdn_out(act):
            act_head_norm(act, "gdn out", GDN_O, [f"gdn oT{p} taken" for p in range(2)], 1.0 / DH)

        def dve_gdn_out(dve):
            dve_head_norm(dve, "gdn out", GDN_O, [par("gdn_on_g")] * 2)
            for p in range(2):
                dve.wait_ge(*after(f"gdn out {p}"))
                v.tensor_tensor(mixT[:, 2 + p, :], mixT[:, 2 + p, :], GDN_O[p], ALU.mult).then_inc(
                    *step("dve", f"mix{2 + p}"))

        AM, SF, QI, KO, KOT, VT, A0, PP, KV, AX_ = 2, 10, 11, 12, 13, 16, 18, 19, 20, 24
        TJ, PROD, O_, HO, TMP, VX, QZ = (4, 5), (8, 9), 14, 34, (28, 29, 30, 31), (28, 29, 30, 31), 32

        def chunks(x):
            return x.rearrange("p (n c) -> p n c", c=LC)

        LA = {"gla": dict(q=mx[:, 6, :], k=mx[:, 7, :], a=mx[:, A0, :], v=[mixT[:, 0, :], mixT[:, 1, :]],
                          o=[mx[:, O_, :], mx[:, O_ + 1, :]], red=["gla0", "gla1"], dk=32, mask="qmask")}
        for p in range(2):
            LA[f"hg{p}"] = dict(q=xT[:, p, :], k=xT[:, 4 + p, :], a=xT[:, 2 + p, :], v=[xT[:, 6 + p, :]],
                                o=[mx[:, HO + p, :]], red=["hsum"], dk=64, mask="hmask")
        am = wtile(AM, 2)
        KVw, AXw = wtile(KV, 4), wtile(AX_, 4)
        for L in LA.values():
            L["heads"] = [(L["dk"] * h, h // 2, 64 * (h % 2)) for h in range(P // L["dk"])]
        cm = C("cmask").unsqueeze(2).to_broadcast([P, 8, DH])
        GROUP = 8

        def la_spread(eng, e, nm, n, engine):
            h, t = divmod(n, TT)
            _, vi, r0 = LA[nm]["heads"][h]
            eng.wait_ge(*after(f"{nm} v{vi} taken"))
            if n >= 4:
                eng.wait_ge(*after(f"{nm} kv{n - 4} full"))
            src = mx[:, VT + vi, t * P + r0:t * P + r0 + DH].unsqueeze(1).to_broadcast([P, 8, DH])
            e.tensor_tensor(mx[:, VX[n % 4], :].rearrange("p (c d) -> p c d", d=DH), src, cm,
                            ALU.mult).then_inc(*step(engine, f"{nm} spread{n}"))

        def la_add(eng, e, nm, j, vi, engine):
            L = LA[nm]
            n, m = LC - j, (j - 1) * len(L["v"]) + vi
            eng.wait_ge(*after(f"{nm} intra{j} {vi} taken"))
            eng.wait_ge(*after(f"{nm} o{j - 1} {vi}" if j >= 2 else f"{nm} intra0 {vi} taken"))
            o3 = chunks(L["o"][vi])[:, :, j:LC]
            e.tensor_tensor(o3, o3, mx[:, TMP[m % 4], 0:NL * n].rearrange("p (n c) -> p n c", c=n),
                            ALU.add).then_inc(*step(engine, f"{nm} o{j} {vi}"))

        def pool_la_setup(pool, nm):
            ax = chunks(LA[nm]["a"])
            pool.wait_ge(*after(f"{nm} am copy"))
            g.memset(mx[:, KO, :], 0.0).then_inc(*step("pool", f"{nm} d1 zeros"))
            if nm == "gla":
                g.memset(AXw.rearrange("p (d c) -> p d c", c=NL)[:, :, 0:1], 0.0).then_inc(*step("pool", "ax zeros"))
            g.memset(chunks(am[:, 0:T])[:, :, 0:1], 0.0)
            g.memset(am[:, T:T + 1], 0.0)
            pool.wait_ge(*after(f"{nm} d1 zeros"))
            g.tensor_copy(chunks(mx[:, KO, :])[:, :, 0:1], ax[:, :, 0:1]).then_inc(*step("pool", f"{nm} scan inputs"))

        def pool_la(pool, nm, before, also):
            L = LA[nm]
            ax = chunks(L["a"])
            pool.wait_ge(*after(before))

            def t_next(j):
                prev = chunks(L["q"] if j == 1 else mx[:, TJ[(j - 1) % 2], :])
                if j >= 3:
                    pool.wait_ge(*after(f"{nm} prod{j - 2}"))
                if j >= 2:
                    pool.wait_ge(*after(f"{nm} t{j - 1}"))
                g.tensor_tensor(chunks(mx[:, TJ[j % 2], :])[:, :, j:LC], prev[:, :, j:LC], ax[:, :, 1:LC + 1 - j],
                                ALU.mult).then_inc(*step("pool", f"{nm} t{j}"))
            t_next(1)
            t_next(2)
            for n in range(1, 4 * len(L["heads"]), 2):
                la_spread(pool, g, nm, n, "pool")
            for j in range(1, LC + 1):
                if 2 < j + 1 < LC:
                    t_next(j + 1)
                if len(L["v"]) == 2 and j >= 2:
                    la_add(pool, g, nm, j - 1, 1, "pool")
                also(j)

        def act_la_decays(act, nm, ready):
            for r in ready:
                act.wait_ge(*after(r))
            a.activation(am[:, 0:T], LA[nm]["a"], ACT.Copy).then_inc(*step("act", f"{nm} am copy"))

        def act_la_setup(act, nm, before=None):
            for vi in range(len(LA[nm]["v"])):
                a.activation(mx[:, VT + vi, :], full(act, f"{nm} v{vi}"), ACT.Copy).then_inc(
                    *step("act", f"{nm} v{vi} taken"))
            a.activation(mx[:, KOT, :], full(act, f"{nm} ko"), ACT.Copy).then_inc(*step("act", f"{nm} ko taken"))
            act.wait_ge(*after(f"{nm} prefix"))
            act.wait_ge(*after(f"{before} states" if before else "ax zeros"))
            A3 = AXw.rearrange("p (d c) -> p d c", c=NL)
            a.activation(A3[:, :, 1:NL], chunks(mx[:, PP, :])[:, 1:NL, LC - 1].unsqueeze(1).to_broadcast([P, DH, NL - 1]),
                         ACT.Copy).then_inc(*step("act", f"{nm} chunk decays"))

        def act_la(act, nm):
            L = LA[nm]
            n = 0
            for h, (row, vi, r0) in enumerate(L["heads"]):
                rows = slice(row, row + L["dk"])
                dst = KVw.rearrange("p (d c) -> p c d", c=NL)
                for t in range(TT):
                    bank = full(act, f"{nm} kv{n}").rearrange("p (c d) -> p c d", d=DH)
                    a.activation(dst[rows, 8 * t:8 * t + 8, :], bank[rows, :, :], ACT.Copy).then_inc(
                        *step("act", f"{nm} kv{n} taken"))
                    n += 1
            act.wait_ge(*after(f"{nm} q_in"))
            for h in range(len(L["heads"])):
                a.activation(mx[:, QZ + h, :], mx[:, QI, :], ACT.Copy, scale=C(L["mask"])[:, h:h + 1]).then_inc(
                    *step("act", f"{nm} qz{h}"))

        def pe_la_setup(pe, nm, vready):
            for vi, x in enumerate(LA[nm]["v"]):
                pe_transpose(pe, f"{nm} v{vi}", x, vready[vi])
            pe_transpose(pe, f"{nm} ko", mx[:, KO, :], f"{nm} k_out")

        def pe_la(pe, nm, also, unit):
            L = LA[nm]
            n_heads = len(L["heads"])
            n = 0
            for h in range(n_heads):
                for t in range(TT):
                    out = pe_ring(pe, f"{nm} kv{n}")
                    pe.wait_ge(*after(f"{nm} spread{n}"))
                    pe.wait_ge(*after(f"{nm} ko taken"))
                    t_.matmul(out, mx[:, KOT, t * P:(t + 1) * P], mx[:, VX[n % 4], :], start=True,
                              stop=True).then_inc(*step("pe", f"{nm} kv{n} full"))
                    n += 1
            for j in range(LC):
                pe.wait_ge(*after(f"{nm} prod{j}"))
                n = NL * (LC - j)
                for vi, red in enumerate(L["red"]):
                    out = pe_ring(pe, f"{nm} intra{j} {vi}")
                    t_.matmul(out[:, 0:n], C(red), mx[:, PROD[j % 2], 0:n], start=True,
                              stop=True).then_inc(*step("pe", f"{nm} intra{j} {vi} full"))
                pe_in(pe, unit + j // KT, (j % KT, j % KT + 1))
                also(j)
            S3 = KVw.rearrange("p (d c) -> p d c", c=NL)
            qz = mx[:, QZ:QZ + n_heads, :]
            pe.wait_ge(*after(f"{nm} states"))
            pe.wait_ge(*after(f"{nm} qz{n_heads - 1}"))
            for gr in range(NL // GROUP):
                out = pe_ring(pe, f"{nm} inter{gr}")
                for c in range(max(GROUP * gr, 1), GROUP * (gr + 1)):
                    at = (c - GROUP * gr) * n_heads * LC
                    last = t_.matmul(out[0:DH, at:at + n_heads * LC].rearrange("p (h t) -> p h t", h=n_heads),
                                     S3[:, :, c - 1], qz[:, :, LC * c:LC * c + LC], start=True, stop=True)
                last.then_inc(*step("pe", f"{nm} inter{gr} full"))

        def dve_la_setup(dve, nm, before=None):
            L = LA[nm]
            dve.wait_ge(*after(f"{nm} scan inputs"))
            v.tensor_tensor_scan(mx[:, PP, :], am[:, 0:T], mx[:, KO, :], 0.0, ALU.mult,
                                 ALU.add).then_inc(*step("dve", f"{nm} prefix"))
            v.tensor_tensor_scan(mx[:, SF, ::-1], am[:, 1:T + 1][:, ::-1], lastone[:, ::-1], 0.0, ALU.mult,
                                 ALU.add).then_inc(*step("dve", f"{nm} suffix"))
            dve.wait_ge(*after(f"{nm} suffix"))
            v.tensor_tensor(mx[:, KO, :], L["k"], mx[:, SF, :], ALU.mult).then_inc(*step("dve", f"{nm} k_out"))
            if before:
                dve.wait_ge(*after(before))
            v.tensor_tensor(mx[:, QI, :], L["q"], mx[:, PP, :], ALU.mult).then_inc(*step("dve", f"{nm} q_in"))

        def dve_la(dve, nm, also, following=None):
            L = LA[nm]
            n_heads, nv = len(L["heads"]), len(L["v"])
            for n in range(4, 4 * n_heads, 2):
                la_spread(dve, v, nm, n, "dve")
            for j in range(LC + 2):
                if j == 3:
                    dve.wait_ge(*after(f"{nm} chunk decays"))
                    dve.wait_ge(*after(f"{nm} kv{4 * n_heads - 1} taken"))
                    v.tensor_tensor_scan(KVw, AXw, KVw, 0.0, ALU.mult, ALU.add).then_inc(*step("dve", f"{nm} states"))
                if j < LC:
                    n = LC - j
                    if j:
                        dve.wait_ge(*after(f"{nm} t{j}"))
                    if j >= 2:
                        dve.wait_ge(*after(f"{nm} intra{j - 2} {nv - 1} full"))
                    tj = chunks(L["q"] if j == 0 else mx[:, TJ[j % 2], :])
                    v.tensor_tensor(mx[:, PROD[j % 2], 0:NL * n].rearrange("p (n c) -> p n c", c=n), tj[:, :, j:LC],
                                    chunks(L["k"])[:, :, 0:n], ALU.mult).then_inc(*step("dve", f"{nm} prod{j}"))
                if j >= 3:
                    la_add(dve, v, nm, j - 2, 0, "dve")
                if 0 < j <= LC:
                    jj, n = j - 1, LC - j + 1
                    for vi in range(nv):
                        bank = full(dve, f"{nm} intra{jj} {vi}")[:, 0:NL * n].rearrange("p (n c) -> p n c", c=n)
                        if jj == 0:
                            dst = chunks(L["o"][vi])
                        else:
                            m = (jj - 1) * nv + vi
                            if m >= 4:
                                jb, vb_ = divmod(m - 4, nv)
                                dve.wait_ge(*after(f"{nm} o{jb + 1} {vb_}"))
                            dst = mx[:, TMP[m % 4], 0:NL * n].rearrange("p (n c) -> p n c", c=n)
                        v.tensor_tensor(dst, bank, chunks(L["v"][vi])[:, :, 0:n],
                                        ALU.mult).then_inc(*step("dve", f"{nm} intra{jj} {vi} taken"))
                also(j)
            for vi in range(nv):
                dve.wait_ge(*after(f"{nm} o{LC - 1} {vi}"))
            if following:
                for n in (0, 2):
                    la_spread(dve, v, following, n, "dve")
            for gr in range(NL // GROUP):
                bank = full(dve, f"{nm} inter{gr}")[0:DH, 0:GROUP * n_heads * LC]
                bank = bank.rearrange("p (c h t) -> p c h t", c=GROUP, h=n_heads)
                first = int(gr == 0)
                for h, (_, vi, r0) in enumerate(L["heads"]):
                    o = chunks(L["o"][vi][r0:r0 + DH, :])[:, GROUP * gr + first:GROUP * (gr + 1), :]
                    last = h == n_heads - 1
                    v.tensor_tensor(o, o, bank[:, first:, h, :], ALU.add).then_inc(
                        *step("dve", f"{nm} inter{gr} taken" if last else f"{nm} inter{gr} {h}"))

        def act_la_out(act, nm, outs):
            act_head_norm(act, f"{nm} out", [o for o, _, _ in outs], [r for _, r, _ in outs], 1.0 / DH)

        def dve_la_norm(dve, nm, gain, outs):
            dve_head_norm(dve, f"{nm} out", [o for o, _, _ in outs], [par(gain)] * len(outs))

        def la_gate(eng, e, nm, outs, i, engine):
            o, _, m = outs[i]
            eng.wait_ge(*after(f"{nm} out {i}"))
            e.tensor_tensor(mixT[:, m, :], mixT[:, m, :], o, ALU.mult).then_inc(*step(engine, f"mix{m}"))

        GLA_OUT = [(mx[:, O_ + i, :], "gla inter3 taken", 6 + i) for i in range(2)]
        HG_OUT = [(mx[:, HO + i, :], f"hg{i} inter3 taken", 4 + i) for i in range(2)]

        def pe_gla_gate(pe):
            out = pe_ring(pe, "gla gate")
            pe.wait_ge(small_loaded, 16 * N_SMALL)
            pe.wait_ge(*after("in0 taken"))
            t_.matmul(out, wgk[:, :], graw[:, :], start=True, stop=True).then_inc(*step("pe", "gla gate full"))

        def act_gla_gate(act):
            z, e = mx[:, A0, :], mx[:, PP, :]
            act.wait_ge(*after("gdn XOXT32 3 taken"))
            a.activation(z, full(act, "gla gate"), ACT.Identity, bias=par("gla_b_gk")).then_inc(
                *step("act", "gla gate taken"))
            act.wait_ge(*after("gla gate taken"))
            a.activation(e, z, ACT.Abs).then_inc(*step("act", "gla abs"))
            act.wait_ge(*after("gla abs"))
            a.activation(e, e, ACT.Exp, scale=-1.0).then_inc(*step("act", "gla exp"))
            act.wait_ge(*after("gla exp"))
            a.activation(e, e, ACT.Ln, bias=1.0).then_inc(*step("act", "gla ln"))

        def dve_gla_gate(dve):
            dve.wait_ge(*after("gla ln"))
            v.scalar_tensor_tensor(mx[:, A0, :], mx[:, A0, :], 0.0, mx[:, PP, :], ALU.min,
                                   ALU.subtract).then_inc(*step("dve", "gla log sigmoid"))

        def act_gla_decay(act):
            act.wait_ge(*after("gla log sigmoid"))
            a.activation(mx[:, A0, :], mx[:, A0, :], ACT.Exp, scale=1.0 / 16).then_inc(*step("act", "gla decay"))
            act_la_decays(act, "gla", ["gla decay"])

        def act_hg_unit(act, n):
            u, p = 15 + n, n % 2
            if n // 2 != 1:
                dst = {0: xT[:, p, :], 2: xT[:, 6 + p, :], 3: mixT[:, 4 + p, :]}[n // 2]
                act_copy_in(act, u, dst)
                split_hi(act, u + 2)
                if n // 2 != 2:
                    act_silu(act, f"hg {u}", dst, f"in{u} taken")
                return
            act.wait_ge(unit_used, u + 1)
            forget, into = xT[:, 2 + p, :], xT[:, 4 + p, :]
            for x, sign, name in ((forget, -1.0, f"hg exp(-f) {p}"), (into, 1.0, f"in{u} taken")):
                a.activation(x, acc(u), ACT.Exp, scale=sign).then_inc(*step("act", name))
            split_hi(act, u + 2)
            for x, name in ((forget, "a"), (into, "k")):
                act.wait_ge(*after(f"in{u} taken"))
                a.activation(x, x, ACT.Ln, bias=1.0).then_inc(*step("act", f"hg ln {name}{p}"))
                act.wait_ge(*after(f"hg ln {name}{p}"))
                a.activation(x, x, ACT.Exp, scale=-1.0).then_inc(*step("act", f"hg {name}{p}"))

        def dve_hg_silu(dve, n):
            u, p = 15 + n, n % 2
            if n // 2 == 0:
                dve_silu(dve, f"hg {u}", xT[:, p, :], 0.125)
            elif n // 2 == 3:
                dve_silu(dve, f"hg {u}", mixT[:, 4 + p, :])

        PB = {}
        LAG = 3

        def attn_pe(pe, tag, heads, logits, values, PT, ready):
            n_all = heads * TT
            for n in range(n_all + LAG + 2):
                if n < n_all:
                    h, i = divmod(n, TT)
                    out = pe_ring(pe, f"{tag} L{n}")
                    if i == 0:
                        ready(pe, h)
                    logits(out[:, 0:P * (i + 1)], h, i).then_inc(*step("pe", f"{tag} L{n} full"))
                m = n - LAG
                if 0 <= m < n_all:
                    i = m % TT
                    out = pe_ring(pe, f"{tag} T{m}")
                    pe.wait_ge(*after(f"{tag} P{m}"))
                    for k in range(i + 1):
                        last = t_.transpose(out[:, k * P:(k + 1) * P], PB[tag][:, m % 4, k * P:(k + 1) * P],
                                            C("ident"))
                    last.then_inc(*step("pe", f"{tag} T{m} full"))
                m -= 2
                if 0 <= m and m % TT == TT - 1:
                    h = m // TT
                    out = pe_ring(pe, f"{tag} O{h}")
                    pe.wait_ge(*after(f"{tag} T{m} taken"))
                    for k in range(TT):
                        last = t_.matmul(out[:, k * P:T], values(k, h), PT[:, h % 2, k, k * P:T], start=k == 0,
                                         stop=k == TT - 1)
                    last.then_inc(*step("pe", f"{tag} O{h} full"))

        def attn_act(act, tag, heads, PT, each=None, start=None):
            n_all = heads * TT
            for n in range(n_all + LAG):
                if n < n_all:
                    i = n % TT
                    W = P * (i + 1)
                    if start and i == 0:
                        start(n // TT)
                    act.wait_ge(*after(f"{tag} max{n}"))
                    if n >= 4:
                        act.wait_ge(*after(f"{tag} T{n - 4} full"))
                    a.activation(PB[tag][:, n % 4, 0:W], full(act, f"{tag} L{n}")[:, 0:W], ACT.Exp,
                                 bias=stat[:, n % 4, 0:1],
                                 accum_out=stat[:, n % 4, 1:2]).then_inc(*step("act", f"{tag} L{n} taken"))
                m = n - LAG
                if m >= 0:
                    h, i = divmod(m, TT)
                    W = P * (i + 1)
                    bank = full(act, f"{tag} T{m}")
                    if h >= 2 and i == 0:
                        act.wait_ge(*after(f"{tag} O{h - 2} full"))
                    a.activation(PT[:, h % 2, 0:i + 1, i * P:(i + 1) * P],
                                 bank[:, 0:W].rearrange("p (k q) -> p k q", q=P),
                                 ACT.Copy).then_inc(*step("act", f"{tag} T{m} taken"))
                    if each and i == 2 and h:
                        each(h - 1)
            if each:
                each(heads - 1)

        def attn_dve(dve, tag, heads, each):
            n_all = heads * TT
            for n in range(n_all + 1):
                if n < n_all:
                    i = n % TT
                    bank = full(dve, f"{tag} L{n}")
                    diag = bank[:, i * P:(i + 1) * P]
                    v.tensor_tensor(diag, diag, C("neg"), ALU.add).then_inc(*step("dve", f"{tag} masked{n}"))
                    dve.wait_ge(*after(f"{tag} masked{n}"))
                    v.tensor_reduce(stat[:, n % 4, 0:1], bank[:, 0:P * (i + 1)], AX.X, ALU.max,
                                    negate=True).then_inc(*step("dve", f"{tag} max{n}"))
                if n:
                    m = n - 1
                    W = P * (m % TT + 1)
                    dve.wait_ge(*after(f"{tag} L{m} taken"))
                    v.reciprocal(stat[:, m % 4, 2:3], stat[:, m % 4, 1:2]).then_inc(*step("dve", f"{tag} 1/sum{m}"))
                    dve.wait_ge(*after(f"{tag} 1/sum{m}"))
                    pm = PB[tag][:, m % 4, 0:W]
                    v.tensor_scalar(pm, pm, stat[:, m % 4, 2:3], None, ALU.mult).then_inc(*step("dve", f"{tag} P{m}"))
                    if m % TT == 1 and m // TT >= 2:
                        each(m // TT - 2)
            each(heads - 2)
            each(heads - 1)

        FZ, FVT, FO = (2, 3, 14, 15), 12, 10
        FOX_IN = [mx[:, 0, :], mx[:, 1, :], mx[:, 6, :], mx[:, 7, :], mixT[:, 0, :], mixT[:, 1, :]]
        PB["fox"] = mx[:, 16:20, :]
        fox_PT = wtile(20, 8).rearrange("p (b k t) -> p b k t", b=2, t=T)
        FOX_QK = FOX_IN[2:4] + FOX_IN[0:2]
        FOX_O = [mx[:, FO + p, :] for p in range(2)]
        X_AGAIN = ((), (), (0, 1), (2, 3, 4), (5, 6, 7))

        def act_fox_unit(act, n):
            act_copy_in(act, 23 + n, FOX_IN[n])
            split_hi(act, 25 + n)

        def pe_fox_v(pe):
            for p in range(2):
                pe_transpose(pe, f"fox v{p}", FOX_IN[4 + p], f"in{27 + p} taken")

        def act_fox_v(act):
            for p in range(2):
                a.activation(mx[:, FVT + p, :], full(act, f"fox v{p}"), ACT.Copy).then_inc(
                    *step("act", f"fox v{p} taken"))

        def pe_fox(pe):
            def ready(pe, h):
                pe.wait_ge(*after(f"fox kz{h}"))
                pe.wait_ge(*after(f"fox v{h // 2} taken"))
                if X_AGAIN[h]:
                    pe_x_again(pe, X_AGAIN[h])

            def logits(out, h, i):
                W = P * (i + 1)
                if (h, i) == (0, 2):
                    pe_head_norm(pe, "hg out", range(2))
                t_.matmul(out, FOX_QK[h // 2][:, i * P:(i + 1) * P], mx[:, FZ[h], 0:W], start=True, stop=False)
                return t_.matmul(out, C(f"foxrow{h}"), grow[:, 0:W], start=False, stop=True)

            attn_pe(pe, "fox", 4, logits, lambda k, h: mx[:, FVT + h // 2, k * P:(k + 1) * P], fox_PT, ready)
            pe_x_again(pe, X_AGAIN[4])
            pe_head_norm(pe, "fox out", range(2))

        def act_fox_norm(act):
            act_head_norm(act, "fox qk", FOX_QK, [f"in{23 + i} taken" for i in (2, 3, 0, 1)], 1.0 / DH)

        def act_fox(act):
            def start(h):
                act_x_again(act, X_AGAIN[h])
                if h:
                    act_mix(act, MIX_ORDER[2 * h - 2:2 * h])
            act.wait_ge(unit_used, FIRST["w_out"])
            attn_act(act, "fox", 4, fox_PT, start=start)
            act_head_norm(act, "fox out", FOX_O, ["fox O1 taken", "fox O3 taken"], 1.0 / DH)
            act_mix(act, MIX_ORDER[6:])
            act_x_again(act, X_AGAIN[4])

        def dve_fox_norm(dve, which):
            if 0 in which:
                v.tensor_scalar(gbias[:, 3:4], par("fox_qn_g"), 0.125, None, ALU.mult).then_inc(
                    *step("dve", "fox q gain"))
                dve.wait_ge(*after("fox q gain"))
            dve_head_norm(dve, "fox qk", FOX_QK, [gbias[:, 3:4]] * 2 + [par("fox_kn_g")] * 2, which)

        def dve_fox(dve):
            def out(h):
                rows = slice(64 * (h % 2), 64 * (h % 2) + 64)
                v.tensor_copy(FOX_O[h // 2][rows, :], full(dve, f"fox O{h}")[rows, :]).then_inc(
                    *step("dve", f"fox O{h} taken"))
                if h < 3:
                    dve_mix(dve, MIX_ORDER[2 * h:2 * h + 2])
            attn_dve(dve, "fox", 4, out)
            for i in range(2):
                dve.wait_ge(*after(f"fox out rs{i}"))
                v.scalar_tensor_tensor(mixT[:, i, :], FOX_O[i], par("fox_on_g"), hr[i], ALU.mult,
                                       ALU.mult).then_inc(*step("dve", f"mix{i}"))

        def pool_fox(pool):
            for h in range(4):
                pool.wait_ge(*after(f"fox qk {2 + h // 2}"))
                g.tensor_scalar(mx[:, FZ[h], :], FOX_QK[2 + h // 2], C("hmask")[:, h % 2:h % 2 + 1], None,
                                ALU.mult).then_inc(*step("pool", f"fox kz{h}"))

        MIX_ORDER = (2, 3, 6, 7, 4, 5, 0, 1)

        def act_mix(act, tiles):
            for m in tiles:
                act.wait_ge(*after(f"mix{m}"))
                a.activation(xhi[:, m, :], mixT[:, m, :], ACT.Copy).then_inc(*step("act", f"mix hi{m}"))

        def dve_mix(dve, tiles):
            for m in tiles:
                dve.wait_ge(*after(f"mix hi{m}"))
                v.tensor_tensor(xlo[:, m, :], mixT[:, m, :], f32(xhi[:, m, :]),
                                ALU.subtract).then_inc(*step("dve", f"mix lo{m}"))

        mixers.close()
        ffn = ctx.enter_context(ExitStack())
        h_hi = sb("h_hi", [P, FT, T], F32R, ffn)
        h_lo = sb("h_lo", [P, FT, T], F32R, ffn)
        zS, yg, yu = (sb(n, [P, 2, T], F32, ffn) for n in ("zS", "yg", "yu"))
        ffn.close()
        conv = ctx.enter_context(ExitStack())
        c_hi = sb("c_hi", [P, KT, T], F32R, conv)
        c_lo = sb("c_lo", [P, KT, T], F32R, conv)
        bS, cS, vS, yS = (sb(n, [P, 2, T], F32, conv) for n in ("bS", "cS", "vS", "yS"))
        r2 = sb("r2", [P, T], c=conv)
        conv.close()
        mla = ctx.enter_context(ExitStack())
        kn = sb("kn", [P, NH2, T], c=mla)
        qn = sb("qn", [P, NH2, T], c=mla)
        qp = sb("qp", [P, NH2 // 2, T], c=mla)
        kpz = sb("kpz", [P, 2, T], c=mla)
        vtok = sb("vtok", [P, TT, D], c=mla)
        rot = sb("rot", [P, 2, T], c=mla)
        latent = ctx.enter_context(ExitStack())
        lhi, llo = (sb(n, [P, 2, T], F32R, latent) for n in ("lhi", "llo"))
        chi, clo = (sb(n, [P, 3, T], F32R, latent) for n in ("chi", "clo"))
        lat = sb("lat", [P, 2, T], c=latent)
        qlat, squares = qn[:, 3:6, :], {"lat": qn[:, 6:8, :], "cq": qn[:, 0:3, :]}
        kraw = sb("kraw", [P, T], c=latent)
        rl = sb("rl", [P, T], c=latent)
        ang, wrap = sb("ang", [P, 2, T], c=latent), sb("wrap", [P, T], c=latent)
        turns = sb("turns", [P, T], I32, latent)
        latent.close()
        attn = ctx.enter_context(ExitStack())
        PB["mla"] = sb("mla_P", [P, 4, T], c=attn)
        mla_PT = sb("mla_PT", [P, 2, TT, T], c=attn)
        attn.close()
        mla.close()
        ffn3 = ctx.enter_context(ExitStack())
        h3_hi = sb("h3_hi", [P, FT, T], F32R, ffn3)
        h3_lo = sb("h3_lo", [P, FT, T], F32R, ffn3)
        zS3, yg3 = (sb(n, [P, 2, T], F32, ffn3) for n in ("zS3", "yg3"))
        ffn3.close()
        fin = sb("fin", [P, TT, D])

        MLA_TILES = [f"dkv{i}" for i in range(3)] + [f"dq{i}" for i in range(3)] + [f"kn{h}" for h in range(NH2)]
        MLA_TILES += [f"v{g}{t}" for g in range(2) for t in range(TT)]
        for _g in range(2):
            MLA_TILES += [f"qp{2 * _g + p}" for p in range(2)] + [f"qn{4 * _g + h}" for h in range(4)]
        tile_no = {n: i for i, n in enumerate(MLA_TILES)}

        def mla_acc(name):
            return acc(tile_no[name])

        def pe_mla_wait(pe, name):
            if tile_no[name] >= 2:
                pe.wait_ge(*after(f"{MLA_TILES[tile_no[name] - 2]} taken"))

        def pe_latent_sum(pe, name, n):
            out = pe_ring(pe, f"{name} sum")
            for k in range(n):
                pe.wait_ge(*after(f"{name} square{k}"))
                last = t_.matmul(out, C("ones"), squares[name][:, k, :], start=k == 0, stop=k == n - 1)
            last.then_inc(*step("pe", f"{name} sum full"))

        def act_latent_square(act, name, x, k, ready):
            act.wait_ge(*after(ready))
            a.activation(squares[name][:, k, :], x[:, k, :], ACT.Square).then_inc(*step("act", f"{name} square{k}"))

        def pe_mla(pe):
            u = FIRST["dkv"]
            for i in range(3):
                pe_mla_wait(pe, f"dkv{i}")
                product(pe, u + i, tile_no[f"dkv{i}"], ready=parts_of("kv_norm_g_2") if i == 0 else None)
                if i == 0:
                    pe_sum(pe, "mla norm", NORM0["ffn2_down"])
            u = FIRST["dq"]
            for i in range(3):
                pe_mla_wait(pe, f"dq{i}")
                for ks in ((0, 6), (6, KT)):
                    product(pe, u + i, tile_no[f"dq{i}"], ready=parts_of("mla_norm_g_2") if i == 0 else None, ks=ks)
                    if i == 0 and ks[0] == 0:
                        pe_latent_sum(pe, "lat", 2)
            out = pe_ring(pe, "k swapped")
            pe.wait_ge(*after("dkv2 taken"))
            t_.matmul(out, C("perm"), kraw[:, :], start=True, stop=True).then_inc(*step("pe", "k swapped full"))
            u = FIRST["ukv"]
            for h in range(NH2):
                pe_mla_wait(pe, f"kn{h}")
                product(pe, u + h // 4, tile_no[f"kn{h}"], x=(lhi, llo),
                        ready=(lambda pe, k: pe.wait_ge(*after(f"lat lo{k}"))) if h == 0 else None,
                        cols=P * (h % 4), full=f"kn{h} full" if h % 4 < 3 else None)
                if h == 3:
                    pe_latent_sum(pe, "cq", 3)
            for gr in range(2):
                pe.wait_ge(lo_split, u + 2 + gr + 1)
                wh, wl = (unit_view(b, u + 2 + gr) for b in (whi, wlo))
                for t in range(TT):
                    pe_mla_wait(pe, f"v{gr}{t}")
                    blk = slice(t * P, (t + 1) * P)
                    for k in range(2):
                        last = passes(mla_acc(f"v{gr}{t}"), lhi[:, k, blk], llo[:, k, blk], wh[:, k, :], wl[:, k, :],
                                      k == 0, k == 1)
                    last.then_inc(*(step("pe", f"v{gr}{t} full") if t < TT - 1 else (unit_used, 1)))
            u = FIRST["uq"]
            for gr in range(2):
                for p in range(2):
                    name = f"qp{2 * gr + p}"
                    pe_mla_wait(pe, name)
                    product(pe, u + 3 * gr, tile_no[name], x=(chi, clo), cols=P * p, full=f"{name} full" if p == 0 else None,
                            ready=(lambda pe, k: pe.wait_ge(*after(f"cq lo{k}"))) if name == "qp0" else None)
                for p in range(2):
                    for hh in range(2):
                        name = f"qn{4 * gr + 2 * p + hh}"
                        pe_mla_wait(pe, name)
                        product(pe, u + 3 * gr + p + 1, tile_no[name], x=(chi, clo), cols=P * hh,
                                full=f"{name} full" if hh == 0 else None)
                    if p == 0:
                        for i in (2 * gr, 2 * gr + 1):
                            out = pe_ring(pe, f"q swapped{i}")
                            pe.wait_ge(*after(f"qp{i} taken"))
                            t_.matmul(out, C("perm"), qp[:, i, :], start=True, stop=True).then_inc(
                                *step("pe", f"q swapped{i} full"))

            def ready(pe, h):
                if h == 0:
                    pe.wait_ge(*after("kpz1"))
                    pe.wait_ge(*after("kpz0"))
                    pe.wait_ge(*after(f"kn{NH2 - 1} taken"))
                    pe.wait_ge(*after("v13 taken"))
                pe.wait_ge(*after(f"qn{h} taken"))
                pe.wait_ge(*after(f"rotated{h // 2}"))

            def logits(out, h, i):
                blk = slice(i * P, (i + 1) * P)
                W = P * (i + 1)
                t_.matmul(out, qn[:, h, blk], kn[:, h, 0:W], start=True, stop=False)
                return t_.matmul(out, qp[:, h // 2, blk], kpz[:, h % 2, 0:W], start=False, stop=True)

            attn_pe(pe, "mla", NH2, logits, lambda k, h: vtok[:, k, h * P:(h + 1) * P], mla_PT, ready)

        QSCALE = float((128 + 64) ** -0.5)

        def act_mla(act):
            act_rstd(act, "mla norm", D, rs[:, :])
            act_positions(act)
            u = FIRST["dkv"]
            for i in range(3):
                if i == 2:
                    act_gain_all(act, "mla_norm_g_2", FIRST["dq"], range(KT // 2))
                    for k in range(2):
                        act_latent_square(act, "lat", lat, k, f"dkv{k} taken")
                    act_gain_all(act, "mla_norm_g_2", FIRST["dq"], range(KT // 2, KT))
                split_hi(act, u + i + 2)
            u = FIRST["dq"]
            split_hi(act, u + 2)
            act_rstd(act, "lat", 2 * P, rl[:, :], table=False)
            act_hi(act, "lat", 2, lhi)
            for i in range(3):
                if i:
                    split_hi(act, u + i + 2)
                act_latent_square(act, "cq", qlat, i, f"dq{i} taken")
            u = FIRST["ukv"]
            for h in range(NH2):
                act.wait_ge(*after(f"kn{h} full") if h % 4 < 3 else (unit_used, u + h // 4 + 1))
                a.activation(kn[:, h, :], mla_acc(f"kn{h}"), ACT.Copy).then_inc(*step("act", f"kn{h} taken"))
                if h % 4 == 3:
                    split_hi(act, u + h // 4 + 2)
            act_rstd(act, "cq", 3 * P, rl[:, :], table=False)
            for gr in range(2):
                for t in range(TT):
                    act.wait_ge(*after(f"v{gr}{t} full") if t < TT - 1 else (unit_used, u + 2 + gr + 1))
                    a.activation(vtok[:, t, 4 * P * gr:4 * P * (gr + 1)], mla_acc(f"v{gr}{t}"), ACT.Copy).then_inc(
                        *step("act", f"v{gr}{t} taken"))
                    if (gr, t) == (0, 1):
                        act_hi(act, "cq", 3, chi)
                split_hi(act, u + 2 + gr + 2)
            for n in ("sin", "cos"):
                act.wait_ge(*after(f"{n} reduced"))
                a.activation(rot[:, n == "sin", :], ang[:, n == "cos", :], ACT.Sin).then_inc(*step("act", n))
            u = FIRST["uq"]
            for gr in range(2):
                for p in range(2):
                    i = 2 * gr + p
                    act.wait_ge(*after(f"qp{i} full") if p == 0 else (unit_used, u + 3 * gr + 1))
                    a.activation(qp[:, i, :], mla_acc(f"qp{i}"), ACT.Copy, scale=QSCALE).then_inc(
                        *step("act", f"qp{i} taken"))
                split_hi(act, u + 3 * gr + 2)
                for p in range(2):
                    for hh in range(2):
                        h = 4 * gr + 2 * p + hh
                        act.wait_ge(*after(f"qn{h} full") if hh == 0 else (unit_used, u + 3 * gr + p + 2))
                        a.activation(qn[:, h, :], mla_acc(f"qn{h}"), ACT.Copy, scale=QSCALE).then_inc(
                            *step("act", f"qn{h} taken"))
                    split_hi(act, u + 3 * gr + p + 3)
            a.preload_act_table_set("natural_log_exp_and_others")

            def each(h):
                a.activation(xhi[:, h, :], full(act, f"mla O{h}"), ACT.Copy).then_inc(*step("act", f"mla hi{h}"))
            attn_act(act, "mla", NH2, mla_PT, each)

        def pool_mla(pool):
            pool.wait_ge(x_lo, XPART0["mla_norm_g_2"])
            g.memset(kpz[:, :, :], 0.0).then_inc(*step("pool", "kpz zeros"))

        def act_positions(act):
            act.dma_start(turns[:, :], A["positions_2"][0].partition_broadcast(P)).then_inc(pos_loaded, 16)

        TWO_PI = 2 * np.pi
        TURN = [6.28125, 0.0019350051879882812, float(TWO_PI - 6.28125 - 0.0019350051879882812)]

        angle_n = [0]

        def angle_step(dve, ins, name=None):
            angle_n[0] += 1
            name = name or f"angle{angle_n[0]}"
            ins.then_inc(*step("dve", name))
            dve.wait_ge(*after(name))

        def dve_angles(dve):
            s, w = ang[:, 0, :], wrap[:, :]
            dve.wait_ge(pos_loaded, 16)
            angle_step(dve, v.tensor_copy(s, turns[:, :]))
            angle_step(dve, v.tensor_scalar(s, s, C("freq"), None, ALU.mult))
            angle_step(dve, v.tensor_scalar(turns[:, :], s, float(1 / TWO_PI), None, ALU.mult))
            angle_step(dve, v.tensor_copy(w, turns[:, :]))
            for part in TURN:
                angle_step(dve, v.scalar_tensor_tensor(s, w, -part, s, ALU.mult, ALU.add))

        def dve_wrap(dve, x, name):
            w = wrap[:, :]
            for side, op in ((1.0, ALU.is_gt), (-1.0, ALU.is_lt)):
                angle_step(dve, v.tensor_scalar(w, x, side * float(np.pi), -side * float(TWO_PI), op, ALU.mult))
                angle_step(dve, v.tensor_tensor(x, x, w, ALU.add))
            if name == "sin":
                angle_step(dve, v.tensor_scalar(ang[:, 1, :], x, float(np.pi / 2), None, ALU.add))
            angle_step(dve, v.tensor_scalar(x, x, 3.1415925, -3.1415925, ALU.min, ALU.max), f"{name} reduced")

        def dve_rotate(dve, key, x, name, before):
            w = xg[:, 0, :]
            dve.wait_ge(*after(before))
            v.tensor_tensor(w, full(dve, key), rot[:, 1, :], ALU.mult).then_inc(*step("dve", f"{key} taken"))
            v.tensor_tensor(x, x, rot[:, 0, :], ALU.mult).then_inc(*step("dve", f"{name} cos"))
            dve.wait_ge(*after(f"{name} cos"))
            v.tensor_tensor(x, x, w, ALU.add).then_inc(*step("dve", name))

        def dve_mla(dve):
            dve.wait_ge(*after("mla norm rstd"))
            u = FIRST["dkv"]
            for i in range(3):
                dve.wait_ge(unit_used, u + i + 1)
                v.tensor_tensor(lat[:, i, :] if i < 2 else kraw[:, :], mla_acc(f"dkv{i}"), rs[:, :], ALU.mult).then_inc(
                    *step("dve", f"dkv{i} taken"))
                if i == 2:
                    dve_gain_all(dve, "mla_norm_g_2")
                split_lo(dve, u + i + 2)
            dve_angles(dve)
            u = FIRST["dq"]
            for i in range(3):
                dve.wait_ge(unit_used, u + i + 1)
                v.tensor_tensor(qlat[:, i, :], mla_acc(f"dq{i}"), rs[:, :], ALU.mult).then_inc(
                    *step("dve", f"dq{i} taken"))
                split_lo(dve, u + i + 2)
                if i == 0:
                    dve_scale(dve, "lat", 2, lat, "kv_latent_norm_g_2", lhi, llo, "lat rstd", rl[:, :])
                elif i == 1:
                    dve_wrap(dve, ang[:, 0, :], "sin")
            u = FIRST["ukv"]
            split_lo(dve, u + 2)
            dve_wrap(dve, ang[:, 1, :], "cos")
            split_lo(dve, u + 3)
            dve_scale(dve, "cq", 3, qlat, "mla_q_norm_g_2", chi, clo, "cq rstd", rl[:, :], "lat lo1")
            split_lo(dve, u + 4)
            split_lo(dve, u + 5)
            dve.wait_ge(*after("cos"))
            s = rot[:, 1, :]
            v.tensor_scalar(s, s, C("sign"), None, ALU.mult).then_inc(*step("dve", "signed sin"))
            dve.wait_ge(*after("signed sin"))
            dve_rotate(dve, "k swapped", kraw[:, :], "k rotated", "cq lo2")
            u = FIRST["uq"]
            for gr in range(2):
                for p in range(3):
                    split_lo(dve, u + 3 * gr + p + 2)
                    if p == 1:
                        for i in (2 * gr, 2 * gr + 1):
                            dve_rotate(dve, f"q swapped{i}", qp[:, i, :], f"rotated{i}",
                                       f"rotated{i - 1}" if i else "k rotated")
                if gr == 0:
                    dve.wait_ge(*after("kpz zeros"))
                    for half in range(2):
                        v.tensor_copy(kpz[64 * half:64 * half + 64, half, :], kraw[64:P, :]).then_inc(
                            *step("dve", f"kpz{half}"))

            def each(h):
                dve.wait_ge(*after(f"mla hi{h}"))
                v.tensor_tensor(xlo[:, h, :], full(dve, f"mla O{h}"), f32(xhi[:, h, :]),
                                ALU.subtract).then_inc(*step("dve", f"mla O{h} taken"))
            attn_dve(dve, "mla", NH2, each)

        HALVES = [(half, t) for half in range(2) for t in range(TT)]
        HALF = D // 2
        final_rstd = stat[:, 0:TT, 0]

        def pe_final(pe):
            for half, t in HALVES:
                if (half, t) == (1, 1):
                    out = pe_ring(pe, "final norm sum")
                    pe.wait_ge(summed, NORM0["ffn3_down"] + KT + 2)
                    for tt in range(TT):
                        last = t_.matmul(out[:, tt:tt + 1], ssq[:, tt * P:(tt + 1) * P], C("ones")[:, 0:1], start=True,
                                         stop=True)
                    last.then_inc(*step("pe", "final norm sum full"))
                out = pe_ring(pe, f"final{half}{t}")
                for k in range(KT // 2):
                    tile = half * KT // 2 + k
                    if t == 0:
                        pe.wait_ge(x_hi, XPART0["final_norm_g_2"] + tile + 1)
                    last = t_.transpose(out[:, k * P:(k + 1) * P], xT[:, tile, t * P:(t + 1) * P], C("ident"))
                last.then_inc(*step("pe", f"final{half}{t} full"))

        def act_final(act):
            act_rstd(act, "final norm", D, final_rstd, TT)
            act.wait_ge(*after("final norm rstd"))
            for half, t in HALVES:
                if t % 2 == 0:
                    a.activation(fin[:, t, half * HALF:(half + 1) * HALF], full(act, f"final{half}{t}"), ACT.Copy,
                                 scale=stat[:, t, 0:1]).then_inc(*step("act", f"final{half}{t} taken"))

        def dve_final(dve):
            dve.wait_ge(*after("final norm rstd"))
            for half, t in HALVES:
                if t % 2:
                    v.tensor_scalar(fin[:, t, half * HALF:(half + 1) * HALF], full(dve, f"final{half}{t}"),
                                    stat[:, t, 0:1], None, ALU.mult).then_inc(*step("dve", f"final{half}{t} taken"))

        def sp_final(sp):
            for half, t in HALVES:
                sp.wait_ge(*after(f"final{half}{t} taken"))
                cols = slice(half * HALF, (half + 1) * HALF)
                sp.dma_start(out_d[0, t * P:(t + 1) * P, cols], fin[:, t, cols]).then_inc(stored, 16)
            sp.wait_ge(stored, 16 * len(HALVES))


        def hg_ready(p):
            return [f"silu{10 + p} used", f"hg a{p}", f"hg k{p}", f"in{19 + p} taken"]

        block = ctx.enter_context(nc.Block())

        @block.sync
        def _(sp):
            sp_load_inputs(sp)
            for u in range(FIRST["w_out"]):
                load_unit(sp, u)
                if u == 1:
                    sp.dma_start(cst[:, NCONST0:], cst_d[:, NCONST0:]).then_inc(cst_loaded, 16)
            def up(i, j):
                return (j % 2) * FF + (j // 2) * P + 2 * P * i
            def one(i, j):
                return j * P + 4 * P * i
            def thirds(i, j):
                return (j // 3) * P + 4 * P * i
            load_loop(sp, "w_out", KT, 4, one)
            load_loop(sp, "ffn1_up", 2 * FT, 4, up)
            load_loop(sp, "ffn1_down", 3 * KT, 12, thirds)
            load_loop(sp, "conv_in", 3 * KT, 12, lambda i, j: (j % 3) * D + (j // 3) * P + 4 * P * i)
            load_loop(sp, "conv_out", KT, 4, one)
            load_loop(sp, "ffn2_up", 2 * FT, 4, up)
            load_loop(sp, "ffn2_down", 3 * KT, 12, thirds)
            for u in range(FIRST["dkv"], FIRST["w_o"]):
                load_unit(sp, u)
            load_loop(sp, "w_o", KT, 4, one)
            load_loop(sp, "ffn3_up", 2 * FT, 4, up)
            load_loop(sp, "ffn3_down", 3 * KT, 12, thirds)
            sp_final(sp)

        @block.gpsimd
        def _(pool):
            pool_init(pool)
            load_small(pool)
            pool.wait_ge(cst_loaded, 16)
            pool_gdn(pool)
            for b in _LEVELS[1:]:
                for h in range(4):
                    pool_gdn_level(pool, b, h)
                    if b == 4:
                        pool_gdn_triangle(pool, h)
            pool_la_setup(pool, "gla")
            pool.wait_ge(*after("gdn o7 full"))

            def in_gla(j):
                if j == 6:
                    pool_la_setup(pool, "hg0")

            def in_hg0(j):
                if j == 3:
                    split_lo(pool, 26, e=g)
                elif j in (5, 6):
                    la_gate(pool, g, "gla", GLA_OUT, j - 5, "pool")
                elif j == 8:
                    pool_la_setup(pool, "hg1")
                elif j == 11:
                    split_lo(pool, 27, e=g)

            def in_hg1(j):
                if j in (3, 11):
                    split_lo(pool, 28 + j // 11, e=g)
            pool_la(pool, "gla", "gdn kv7 taken", in_gla)
            pool_la(pool, "hg0", "gla o15 0", in_hg0)
            pool_la(pool, "hg1", "hg0 o15 0", in_hg1)
            pool_fox(pool)
            pool_load_again(pool)
            pool_residual(pool, "w_out", "mix1")
            pool_products(pool, "ffn1_up", FT, h_hi, h_lo)
            pool_residual(pool, "ffn1_down", "norm2 sum full")
            pool_products(pool, "conv_in", KT, c_hi, c_lo)
            pool_residual(pool, "conv_out", "conv norm sum full")
            pool_products(pool, "ffn2_up", FT, h_hi, h_lo)
            pool_residual(pool, "ffn2_down", "ffn2 norm sum full")
            pool_mla(pool)
            pool_residual(pool, "w_o", "mla norm sum full")
            pool_products(pool, "ffn3_up", FT, h3_hi, h3_lo)
            pool_residual(pool, "ffn3_down", "ffn3 norm sum full")

        @block.tensor
        def _(pe):
            pe_load(pe)
            pe.wait_ge(cst_loaded, 16)
            for u in range(11):
                pe_in(pe, u)
            pe_gates(pe)
            for u in range(11, 13):
                pe_in(pe, u)
            pe_head_norm(pe, "gdn qk", range(0, 2))
            pe_in(pe, 13, (0, KT // 2))
            pe_head_norm(pe, "gdn qk", range(2, 4))
            pe_in(pe, 13, (KT // 2, KT))
            pe_gdn_setup(pe)
            pe_gdn_triangles(pe)
            pe_in(pe, 14)
            pe_gdn_inverse(pe)
            pe_gdn_operands(pe)
            pe_gla_gate(pe)

            def in_chunks(c):
                if c == 4:
                    pe_la_setup(pe, "gla", ["in11 taken", "in12 taken"])

            def in_gla(j):
                if j == 3:
                    pe_head_norm(pe, "gdn out", range(2))
                elif j == 10:
                    pe_la_setup(pe, "hg0", ["in19 taken"])

            def in_hg0(j):
                if j == 2:
                    pe_head_norm(pe, "gla out", range(2))
                elif j == 13:
                    pe_la_setup(pe, "hg1", ["in20 taken"])
            pe_gdn_chunks(pe, 15, in_chunks)
            pe_gdn_oT(pe)
            pe_la(pe, "gla", in_gla, 23)

            def in_hg1(j):
                if j in (4, 6):
                    pe_head_norm(pe, "fox qk", range(j - 4, j - 2))
            pe_la(pe, "hg0", in_hg0, 25)
            pe_la(pe, "hg1", in_hg1, 27)
            pe_fox_v(pe)
            pe_fox(pe)

            pe_residual(pe, "w_out", False, (xhi, xlo), lambda pe, k: pe.wait_ge(*after(f"mix lo{k}")), MIX_ORDER)
            pe_up(pe, "ffn1_up", "norm2", "norm2_g", "w_out")

            def products(stage):
                return lambda pe, k: pe.wait_ge(prod_lo, PAIR0[stage] + k + 3)
            pe_residual(pe, "ffn1_down", True, (h_hi, h_lo), products("ffn1_up"))
            pe_conv_in(pe)
            pe_residual(pe, "conv_out", False, (c_hi, c_lo), products("conv_in"))
            pe_up(pe, "ffn2_up", "ffn2 norm", "conv_ffn_norm_g_2", "conv_out")
            pe_residual(pe, "ffn2_down", True, (h_hi, h_lo), products("ffn2_up"))
            pe_mla(pe)
            pe_residual(pe, "w_o", False, (xhi, xlo), lambda pe, k: pe.wait_ge(*after(f"mla O{k} taken")))
            pe_up(pe, "ffn3_up", "ffn3 norm", "mla_ffn_norm_g_2", "w_o")
            pe_residual(pe, "ffn3_down", True, (h3_hi, h3_lo), products("ffn3_up"))
            pe_final(pe)

        @block.scalar
        def _(act):
            act.dma_start(cst[:, 0:NCONST0], cst_d[:, 0:NCONST0]).then_inc(cst0_loaded, 16)
            load_rows(act)
            act_load(act)
            act.wait_ge(cst_loaded, 16)
            for u in range(9):
                if 1 <= u <= 6:
                    act_gdn_tap(act, u - 1)
                    if u >= 2:
                        act_silu(act, f"conv{u - 2}", mx[:, u - 2, :], f"in{u - 1} taken")
                elif u >= 7:
                    act_copy_in(act, u, mixT[:, u - 5, :])
                    if u == 7:
                        act_silu(act, "conv5", mx[:, 5, :], "in6 taken")
                    act_silu(act, f"z{u - 7}", mixT[:, u - 5, :], f"in{u} taken")
                split_hi(act, u + 2)
            act_gates(act)

            def unit(u):
                dst = (mx[:, 6, :], mx[:, 7, :], mixT[:, 0, :], mixT[:, 1, :], mixT[:, 6, :], mixT[:, 7, :])[u - 9]
                act_copy_in(act, u, dst, 32 ** -0.5 if u == 9 else 1.0)
                split_hi(act, u + 2)
                if u == 10:
                    act_ecol(act)
                elif u == 11:
                    act_gdn_norm(act)
                elif u >= 13:
                    act_silu(act, f"gla g{u - 13}", dst, f"in{u} taken")
            for u in range(9, 14):
                unit(u)
            act_gdn_setup(act)
            unit(14)
            act_gdn_inverse(act)
            act_gdn_operands(act)

            def in_chunks(c):
                if c == 0:
                    act_gla_gate(act)
                elif c == 2:
                    act_gla_decay(act)
                elif c == 5:
                    act_la_setup(act, "gla")
            act_gdn_chunks(act, lambda n: act_hg_unit(act, n), in_chunks)
            act_gdn_oT(act)
            act_la(act, "gla")
            act_gdn_out(act)
            act_la_decays(act, "hg0", hg_ready(0))
            act_fox_unit(act, 0)
            act_la_setup(act, "hg0", "gla")
            act_fox_unit(act, 1)
            act_la(act, "hg0")
            act_la_out(act, "gla", GLA_OUT)
            act_la_decays(act, "hg1", hg_ready(1))
            act_fox_unit(act, 2)
            act_la_setup(act, "hg1", "hg0")
            act_fox_unit(act, 3)
            act_la(act, "hg1")
            act_fox_norm(act)
            act_fox_unit(act, 4)
            act_fox_unit(act, 5)
            act_fox_v(act)
            act_la_out(act, "hg", HG_OUT)
            act_fox(act)
            act_residual(act, "w_out", False, None, "norm2_g")
            act_rstd(act, "norm2", D, rs[:, :])
            act_up(act, "ffn1_up", True, h_hi, zS, yg, yu)
            act_residual(act, "ffn1_down", True, "conv_norm_g_2")
            act_rstd(act, "conv norm", D, rs[:, :])
            act_conv_in(act, c_hi, vS, yS)
            act_residual(act, "conv_out", False, "conv_ffn_norm_g_2")
            act_rstd(act, "ffn2 norm", D, rs[:, :])
            act_up(act, "ffn2_up", False, h_hi, zS, yg, yu)
            act_residual(act, "ffn2_down", True, "kv_norm_g_2")
            act_mla(act)
            act_residual(act, "w_o", False, None, "mla_ffn_norm_g_2")
            act_rstd(act, "ffn3 norm", D, rs[:, :])
            act_up(act, "ffn3_up", False, h3_hi, zS3, yg3, None)
            act_residual(act, "ffn3_down", True, "final_norm_g_2")
            act_final(act)

        @block.vector
        def _(dve):
            dve_load(dve)
            dve.wait_ge(cst_loaded, 16)
            for u in range(9):
                if u == 0:
                    dve_gate_in(dve)
                elif u <= 6:
                    dve_gdn_conv(dve, u - 1)
                    if u >= 2:
                        dve_silu(dve, f"conv{u - 2}", mx[:, u - 2, :])
                else:
                    if u == 7:
                        dve_silu(dve, "conv5", mx[:, 5, :])
                    dve_silu(dve, f"z{u - 7}", mixT[:, u - 5, :])
                split_lo(dve, u + 2)
            dve_gates(dve)
            dve_gcol(dve)
            for u in range(9, 14):
                split_lo(dve, u + 2)
                if u == 11:
                    dve_gdn_norm(dve)
                elif u == 13:
                    dve_silu(dve, "gla g0", mixT[:, 6, :])
            dve_gdn_setup(dve)
            dve_gdn_triangles(dve)
            split_lo(dve, 16)
            dve_silu(dve, "gla g1", mixT[:, 7, :])
            dve_gdn_inverse(dve)
            dve_gdn_operands(dve)

            def in_chunks(c):
                if c >= 1:
                    dve_hg_silu(dve, c - 1)
                if c == 1:
                    dve_gla_gate(dve)
                elif c == 4:
                    dve_la_setup(dve, "gla")

            def in_gla(j):
                if j == 5:
                    dve_gdn_out(dve)
                elif j == 9:
                    dve_la_setup(dve, "hg0", "gla qz3")
                elif j == 11:
                    split_lo(dve, 25)

            def in_hg0(j):
                if j == 4:
                    dve_la_norm(dve, "gla", "gla_on_g", GLA_OUT)
                elif j == 12:
                    dve_la_setup(dve, "hg1", "hg0 qz1")

            def in_hg1(j):
                if j in (5, 7):
                    dve_fox_norm(dve, range(j - 5, j - 3))
                elif j == LC + 1:
                    split_lo(dve, 30)
            dve_gdn_chunks(dve, 15, in_chunks)
            for n in (0, 2):
                la_spread(dve, v, "gla", n, "dve")
            split_lo(dve, 24)
            dve_hg_silu(dve, 7)
            dve_la(dve, "gla", in_gla, "hg0")
            dve_la(dve, "hg0", in_hg0, "hg1")
            dve_la(dve, "hg1", in_hg1)
            dve_la_norm(dve, "hg", "hg_on_g", HG_OUT)
            for i in range(2):
                la_gate(dve, v, "hg", HG_OUT, i, "dve")
            dve_fox(dve)
            dve_mix(dve, MIX_ORDER[6:])
            dve_residual(dve, "w_out", False, None, "norm2_g")
            dve_up(dve, "ffn1_up", True, "norm2 rstd", zS, yg, yu)
            dve_residual(dve, "ffn1_down", True, "conv_norm_g_2")
            dve_conv_in(dve, bS, cS, vS, yS, r2)
            dve_residual(dve, "conv_out", False, "conv_ffn_norm_g_2")
            dve_up(dve, "ffn2_up", False, "ffn2 norm rstd", zS, yg, yu)
            dve_residual(dve, "ffn2_down", True, "kv_norm_g_2")
            dve_mla(dve)
            dve_residual(dve, "w_o", False, None, "mla_ffn_norm_g_2")
            dve_up(dve, "ffn3_up", False, "ffn3 norm rstd", zS3, yg3, None)
            dve_residual(dve, "ffn3_down", True, None)
            dve_final(dve)

    return S


_OUT = (1, T, D)


def _program(nc, arrays, known):
    aps = {n: nc.dram_tensor(f"in_{n}", a.shape, mybir.dt.from_np(a.dtype), kind="ExternalInput").ap()
           for n, a in arrays.items()}
    out = nc.dram_tensor("out_0", _OUT, F32, kind="ExternalOutput").ap()
    cst = aps.pop("constants")
    flat = {n: (x[0] if len(x.shape) == 3 and n in _WEIGHTS else x) for n, x in aps.items()}
    return build(nc, flat, cst, out, known)


_WEIGHTS = {u[0] for u in UNITS}


def lay_out(inputs):
    arrays = {n: np.ascontiguousarray(a) for n, a in inputs.items()}
    params = np.zeros((P, PARAM_COLS), np.float32)
    rows = [np.tile(x.reshape(1, DH), 2) if x.shape[-1] == DH else x.reshape(-1, P)
            for x in (arrays.pop(n) for n in _ROWS)]
    params[0:NROW0, 0:P] = np.concatenate(rows)
    conv = np.concatenate([arrays.pop(n).reshape(-1, P) for n in ("ffn_conv_w", "ffn_conv_b")])
    params[:, P:2 * P] = conv[0:P]
    params[0:NROW2, 2 * P:3 * P] = conv[P:]
    params[96:112, 3 * P:4 * P] = arrays.pop("gla_w_gk")[0]
    params[0:4, 4 * P] = arrays.pop("fox_b_f")[0]
    params[64:68, 4 * P] = arrays.pop("gdn_dt_bias")[0]
    params[64:68, 4 * P + 1] = arrays.pop("gdn_a_log")[0]
    arrays.update(params=params, constants=constants())
    return arrays


def kernel(**inputs):
    import concourse.bacc as bacc
    from concourse.bass_utils import run_bass_kernel_spmd

    arrays = lay_out(inputs)
    numbers = None
    for _ in range(2):
        nc = bacc.Bacc("TRN2", target_bir_lowering=False, num_devices=1)
        numbers = _program(nc, arrays, numbers)
    r = run_bass_kernel_spmd(nc, [{f"in_{n}": a for n, a in arrays.items()}], core_ids=[0])
    return r.results[0]["out_0"]
```
